# Optimizing a Trainium2 kernel written in Bass

```python
import jax, jax.numpy as jnp
from jax import lax
import numpy as np
import math

D_MODEL = 1024
BATCH = 1
SEQ = 256
DEPTH = 2

HEAD_DIM = 64
ROPE_THETA = 10000.0
A_HEADS = 8
A_CONFIGS = ((128, 1), (512, 4), (2048, 16))
B_HEADS = 8
B_KV_HEADS = 2
B_WINDOW = 128
C_HEADS = 8
IDX_HEADS = 8
IDX_DIM = 64
TOPK_MAX = 256
QUERY_BLOCK = 128
BAND_BLOCK = 128
D_FF = 2816
LN_EPS = 1e-5
DN_ALPHA = (2 * DEPTH) ** 0.25
DN_BETA = (8 * DEPTH) ** -0.25

A_W = A_HEADS * HEAD_DIM
B_QW = B_HEADS * HEAD_DIM
B_KW = B_KV_HEADS * HEAD_DIM
C_W = C_HEADS * HEAD_DIM
IN_SIZES = (A_W, A_W, A_W,
            B_QW, B_KW, B_KW,
            C_W, HEAD_DIM, HEAD_DIM,
            IDX_HEADS * IDX_DIM, IDX_DIM, IDX_HEADS,
            D_MODEL, D_MODEL, D_MODEL)
D_IN = sum(IN_SIZES)


def layer_norm(x, g, b):
    xf = x.astype(jnp.float32)
    mu = xf.mean(-1, keepdims=True)
    var = jnp.square(xf - mu).mean(-1, keepdims=True)
    y = (xf - mu) * lax.rsqrt(var + LN_EPS)
    return (y * g.astype(jnp.float32) + b.astype(jnp.float32)).astype(x.dtype)

def rope_tables(positions, dim):
    inv = ROPE_THETA ** (-jnp.arange(0, dim, 2, dtype=jnp.float32) / dim)
    ang = positions.astype(jnp.float32)[..., None] * inv
    return jnp.cos(ang), jnp.sin(ang)

def apply_rope(t, cos, sin):
    tf = t.astype(jnp.float32)
    t1, t2 = jnp.split(tf, 2, axis=-1)
    c = cos[:, :, None, :]
    s = sin[:, :, None, :]
    return jnp.concatenate([t1 * c - t2 * s, t2 * c + t1 * s], axis=-1).astype(t.dtype)

def swiglu(x, w_in, w_out):
    gate, up = jnp.split(x @ w_in, 2, axis=-1)
    return (jax.nn.silu(gate) * up) @ w_out

def banded_attention(q, k, v, max_dist, sink=None):
    n, l, h, dh = q.shape
    g = k.shape[2]
    r = h // g
    blk = BAND_BLOCK
    nb = -(-l // blk)
    pad = nb * blk - l
    qp = jnp.pad(q, ((0, 0), (0, pad), (0, 0), (0, 0))).reshape(n, nb, blk, g, r, dh)

    def kv_blocks(t):
        tp = jnp.pad(t, ((0, 0), (blk, pad), (0, 0), (0, 0))).reshape(n, nb + 1, blk, g, dh)
        return jnp.concatenate([tp[:, :-1], tp[:, 1:]], axis=2)

    kb, vb = kv_blocks(k), kv_blocks(v)
    s = jnp.einsum('nbqgrd,nbkgd->nbgrqk', qp, kb, preferred_element_type=jnp.float32) * (dh ** -0.5)
    qi = jnp.arange(blk)[:, None]
    kj = jnp.arange(2 * blk)[None, :]
    dist = qi + blk - kj
    kpos = jnp.arange(nb)[:, None, None] * blk - blk + kj[None]
    valid = (dist >= 0) & (dist <= max_dist) & (kpos >= 0)
    s = jnp.where(valid[:, None, None], s, -jnp.inf)
    m = s.max(-1)
    if sink is not None:
        sk = sink.astype(jnp.float32).reshape(g, r)[:, :, None]
        m = jnp.maximum(m, sk)
    p = jnp.exp(s - m[..., None])
    den = p.sum(-1)
    if sink is not None:
        den = den + jnp.exp(sk - m)
    o = jnp.einsum('nbgrqk,nbkgd->nbqgrd', p.astype(v.dtype), vb, preferred_element_type=jnp.float32)
    o = o / den.transpose(0, 1, 4, 2, 3)[..., None]
    o = o.reshape(n, nb * blk, h, dh)[:, :l].astype(q.dtype)
    lse = (m + jnp.log(den)).transpose(0, 1, 4, 2, 3).reshape(n, nb * blk, h)[:, :l]
    return o, lse

def dilated_attention(q, k, v):
    b, s, h, dh = q.shape
    outs, lses = [], []
    for window, dil in A_CONFIGS:
        def fold(t):
            return t.reshape(b, s // dil, dil, h, dh).transpose(0, 2, 1, 3, 4).reshape(b * dil, s // dil, h, dh)
        o, lse = banded_attention(fold(q), fold(k), fold(v), window // dil)
        outs.append(o.reshape(b, dil, s // dil, h, dh).transpose(0, 2, 1, 3, 4).reshape(b, s, h, dh))
        lses.append(lse.reshape(b, dil, s // dil, h).transpose(0, 2, 1, 3).reshape(b, s, h))
    wts = jax.nn.softmax(jnp.stack(lses, 0), axis=0)
    o = jnp.einsum('cbsh,cbshd->bshd', wts, jnp.stack(outs, 0).astype(jnp.float32))
    return o.astype(q.dtype)

def dsa_attention(q, k, v, q_idx, k_idx, w_idx):
    b, s, h, dh = q.shape
    k_sel = min(TOPK_MAX, s // 4)
    nq = s // QUERY_BLOCK
    key_pos = jnp.arange(s)
    gather = jax.vmap(lambda t, ix: t[ix])

    def block(i):
        start = i * QUERY_BLOCK
        qb = lax.dynamic_slice_in_dim(q, start, QUERY_BLOCK, axis=1)
        qib = lax.dynamic_slice_in_dim(q_idx, start, QUERY_BLOCK, axis=1)
        wb = lax.dynamic_slice_in_dim(w_idx, start, QUERY_BLOCK, axis=1)
        qpos = start + jnp.arange(QUERY_BLOCK)
        causal = key_pos[None, :] <= qpos[:, None]
        dots = jnp.einsum('bqhd,bsd->bqhs', qib, k_idx, preferred_element_type=jnp.float32)
        score = jnp.einsum('bqhs,bqh->bqs', jax.nn.relu(dots), wb.astype(jnp.float32))
        score = jnp.where(causal[None], score, -jnp.inf)
        _, idx = lax.top_k(score, k_sel)
        sel_valid = idx <= qpos[None, :, None]
        kg = gather(k, idx)
        vg = gather(v, idx)
        att = jnp.einsum('bqhd,bqkd->bhqk', qb, kg, preferred_element_type=jnp.float32) * (dh ** -0.5)
        att = jnp.where(sel_valid[:, None], att, -jnp.inf)
        p = jax.nn.softmax(att, axis=-1)
        return jnp.einsum('bhqk,bqkd->bqhd', p.astype(v.dtype), vg,
                          preferred_element_type=jnp.float32).astype(q.dtype)

    out = lax.map(block, jnp.arange(nq))
    return out.transpose(1, 0, 2, 3, 4).reshape(b, s, h, dh)

def hybrid_mixer(x, cos, sin, w_in, sink_b, w_br_a, w_br_b, w_br_c, w_out):
    b, s, _ = x.shape
    proj = x @ w_in
    splits = [int(c) for c in np.cumsum(IN_SIZES)[:-1]]
    (qa, ka, va, qb, kb, vb, qc, kc, vc, qi, ki, wi, ga, gb, gc) = jnp.split(proj, splits, axis=-1)

    def heads(t, nh):
        return t.reshape(b, s, nh, -1)

    o_a = dilated_attention(apply_rope(heads(qa, A_HEADS), cos, sin),
                            apply_rope(heads(ka, A_HEADS), cos, sin),
                            heads(va, A_HEADS)).reshape(b, s, A_W)
    o_b, _ = banded_attention(apply_rope(heads(qb, B_HEADS), cos, sin),
                              apply_rope(heads(kb, B_KV_HEADS), cos, sin),
                              heads(vb, B_KV_HEADS), B_WINDOW - 1, sink_b)
    o_b = o_b.reshape(b, s, B_QW)
    o_c = dsa_attention(apply_rope(heads(qc, C_HEADS), cos, sin),
                        apply_rope(heads(kc, 1), cos, sin)[:, :, 0],
                        vc,
                        apply_rope(heads(qi, IDX_HEADS), cos, sin),
                        apply_rope(heads(ki, 1), cos, sin)[:, :, 0],
                        wi).reshape(b, s, C_W)
    merged = (jax.nn.sigmoid(ga) * (o_a @ w_br_a)
              + jax.nn.sigmoid(gb) * (o_b @ w_br_b)
              + jax.nn.sigmoid(gc) * (o_c @ w_br_c))
    return merged @ w_out

def first_inputs(seed: int = 0) -> dict:
    key = jax.random.key(seed)
    ks = jax.random.split(key, 16)
    f32 = jnp.float32

    def nrm(k, shape, scale):
        return jax.random.normal(k, shape, f32) * scale

    x = jax.random.normal(ks[0], (BATCH, SEQ, D_MODEL), f32)
    offs = jax.random.randint(ks[1], (BATCH, 1), 0, 4096, dtype=jnp.int32)
    positions = jnp.arange(SEQ, dtype=jnp.int32)[None, :] + offs
    return {
        "x": x,
        "positions": positions,
        "w_in": nrm(ks[2], (DEPTH, D_MODEL, D_IN), D_MODEL ** -0.5),
        "sink_b": nrm(ks[3], (DEPTH, B_HEADS), 0.5),
        "w_br_a": nrm(ks[4], (DEPTH, A_W, D_MODEL), A_W ** -0.5),
        "w_br_b": nrm(ks[5], (DEPTH, B_QW, D_MODEL), B_QW ** -0.5),
        "w_br_c": nrm(ks[6], (DEPTH, C_W, D_MODEL), C_W ** -0.5),
        "w_out": nrm(ks[7], (DEPTH, D_MODEL, D_MODEL), D_MODEL ** -0.5 * DN_BETA),
        "ffn1_in": nrm(ks[8], (DEPTH, D_MODEL, 2 * D_FF), D_MODEL ** -0.5),
        "ffn1_out": nrm(ks[9], (DEPTH, D_FF, D_MODEL), D_FF ** -0.5 * DN_BETA),
        "ffn2_in": nrm(ks[10], (DEPTH, D_MODEL, 2 * D_FF), D_MODEL ** -0.5),
        "ffn2_out": nrm(ks[11], (DEPTH, D_FF, D_MODEL), D_FF ** -0.5 * DN_BETA),
        "ln_g": 1.0 + nrm(ks[12], (DEPTH, 3, D_MODEL), 0.02),
        "ln_b": nrm(ks[13], (DEPTH, 3, D_MODEL), 0.02),
    }

def first_block(x, positions, w_in, sink_b, w_br_a, w_br_b, w_br_c, w_out,
              ffn1_in, ffn1_out, ffn2_in, ffn2_out, ln_g, ln_b):
    cos, sin = rope_tables(positions, HEAD_DIM)
    for l in range(DEPTH):
        x = layer_norm(DN_ALPHA * x + 0.5 * swiglu(x, ffn1_in[l], ffn1_out[l]), ln_g[l, 0], ln_b[l, 0])
        x = layer_norm(DN_ALPHA * x + hybrid_mixer(x, cos, sin, w_in[l], sink_b[l], w_br_a[l],
                                                   w_br_b[l], w_br_c[l], w_out[l]),
                       ln_g[l, 1], ln_b[l, 1])
        x = layer_norm(DN_ALPHA * x + 0.5 * swiglu(x, ffn2_in[l], ffn2_out[l]), ln_g[l, 2], ln_b[l, 2])
    return x


D_ATTN = D_MODEL // 2
ATTN_HEADS = D_ATTN // HEAD_DIM
Q_BLOCK = 128
D_CONV = D_MODEL // 4
CONV_K = 3
D_POOL = D_MODEL // 4
POOL_WINDOWS = (2, 4, 8, 16)
POOL_GROUPS = len(POOL_WINDOWS)
POOL_GROUP_DIM = D_POOL // POOL_GROUPS
POOL_OUT_DIM = D_MODEL // POOL_GROUPS
N_BRANCHES = 3
D_FF_2 = -(-8 * D_MODEL // (3 * 256)) * 256
EPS = 1e-6

IN_SIZES_2 = (D_ATTN, D_ATTN, D_ATTN, ATTN_HEADS, D_CONV, D_CONV, D_CONV, D_POOL, N_BRANCHES * D_MODEL)
D_IN_2 = sum(IN_SIZES_2)
IN_SPLITS = tuple(int(v) for v in np.cumsum(IN_SIZES_2)[:-1])


def rmsnorm(x, g):
    xf = x.astype(jnp.float32)
    y = xf * lax.rsqrt(jnp.mean(xf * xf, axis=-1, keepdims=True) + EPS)
    return (y * g.astype(jnp.float32)).astype(x.dtype)

def forgetting_attention(q, k, v, logf):
    S = q.shape[2]
    c = jnp.cumsum(logf, axis=-1)
    scale = HEAD_DIM ** -0.5
    outs = []
    for i in range(S // Q_BLOCK):
        q0, q1 = i * Q_BLOCK, (i + 1) * Q_BLOCK
        qb = q[:, :, q0:q1]
        kb = k[:, :, :q1]
        vb = v[:, :, :q1]
        logits = jnp.einsum('bhqd,bhkd->bhqk', qb, kb, preferred_element_type=jnp.float32) * scale
        logits = logits + (c[:, :, q0:q1, None] - c[:, :, None, :q1])
        causal = (q0 + jnp.arange(Q_BLOCK))[:, None] >= jnp.arange(q1)[None, :]
        logits = jnp.where(causal, logits, -jnp.inf)
        p = jax.nn.softmax(logits, axis=-1)
        outs.append(jnp.einsum('bhqk,bhkd->bhqd', p.astype(vb.dtype), vb))
    return jnp.concatenate(outs, axis=2)

def short_conv_mixer(u, b_gate, c_gate, w):
    S = u.shape[1]
    z = c_gate * u
    zp = jnp.pad(z, ((0, 0), (CONV_K - 1, 0), (0, 0)))
    conv = w[0] * zp[:, 0:S]
    for j in range(1, CONV_K):
        conv = conv + w[j] * zp[:, j:j + S]
    return b_gate * conv

def pooling_mixer(u, w_grp, scale):
    Bsz, S, _ = u.shape
    uf = u.astype(jnp.float32)
    cs = jnp.cumsum(uf, axis=1)
    t = jnp.arange(S, dtype=jnp.float32)
    groups = []
    for g, w in enumerate(POOL_WINDOWS):
        sl = slice(g * POOL_GROUP_DIM, (g + 1) * POOL_GROUP_DIM)
        csg = cs[:, :, sl]
        lagged = jnp.pad(csg[:, :S - w], ((0, 0), (w, 0), (0, 0)))
        counts = jnp.minimum(t + 1.0, float(w))[None, :, None]
        groups.append((csg - lagged) / counts - uf[:, :, sl])
    d = jnp.stack(groups, axis=2).astype(u.dtype)
    out = jnp.einsum('bsgc,gcd->bsgd', d, w_grp).reshape(Bsz, S, D_MODEL)
    return out * scale

def second_inputs(seed: int = 0) -> dict:
    key = jax.random.key(seed)
    ks = jax.random.split(key, 16)
    nrm = lambda k, shape, fan_in: jax.random.normal(k, shape, jnp.float32) * (fan_in ** -0.5)
    return {
        "x": jax.random.normal(ks[0], (BATCH, SEQ, D_MODEL), jnp.float32),
        "norm_mix_g": 1.0 + 0.02 * jax.random.normal(ks[1], (DEPTH, D_MODEL), jnp.float32),
        "w_in": nrm(ks[2], (DEPTH, D_MODEL, D_IN_2), D_MODEL),
        "forget_b": jax.random.uniform(ks[3], (DEPTH, ATTN_HEADS), jnp.float32, 2.0, 5.0),
        "q_norm_g": 1.0 + 0.02 * jax.random.normal(ks[4], (DEPTH, HEAD_DIM), jnp.float32),
        "k_norm_g": 1.0 + 0.02 * jax.random.normal(ks[5], (DEPTH, HEAD_DIM), jnp.float32),
        "w_attn_out": nrm(ks[6], (DEPTH, D_ATTN, D_MODEL), D_ATTN),
        "conv_w": nrm(ks[7], (DEPTH, CONV_K, D_CONV), CONV_K),
        "w_conv_out": nrm(ks[8], (DEPTH, D_CONV, D_MODEL), D_CONV),
        "pool_w": nrm(ks[9], (DEPTH, POOL_GROUPS, POOL_GROUP_DIM, POOL_OUT_DIM), POOL_GROUP_DIM),
        "pool_scale": 1.0 + 0.1 * jax.random.normal(ks[10], (DEPTH, D_MODEL), jnp.float32),
        "w_o": nrm(ks[11], (DEPTH, D_MODEL, D_MODEL), D_MODEL),
        "norm_ffn_g": 1.0 + 0.02 * jax.random.normal(ks[12], (DEPTH, D_MODEL), jnp.float32),
        "w_ffn_in": nrm(ks[13], (DEPTH, D_MODEL, 2 * D_FF_2), D_MODEL),
        "w_ffn_out": nrm(ks[14], (DEPTH, D_FF_2, D_MODEL), D_FF_2),
    }

def second_block(x, norm_mix_g, w_in, forget_b, q_norm_g, k_norm_g, w_attn_out, conv_w,
              w_conv_out, pool_w, pool_scale, w_o, norm_ffn_g, w_ffn_in, w_ffn_out):
    Bsz, S, _ = x.shape

    def heads(t):
        return t.reshape(Bsz, S, ATTN_HEADS, HEAD_DIM).transpose(0, 2, 1, 3)

    for l in range(DEPTH):
        h = rmsnorm(x, norm_mix_g[l])
        proj = h @ w_in[l]
        q, k, v, f_logit, cx, cb, cc, px, gate_logit = jnp.split(proj, IN_SPLITS, axis=-1)

        qh = rmsnorm(heads(q), q_norm_g[l])
        kh = rmsnorm(heads(k), k_norm_g[l])
        vh = heads(v)
        logf = jax.nn.log_sigmoid((f_logit + forget_b[l]).astype(jnp.float32)).transpose(0, 2, 1)
        a = forgetting_attention(qh, kh, vh, logf).transpose(0, 2, 1, 3).reshape(Bsz, S, D_ATTN)
        y_attn = a @ w_attn_out[l]

        y_conv = short_conv_mixer(cx, cb, cc, conv_w[l]) @ w_conv_out[l]

        y_pool = pooling_mixer(px, pool_w[l], pool_scale[l])

        g = jax.nn.sigmoid(gate_logit).reshape(Bsz, S, N_BRANCHES, D_MODEL)
        merged = g[:, :, 0] * y_attn + g[:, :, 1] * y_conv + g[:, :, 2] * y_pool
        x = x + merged @ w_o[l]

        h = rmsnorm(x, norm_ffn_g[l])
        gt, up = jnp.split(h @ w_ffn_in[l], 2, axis=-1)
        x = x + (jax.nn.silu(gt) * up) @ w_ffn_out[l]
    return x


def setup_inputs(seed=0):
    out = dict(first_inputs(seed))
    for name, value in second_inputs(seed + 1).items():
        if name != "x":
            out[name + "_2"] = value
    return out


def reference(
    x, positions, w_in, sink_b, w_br_a, w_br_b, w_br_c, w_out, ffn1_in, ffn1_out, ffn2_in,
    ffn2_out, ln_g, ln_b, norm_mix_g_2, w_in_2, forget_b_2, q_norm_g_2, k_norm_g_2,
    w_attn_out_2, conv_w_2, w_conv_out_2, pool_w_2, pool_scale_2, w_o_2, norm_ffn_g_2,
    w_ffn_in_2, w_ffn_out_2,
):
    x = first_block(
        x, positions, w_in, sink_b, w_br_a, w_br_b, w_br_c, w_out, ffn1_in, ffn1_out, ffn2_in,
        ffn2_out, ln_g, ln_b,
    )
    return second_block(
        x, norm_mix_g_2, w_in_2, forget_b_2, q_norm_g_2, k_norm_g_2, w_attn_out_2, conv_w_2,
        w_conv_out_2, pool_w_2, pool_scale_2, w_o_2, norm_ffn_g_2, w_ffn_in_2, w_ffn_out_2,
    )


_drawn_inputs = setup_inputs


def setup_inputs(seed=0):
    import zlib

    import numpy as np

    out = dict(_drawn_inputs(seed))
    spreads = {}
    factors = {'sink_b': 8.0, 'q_norm_g_2': 8.0, 'k_norm_g_2': 8.0, 'norm_ffn_g_2': 2.988}
    for name, (base, spread) in spreads.items():
        noise = np.random.default_rng([zlib.crc32(name.encode()), seed]).standard_normal(out[name].shape)
        drawn = base * np.exp(spread * noise) if base else spread * noise
        out[name] = __import__('jax').numpy.asarray(drawn.astype(out[name].dtype))
    for name, factor in factors.items():
        out[name] = (out[name] * factor).astype(out[name].dtype)
    return out
```

```python
from contextlib import ExitStack

import numpy as np

import concourse.bass as bass
from concourse import mybir

F32 = mybir.dt.float32
F32R = mybir.dt.float32r
I32 = mybir.dt.int32
ALU = mybir.AluOpType
ACT = mybir.ActivationFunctionType
AX = mybir.AxisListType.X

P = 128
SEQ, DM, LAYERS = 256, 1024, 2
TT = SEQ // P
KT = DM // P
HD = 64
HEADS = 8
DFF = 2816
PANEL = 512
FJ = DFF // 256
RING = 3
CH = 2048
DN_ALPHA = float((2 * LAYERS) ** 0.25)
LN_EPS, RMS_EPS = 1e-5, 1e-6
TOPK = 64
LAG = 16
SCALE = HD ** -0.5
MASKED = -1e30
TAKEN = -3e38
MAGIC = 12582912.0

G_FFN = 3 * FJ // RING
G_MIX1 = 36 // RING
G_MIX2 = 30 // RING
G_L1 = 2 * G_FFN + G_MIX1
G_L2 = G_FFN + G_MIX2

QA, KA, VA, QB, KB, VB, QC, KC, VC, QI, KI, WI, GATES1 = (
    0, 512, 1024, 1536, 2048, 2176, 2304, 2816, 2880, 2944, 3456, 3520, 3528)
MISC_W = 456
Q2, K2, V2, F2, CX2, CC2, GATES2 = 0, 512, 1024, 1536, 1544, 2056, 2568


def two_pi_parts():
    rest, parts = 2 * np.pi, []
    for _ in range(4):
        step = 2.0 ** (np.floor(np.log2(rest)) - 7)
        part = np.floor(rest / step) * step
        parts.append(float(part))
        rest -= part
    return parts + [float(rest)]


def shape_constants():
    t = np.arange(P)[:, None] + P
    s = np.arange(SEQ)[None, :]
    dist = t - s
    count = (dist <= 128) + 0 * dist + (dist % 4 == 0) + (dist % 16 == 0)
    count = np.where(dist >= 0, count, 0)
    mask_a = np.where(count > 0, np.log(np.maximum(count, 1)), MASKED)
    mask_b = np.where((dist >= 0) & (dist <= 127), 0.0, MASKED)
    causal = np.where(dist >= 0, 0.0, MASKED)
    up_to = (np.arange(P)[:, None] <= np.arange(SEQ)[None, :]).astype(np.float32)
    inv = 10000.0 ** (-np.arange(0, HD, 2) / HD)
    wide = np.concatenate(
        [np.eye(P), mask_a, mask_b, causal, up_to, np.broadcast_to(np.concatenate([inv, inv]), (P, HD))], 1)
    pool = np.zeros((P, 2, SEQ))
    for ch in range(2):
        for half in range(2):
            w = (2, 4, 8, 16)[2 * ch + half]
            pool[64 * half:64 * half + 64, ch] = 1.0 / np.minimum(np.arange(SEQ) + 1.0, w)
    return {"c_wide": wide.astype(np.float32), "c_pool": pool.astype(np.float32)}


def build_program(nc, d, out):
    with ExitStack() as ctx:
        def sem(name):
            return ctx.enter_context(nc.semaphore(name))

        def sb(name, shape, dt=F32, scope=ctx):
            return scope.enter_context(nc.sbuf_tensor(name, shape, dt))

        def bank(name):
            return ctx.enter_context(nc.psum_tensor(name, [P, PANEL], F32))

        A = [bank("bankA0"), bank("bankA1")]
        O = [bank(f"bankO{i}") for i in range(4)]
        T = [bank("bankT0"), bank("bankT1")]

        w_raw = sb("w_raw", [P, RING, CH])
        w_hi = sb("w_hi", [P, RING, CH], F32R)
        w_lo = sb("w_lo", [P, RING, CH], F32R)
        x = sb("x", [P, TT, DM])
        xT_hi = sb("xT_hi", [P, KT, SEQ], F32R)
        xT_lo = sb("xT_lo", [P, KT, SEQ], F32R)
        wide = sb("wide", [P, 128 + 4 * SEQ + HD])
        ident = wide[:, 0:P]
        mask_a = wide[:, 128:384]
        mask_b = wide[:, 384:640]
        causal = wide[:, 640:896]
        up_to = wide[:, 896:1152]
        inv_freq = wide[:, 1152:1152 + HD]
        cos = sb("cos", [P, TT, HD])
        sin = sb("sin", [P, TT, HD])
        stats = sb("stats", [P, TT, 2, 6])
        mean_var = sb("mean_var", [P, TT, 2])
        var_eps = sb("var_eps", [P, TT, 16])
        rstd = sb("rstd", [P, TT, 16])
        sum_sq = sb("sum_sq", [P, TT, 1])
        qk_var = sb("qk_var", [P, 2, TT, HEADS])
        qk_rstd = sb("qk_rstd", [P, 2, TT, HEADS])
        minus_half = sb("minus_half", [P, 16])

        with ExitStack() as ff:
            gb = sb("gb", [P, 2, DM], scope=ff)
            h_sb = sb("h_sb", [P, TT, 256], scope=ff)
            th_sb = sb("th_sb", [P, TT, 256], scope=ff)
            hT_hi = sb("hT_hi", [P, 2, SEQ], F32R, scope=ff)
            hT_lo = sb("hT_lo", [P, 2, SEQ], F32R, scope=ff)
            pos_i = sb("pos_i", [P, TT], I32, scope=ff)
            pos_f = sb("pos_f", [P, TT], scope=ff)
            ang = sb("ang", [P, TT, HD], scope=ff)
            turns = sb("turns", [P, TT, HD], scope=ff)
            hn = sb("hn", [P, TT, DM], scope=ff)
        with ExitStack() as mx:
            q_raw = sb("q_raw", [P, TT, PANEL], scope=mx)
            rope_out = sb("rope_out", [P, TT, PANEL], scope=mx)
            S_sb = sb("S_sb", [P, 6, PANEL], scope=mx)
            merged = S_sb[:, 0:4, :].rearrange("p (t n) c -> p t (n c)", t=TT)
            misc = sb("misc", [P, TT, MISC_W], scope=mx)
            gates = sb("gates", [P, TT, 3 * DM], scope=mx)
            qi_T = sb("qi_T", [P, 4, SEQ], scope=mx)
            qc_T = sb("qc_T", [P, 4, SEQ], scope=mx)
            kx_T = sb("kx_T", [P, 4, SEQ], scope=mx)
            va = sb("va", [P, TT, 512], scope=mx)
            pT = sb("pT", [P, CH], scope=mx)
            bias_c = sb("bias_c", [P, TT, SEQ], scope=mx)
            max8 = sb("max8", [P, TT, 8], scope=mx)
            nmax = sb("nmax", [P, TT, 3, HEADS], scope=mx)
            rsum = sb("rsum", [P, TT, 3, HEADS], scope=mx)
            rinv = sb("rinv", [P, TT, HEADS], scope=mx)
            sink = sb("sink", [P, HEADS], scope=mx)
            sinkm = sb("sinkm", [P, TT, HEADS], scope=mx)
            tmp = sb("tmp", [P, PANEL], scope=mx)
            qb_T = sb("qb_T", [P, 4, SEQ], scope=mx)
            oT_hi = {"B": sb("oT_hiB", [P, 4, SEQ], F32R, scope=mx)}
            oT_lo = {"B": sb("oT_loB", [P, 4, SEQ], F32R, scope=mx)}
            with ExitStack() as m1:
                oT_hi["C"] = sb("oT_hiC", [P, 4, SEQ], F32R, scope=m1)
                oT_lo["C"] = sb("oT_loC", [P, 4, SEQ], F32R, scope=m1)
                with ExitStack() as early:
                    ka_T = sb("ka_T", [P, 4, SEQ], scope=early)
                    rope_tmp = sb("rope_tmp", [P, PANEL], scope=early)
                oT_hi["A"] = sb("oT_hiA", [P, 4, SEQ], F32R, scope=m1)
                oT_lo["A"] = sb("oT_loA", [P, 4, SEQ], F32R, scope=m1)
            with ExitStack() as m2:
                conv_hi = sb("conv_hi", [P, 2, SEQ], F32R, scope=m2)
                conv_lo = sb("conv_lo", [P, 2, SEQ], F32R, scope=m2)
                pool_hi = sb("pool_hi", [P, 2, SEQ], F32R, scope=m2)
                pool_lo = sb("pool_lo", [P, 2, SEQ], F32R, scope=m2)
                z_pad = sb("z_pad", [P, 2, 2 + SEQ], scope=m2)
                run_b = sb("run_b", [P, 2, LAG + SEQ], scope=m2)
                inv_count = sb("inv_count", [P, 2, SEQ], scope=m2)
                conv_taps = sb("conv_taps", [P, 2, 3], scope=m2)
                wf_raw = sb("wf_raw", [P, KT, HEADS], scope=m2)
                wf_hi = sb("wf_hi", [P, KT, HEADS], F32R, scope=m2)
                wf_lo = sb("wf_lo", [P, KT, HEADS], F32R, scope=m2)
                qk_gain = sb("qk_gain", [P, 2, HD], scope=m2)
                forget = sb("forget", [P, 4, TT, HEADS], scope=m2)
        q2_T, k2_T = qi_T, qc_T
        oT_hi["D"], oT_lo["D"] = oT_hi["B"], oT_lo["B"]
        cx_sb, cb_sb = qb_T[:, 0:2, :], qb_T[:, 2:4, :]
        u_pad = misc[:].rearrange("p t c -> p (t c)")[:, 0:2 * (LAG + SEQ)].rearrange("p (c s) -> p c s", c=2)
        kx_flat = kx_T[:].rearrange("p a b -> p (a b)")
        run_a = kx_flat[:, 0:2 * (LAG + SEQ)].rearrange("p (c s) -> p c s", c=2)
        neg_cT = kx_flat[:, 2 * (LAG + SEQ):2 * (LAG + SEQ) + SEQ]
        window_d = bias_c
        logf_wide = pT[:, 0:2 * P].rearrange("p (t c) -> p t c", t=TT)
        relu = pT[:, 0:1024].rearrange("p (b c) -> p b c", b=2)
        qa_T = qi_T
        o_tile = [S_sb[:, 0, :], S_sb[:, 1, :]]

        consts_loaded = sem("consts_loaded")
        waits_met = sem("waits_met")
        x_loaded = sem("x_loaded")
        pos_loaded = sem("pos_loaded")
        setup = sem("setup")
        setup_act = sem("setup_act")
        half_set = sem("half_set")
        raw_loaded = [sem(f"raw_loaded{i}") for i in range(RING)]
        misc_loaded = [sem(f"misc_loaded{i}") for i in range(2)]
        hi_done = sem("hi_done")
        lo_done = sem("lo_done")
        chunk_used = sem("chunk_used")
        x_ready = sem("x_ready")
        xT_psum = sem("xT_psum")
        xT_hi_done = sem("xT_hi_done")
        xT_lo_done = sem("xT_lo_done")
        gu_ready = sem("gu_ready")
        th_ready = sem("th_ready")
        t1_done = sem("t1_done")
        h_ready = sem("h_ready")
        hT_psum = sem("hT_psum")
        hT_hi_done = sem("hT_hi_done")
        hT_lo_done = sem("hT_lo_done")
        acc_ready = sem("acc_ready")
        ln_step = sem("ln_step")
        var_ready = sem("var_ready")
        rstd_ready = sem("rstd_ready")
        gb_loaded = sem("gb_loaded")
        stored = sem("stored")
        sink_loaded = sem("sink_loaded")
        rope_step = sem("rope_step")
        rope_done = sem("rope_done")
        relu_done = sem("relu_done")
        acc_step = sem("acc_step")
        smax_step = sem("smax_step")
        sink_exp = sem("sink_exp")
        merge_step = sem("merge_step")

        hn_ready = sem("hn_ready")
        row_sq = sem("row_sq")
        x2_step = sem("x2_step")
        gain_loaded = sem("gain_loaded")
        small_loaded = sem("small_loaded")
        scale_loaded = sem("scale_loaded")
        qk_step = sem("qk_step")
        qk_var_ready = sem("qk_var_ready")
        qk_rstd_ready = sem("qk_rstd_ready")
        qk_half = sem("qk_half")
        qk_done = sem("qk_done")
        wf_hi_done = sem("wf_hi_done")
        wf_lo_done = sem("wf_lo_done")
        f_step = sem("f_step")
        f_exp = sem("f_exp")
        conv_step = sem("conv_step")
        conv_hi_done = sem("conv_hi_done")
        conv_lo_done = sem("conv_lo_done")
        pool_step = sem("pool_step")
        pool_made = sem("pool_made")
        pool_hi_done = sem("pool_hi_done")
        pool_lo_done = sem("pool_lo_done")
        scaled = sem("scaled")
        pads_set = sem("pads_set")
        pool_half = sem("pool_half")

        class Mixer:

            def __init__(self, tag, jobs, order, total, last_chunk, ready_no, first_gate, first_branch):
                self.ticket = {job: k for k, job in enumerate(jobs)}
                self.uses = [sum(k % 4 == b for k in range(len(jobs))) for b in range(4)]
                self.order, self.total, self.last_chunk, self.ready_no = order, total, last_chunk, ready_no
                self.first_gate, self.first_branch = first_gate, first_branch
                self.panels = len(ready_no)
                self.m_uses = [(total + 1) // 2, total // 2]
                self.splits = 2 * len(order) + 4
                self.recips = 2 * len(order) + 2 * ("B" in order)
                self.attn = 6 * len(order)
                self.panel_ready = sem(tag + "panel_ready")
                self.m_free = [[sem(f"{tag}m_free{p}{t}") for t in range(TT)] for p in range(2)]
                self.w_ready = [sem(f"{tag}w_ready{b}") for b in range(4)]
                self.w_free = [sem(f"{tag}w_free{b}") for b in range(4)]
                self.smax = sem(tag + "smax")
                self.exp_done = sem(tag + "exp_done")
                self.rinv_step = sem(tag + "rinv_step")
                self.split_hi = sem(tag + "split_hi")

            def small(self, job):
                k = self.ticket[job]
                return k % 4, SMALL[k % 4], k // 4

        def loaded(g, i):
            return g * 32 + 32 * (i // RING + 1)

        def steady(eng):
            eng.sem_inc(waits_met, 1)

        def chunk_no(g, i):
            return g * RING + (i + 1)

        def sp_chunk(sp, g, i, pieces):
            sp.wait_ge(lo_done, chunk_no(g, i))
            steady(sp)
            for dst, src in pieces:
                sp.dma_start(dst, src).then_inc(raw_loaded[i % RING], 16)

        def halves(i, src, width=PANEL):
            v = w_raw[:, i % RING, :].rearrange("p (t c) -> p t c", t=4)
            return [(v[:, 0:2, 0:width], src[:, 0:2, :]), (v[:, 2:4, 0:width], src[:, 2:4, :])]

        def act_split(act, g, i, n=CH):
            act.wait_ge(raw_loaded[i % RING], loaded(g, i))
            act.wait_ge(chunk_used, chunk_no(g, i))
            act.activation(cut(w_hi, i, n), cut(w_raw, i, n), ACT.Copy).then_inc(hi_done, 1)

        def cut(ring, i, n):
            v = ring[:, i % RING, :]
            if n == MISC_W:
                return v.rearrange("p (t c) -> p t c", t=4)[:, :, 0:n]
            return v[:, 0:n]

        def dve_split(dve, g, i, n=CH):
            dve.wait_ge(hi_done, chunk_no(g, i))
            dve.tensor_tensor(cut(w_lo, i, n), cut(w_raw, i, n), cut(w_hi, i, n).bitcast(F32),
                              ALU.subtract).then_inc(lo_done, 1)

        def three(pe, dst, hi, lo, whi, wlo, start, stop):
            pe.matmul(dst, hi, whi, start=start, stop=False, skip_group_check=True)
            pe.matmul(dst, hi, wlo, start=False, stop=False, skip_group_check=True)
            return pe.matmul(dst, lo, whi, start=False, stop=stop, skip_group_check=True)

        def pe_part(pe, i, dst, tok, k0, nk, first, last, hiT, loT, n=PANEL, col=0, pitch=PANEL):
            for t in range(nk):
                c = t * pitch + col
                mm = three(pe, dst[:, 0:n], hiT[:, k0 + t, tok * P:(tok + 1) * P],
                           loT[:, k0 + t, tok * P:(tok + 1) * P],
                           w_hi[:, i % RING, c:c + n], w_lo[:, i % RING, c:c + n],
                           first and t == 0, last and t == nk - 1)
            return mm

        def pe_panel(pe, g, i, banks, ready, n=PANEL):
            for h in range(2):
                pe.wait_ge(lo_done, chunk_no(g, i + h) + RING)
                for tok in range(TT):
                    mm = pe_part(pe, i + h, banks[tok], tok, 4 * h, 4, h == 0, h == 1, xT_hi, xT_lo, n)
                    if h == 1 and tok == 0:
                        mm.then_inc(ready, 1)
                mm.then_inc(chunk_used, 1)

        def pe_transposes(pe, ph, src, tok):
            buf, ready, base = src
            pe.wait_ge(ready, base + (tok + 1))
            for half in range(2):
                if tok == 1:
                    pe.wait_ge(xT_lo_done, ph * 4 + (half + 1))
                for q in range(4):
                    kt = 4 * half + q
                    mm = pe.transpose(T[half][:, q * P:(q + 1) * P], buf[:, tok, kt * P:(kt + 1) * P], ident)
                mm.then_inc(xT_psum, 1)

        def pe_first_panel(pe, g, ph, banks, ready, src, n=PANEL):
            for tok in range(TT):
                pe_transposes(pe, ph, src, tok)
                for h in range(2):
                    pe.wait_ge(lo_done, chunk_no(g, h) + RING)
                    pe.wait_ge(xT_lo_done, ph * 4 + (2 * tok + h + 1))
                    mm = pe_part(pe, h, banks[tok], tok, 4 * h, 4, h == 0, h == 1, xT_hi, xT_lo, n)
                    if tok == 1:
                        mm.then_inc(chunk_used, 1)
                    elif h == 1:
                        mm.then_inc(ready, 1)

        def act_xT(act, ph):
            for u in range(4):
                tok, half = divmod(u, 2)
                act.wait_ge(xT_psum, ph * 4 + (u + 1))
                act.activation(xT_hi[:, 4 * half:4 * half + 4, tok * P:(tok + 1) * P],
                               T[half].rearrange("p (k c) -> p k c", k=4), ACT.Copy).then_inc(xT_hi_done, 1)

        def dve_xT(dve, ph):
            for u in range(4):
                tok, half = divmod(u, 2)
                dve.wait_ge(xT_hi_done, ph * 4 + (u + 1))
                o = (slice(None), slice(4 * half, 4 * half + 4), slice(tok * P, (tok + 1) * P))
                dve.tensor_tensor(xT_lo[o], T[half].rearrange("p (k c) -> p k c", k=4),
                                  xT_hi[o].bitcast(F32), ALU.subtract).then_inc(xT_lo_done, 1)

        def in_chunk(k):
            return 0 if k == 0 else 3 * k - 1

        def sp_ffn(sp, g, w_in, w_out):
            def load_in(gg, i, k, h):
                v = w_raw[:, i % RING, :].rearrange("p (t s c) -> p t s c", t=4, s=2)
                sp_chunk(sp, gg, i, [(v[:, :, s, :], w_in[h, :, :, s, bass.ds(k * 256, 256)]) for s in range(2)])

            def load_out(gg, i, k):
                v = w_raw[:, i % RING, :].rearrange("p (t c) -> p t c", t=2)
                sp_chunk(sp, gg, i, [(v[:, t, :], w_out[bass.ds(k * 256 + t * P, P), :]) for t in range(2)])

            load_in(g, 0, 0, 0)
            load_in(g, 1, 0, 1)
            load_in(g, 2, 1, 0)
            load_in(g, 3, 1, 1)
            load_out(g, 4, 0)
            with sp.Fori(1, FJ - 1) as j:
                load_in(g + j, 2, j + 1, 0)
                load_in(g + j, 3, j + 1, 1)
                load_out(g + j, 4, j)
            load_out(g, 32, FJ - 1)

        def pe_ffn(pe, g, ph, f, src):
            def down(gg, i, first, last):
                pe.wait_ge(lo_done, chunk_no(gg, i) + RING)
                for tok in range(TT):
                    for n in range(2):
                        mm = pe_part(pe, i, O[2 * tok + n], tok, 0, 2, first, last, hT_hi, hT_lo,
                                     col=n * PANEL, pitch=DM)
                    if last and tok == 0:
                        mm.then_inc(acc_ready, 1)
                mm.then_inc(chunk_used, 1)

            def h_transposes(k):
                for tok in range(TT):
                    pe.wait_ge(h_ready, f * (2 * FJ) + (k * 2 + tok + 1))
                    for t in range(2):
                        mm = pe.transpose(T[0][:, (2 * t + tok) * P:(2 * t + tok + 1) * P],
                                          h_sb[:, tok, t * P:(t + 1) * P], ident)
                mm.then_inc(hT_psum, 1)

            pe_first_panel(pe, g, ph, O[0:2], gu_ready, src)
            pe_panel(pe, g, 2, A, gu_ready)
            h_transposes(0)
            pe.wait_ge(hT_lo_done, f * FJ + 1)
            down(g, 4, True, False)
            h_transposes(1)
            with pe.Fori(1, FJ - 1) as j:
                pe_panel(pe, g + j, 2, A, gu_ready)
                pe.wait_ge(hT_lo_done, f * FJ + (j + 1))
                down(g + j, 4, False, False)
                h_transposes(j + 1)
            pe.wait_ge(hT_lo_done, f * FJ + FJ)
            down(g, 32, False, True)

        def act_ffn(act, g, ph, f, prefetched, prefetch):
            def tanh(k, banks, gg, last_chunk):
                for tok in range(TT):
                    if tok == 0:
                        act.wait_ge(gu_ready, f * FJ + (k + 1))
                    else:
                        act.wait_ge(chunk_used, chunk_no(gg, last_chunk) + RING)
                    act.activation(th_sb[:, tok, :], banks[tok][:, 0:256], ACT.Tanh, scale=0.5).then_inc(th_ready, 1)

            def hT(k):
                act.wait_ge(hT_psum, f * FJ + (k + 1))
                act.activation(hT_hi[:], T[0].rearrange("p (k c) -> p k c", k=2), ACT.Copy).then_inc(hT_hi_done, 1)

            if not prefetched:
                act_split(act, g, 0)
                act_split(act, g, 1)
            act_xT(act, ph)
            act_split(act, g, 2)
            act_split(act, g, 3)
            tanh(0, O, g, 1)
            act_split(act, g, 4)
            act_split(act, g, 5)
            hT(0)
            act.wait_ge(h_ready, f * (2 * FJ) + 2)
            tanh(1, A, g, 3)
            act_split(act, g, 6)
            hT(1)
            with act.Fori(1, FJ - 2) as j:
                act_split(act, g + j, 4)
                act_split(act, g + j, 5)
                tanh(j + 1, A, g + j, 3)
                act_split(act, g + j, 6)
                hT(j + 1)
            act_split(act, g, 31)
            act_split(act, g, 32)
            tanh(FJ - 1, A, g, 30)
            if prefetch:
                prefetch(0)
            hT(FJ - 1)
            if prefetch:
                prefetch(1)

        def dve_ffn(dve, g, ph, f, prefetched, prefetch, h_scale):
            def swiglu(k, banks):
                for tok in range(TT):
                    n = k * 2 + tok + 1
                    dve.wait_ge(th_ready, f * (2 * FJ) + n)
                    dve.scalar_tensor_tensor(th_sb[:, tok, :], th_sb[:, tok, :], 1.0, banks[tok][:, 0:256],
                                             ALU.add, ALU.mult).then_inc(t1_done, 1)
                    dve.wait_ge(t1_done, f * (2 * FJ) + n)
                    dve.scalar_tensor_tensor(h_sb[:, tok, :], th_sb[:, tok, :], h_scale, banks[tok][:, 256:512],
                                             ALU.mult, ALU.mult).then_inc(h_ready, 1)

            def hT(k):
                dve.wait_ge(hT_hi_done, f * FJ + (k + 1))
                dve.tensor_tensor(hT_lo[:], T[0].rearrange("p (k c) -> p k c", k=2), hT_hi[:].bitcast(F32),
                                  ALU.subtract).then_inc(hT_lo_done, 1)

            if not prefetched:
                dve_split(dve, g, 0)
                dve_split(dve, g, 1)
            dve_xT(dve, ph)
            dve_split(dve, g, 2)
            dve_split(dve, g, 3)
            swiglu(0, O)
            dve_split(dve, g, 4)
            dve_split(dve, g, 5)
            hT(0)
            swiglu(1, A)
            dve_split(dve, g, 6)
            hT(1)
            with dve.Fori(1, FJ - 2) as j:
                dve_split(dve, g + j, 4)
                dve_split(dve, g + j, 5)
                swiglu(j + 1, A)
                dve_split(dve, g + j, 6)
                hT(j + 1)
            dve_split(dve, g, 31)
            dve_split(dve, g, 32)
            swiglu(FJ - 1, A)
            if prefetch:
                prefetch(0)
            hT(FJ - 1)
            if prefetch:
                prefetch(1)

        LN_STEPS = 7

        def dve_layer_norm(dve, g, ph, last_chunk, banks, acc):
            for tok in range(TT):
                base = ph * (2 * LN_STEPS) + tok * LN_STEPS
                if tok == 0:
                    dve.wait_ge(acc_ready, acc + 1)
                else:
                    dve.wait_ge(chunk_used, chunk_no(g, last_chunk) + RING)
                for n in range(2):
                    xs = x[:, tok, n * PANEL:(n + 1) * PANEL]
                    dve.scalar_tensor_tensor(xs, xs, DN_ALPHA, banks[tok][n][:, :], ALU.mult, ALU.add).then_inc(ln_step, 1)
                for n in range(2):
                    dve.wait_ge(ln_step, base + (n + 1))
                    dve.bn_stats(stats[:, tok, n, :], x[:, tok, n * PANEL:(n + 1) * PANEL]).then_inc(ln_step, 1)
                dve.wait_ge(ln_step, base + 4)
                steady(dve)
                dve.bn_aggr(mean_var[:, tok, :], stats[:, tok, :, :].rearrange("p a b -> p (a b)")).then_inc(ln_step, 1)
                dve.wait_ge(ln_step, base + 5)
                dve.tensor_scalar(var_eps[:, tok, 0:1], mean_var[:, tok, 1:2], LN_EPS, None, ALU.add).then_inc(var_ready, 1)
                dve.wait_ge(rstd_ready, ph * 2 + (tok + 1))
                dve.tensor_scalar(x[:, tok, :], x[:, tok, :], mean_var[:, tok, 0:1], rstd[:, tok, 0:1],
                                  ALU.subtract, ALU.mult).then_inc(ln_step, 1)
                dve.wait_ge(ln_step, base + 6)
                dve.wait_ge(gb_loaded, ph * 32 + 32)
                dve.tensor_tensor(x[:, tok, :], x[:, tok, :], gb[:, 0, :], ALU.mult).then_inc(ln_step, 1)
                dve.wait_ge(ln_step, base + 7)
                dve.tensor_tensor(x[:, tok, :], x[:, tok, :], gb[:, 1, :], ALU.add).then_inc(x_ready, 1)

        def pool_rstd(pool, ph, n=1):
            for tok in range(TT):
                pool.wait_ge(var_ready, ph * 2 + (tok + 1))
                pool.tensor_tensor(rstd[:, tok, 0:n], var_eps[:, tok, 0:n], minus_half[:, 0:n], ALU.pow).then_inc(rstd_ready, 1)

        def sp_gain_bias(sp, ph, gain, bias):
            sp.wait_ge(x_ready, ph * 2 + 2)
            steady(sp)
            sp.dma_start(gb[:, 0, :], gain.partition_broadcast(P)).then_inc(gb_loaded, 16)
            sp.dma_start(gb[:, 1, :], bias.partition_broadcast(P)).then_inc(gb_loaded, 16)

        SMALL = [O[2], O[3], T[0], T[1]]
        ROPES = 6
        jobs1 = [("rope", 0, t) for t in range(TT)]
        jobs1 += [("rope", 1, t) for t in range(TT)]
        jobs1 += [("index", u) for u in range(6)]
        jobs1 += [("rope", 2, t) for t in range(TT)]
        jobs1 += [("rope", 3, t) for t in range(TT)]
        jobs1 += [("rope", 4, t) for t in range(TT)]
        jobs1 += [("score", "B", u) for u in range(6)]
        jobs1 += [("rope", 5, t) for t in range(TT)]

        def value_jobs(n):
            return ([("pT", n, 0), ("pT", n, 1), ("pv", n, 0)] + [("pT", n, u) for u in range(2, 6)]
                    + [("pv", n, 1)])

        jobs1 += value_jobs("B")
        jobs1 += [("oT", "B", t) for t in range(TT)]
        jobs1 += [("score", "C", u) for u in range(6)] + value_jobs("C")
        jobs1 += [("oT", "C", t) for t in range(TT)]
        jobs1 += [("score", "A", u) for u in range(6)] + value_jobs("A")
        jobs1 += [("oT", "A", t) for t in range(TT)]
        jobs1 += [("mT", n, t) for n in range(2) for t in range(TT)]
        ORDER = "BCA"
        BRANCH_PANELS = [(13 + i, "BCA"[i % 3], i // 3) for i in range(6)]
        Q_OF = {"A": qa_T, "B": qb_T, "C": qc_T}
        UNITS = [(0, (0, 2, 4, 6)), (0, (1, 3, 5, 7)), (1, (0, 2)), (1, (1, 3)), (1, (4, 6)), (1, (5, 7))]

        def of_unit(ap, heads):
            return ap[:, heads[0]:heads[-1] + 1:2]

        def m_banks(i):
            return A if i % 2 == 0 else O[0:2]

        def panel_chunk(i):
            return 2 * i + 1 if i < 13 else 26 + i - 13

        M1 = Mixer("m1_", jobs1, ORDER, 19, panel_chunk, {(i, 0): i + 1 for i in range(19)}, 7, 13)

        jobs2 = [("qk", 0, t) for t in range(TT)] + [("f",)] + [("qk", 1, t) for t in range(TT)] + [("c",), ("cT",)]
        jobs2 += [("score", "D", u) for u in range(6)] + value_jobs("D") + [("oT", "D", t) for t in range(TT)]
        jobs2 += [("mT", n, t) for n in range(2) for t in range(TT)]
        POOL_CHUNK, CONV_CHUNK, ATTN_CHUNK, WO_CHUNK = 22, 23, 24, 26

        def panel_chunk2(i):
            return 2 * i + 1 if i < 11 else (POOL_CHUNK, POOL_CHUNK, CONV_CHUNK, CONV_CHUNK, ATTN_CHUNK, ATTN_CHUNK + 1)[i - 11]

        ready2 = {(i, 0): i + 1 for i in range(11)}
        for at in ((11, 0), (11, 1), (12, 0), (13, 0), (13, 1), (14, 0), (15, 0), (16, 0)):
            ready2[at] = len(ready2) + 1
        M2 = Mixer("m2_", jobs2, "D", 17, panel_chunk2, ready2, 5, 11)
        SMALL_LOADS = 7

        def sp_mix1(sp, g, ph, l):
            M = M1
            w = d["w_in"][l].rearrange("(h t p) n -> h p t n", p=P, t=4)
            for h in range(2):
                sp.wait_ge(lo_done, chunk_no(g, h))
                steady(sp)
                v = w_raw[:, h, :].rearrange("p (t c) -> p t c", t=4)
                for c, src, n, s in ((0, KB, 128, raw_loaded[h]), (128, KC, 64, raw_loaded[h]),
                                     (192, KI, 64, misc_loaded[h]), (256, VB, 128, misc_loaded[h]),
                                     (384, VC, 64, misc_loaded[h]), (448, WI, 8, misc_loaded[h])):
                    sp.dma_start(v[:, :, c:c + n], w[h, :, :, src:src + n]).then_inc(s, 16)
            sp.wait_ge(x_ready, ph * 2 + 2)
            steady(sp)
            sp.dma_start(sink[:], d["sink_b"][l].partition_broadcast(P)).then_inc(sink_loaded, 16)
            for i, c in enumerate((QI, QC, QB, QA, KA, VA, *(GATES1 + PANEL * q for q in range(6)))):
                for h in range(2):
                    sp_chunk(sp, g, 2 + 2 * i + h, halves(2 + 2 * i + h, w[h, :, :, c:c + PANEL]))
            for i, n, half in BRANCH_PANELS:
                src = d["w_br_" + n.lower()][l].rearrange("(t p) n -> p t n", p=P)
                sp_chunk(sp, g, 26 + i - 13, halves(26 + i - 13, src[:, :, half * PANEL:(half + 1) * PANEL]))
            b, _, k = M.small(("rope", 5, 1))
            sp.wait_ge(M.w_ready[b], l * M.uses[b] + (k + 1))
            steady(sp)
            sp_gain_bias(sp, ph, d["ln_g"][l, 1, :], d["ln_b"][l, 1, :])
            wo = d["w_out"][l].rearrange("(h t p) n -> h p t n", p=P, t=4)
            for i in range(4):
                h, n = divmod(i, 2)
                sp_chunk(sp, g, 32 + i, halves(32 + i, wo[h, :, :, n * PANEL:(n + 1) * PANEL]))

        def pe_common(pe, M, g, l, ml):
            def take(job):
                b, dst, k = M.small(job)
                if k:
                    pe.wait_ge(M.w_free[b], l * M.uses[b] + k)
                return b, dst

            def freed(job):
                b, _, k = M.small(job)
                pe.wait_ge(M.w_free[b], l * M.uses[b] + (k + 1))
                steady(pe)

            def panel(i, n=PANEL):
                for h in range(2):
                    pe.wait_ge(lo_done, chunk_no(g, 2 * i + h) + RING)
                    for tok in range(TT):
                        if h == 0 and i >= 2:
                            pe.wait_ge(M.m_free[i % 2][tok], l * M.m_uses[i % 2] + i // 2)
                        mm = pe_part(pe, 2 * i + h, m_banks(i)[tok], tok, 4 * h, 4, h == 0, h == 1, xT_hi, xT_lo, n)
                        if h == 1 and tok == 0:
                            mm.then_inc(M.panel_ready, 1)
                    mm.then_inc(chunk_used, 1)

            def values(n):
                for u, (tile, heads) in enumerate(UNITS):
                    b, dst = take(("pT", n, u))
                    pe.wait_ge(M.exp_done, l * M.attn + (M.order.index(n) * 6 + u + 1))
                    for q in range(4):
                        mm = pe.transpose(dst[:, q * P:(q + 1) * P], S_sb[:, u, q * P:(q + 1) * P], ident)
                    mm.then_inc(M.w_ready[b], 1)
                    if u in (1, 5):
                        b, dst = take(("pv", n, tile))
                        freed(("pT", n, u))
                        for h in range(HEADS):
                            for kk in range(tile + 1):
                                v = {"A": va[:, kk, h * 64:h * 64 + 64], "D": va[:, kk, h * 64:h * 64 + 64],
                                     "B": misc[:, kk, 256 + 64 * (h // 4):320 + 64 * (h // 4)],
                                     "C": misc[:, kk, 384:448]}[n]
                                c = (h % 2 * 4 + h // 2 if tile == 0 else (2 * (h // 4) + h % 2) * 4 + h % 4 // 2 * 2 + kk) * P
                                mm = pe.matmul(dst[:, h * 64:h * 64 + 64], pT[:, c:c + P], v,
                                               start=kk == 0, stop=kk == tile)
                        mm.then_inc(M.w_ready[b], 1)

            def o_transposes(n):
                for tok in range(TT):
                    b, dst = take(("oT", n, tok))
                    freed(("pv", n, tok))
                    for q in range(4):
                        mm = pe.transpose(dst[:, q * P:(q + 1) * P], o_tile[tok][:, q * P:(q + 1) * P], ident)
                    mm.then_inc(M.w_ready[b], 1)

            def branch(i, n, half):
                ch = M.last_chunk(i)
                pe.wait_ge(lo_done, chunk_no(g, ch) + RING)
                if half == 0:
                    freed(("oT", n, 1))
                for tok in range(TT):
                    pe.wait_ge(M.m_free[i % 2][tok], l * M.m_uses[i % 2] + i // 2)
                    mm = pe_part(pe, ch, m_banks(i)[tok], tok, 0, 4, True, True, oT_hi[n], oT_lo[n])
                    if tok == 0:
                        mm.then_inc(M.panel_ready, 1)
                mm.then_inc(chunk_used, 1)

            def merged_transposes(half, sums):
                for tok in range(TT):
                    b, dst = take(("mT", half, tok))
                    pe.wait_ge(merge_step, ml * 8 + (sums + tok + 1))
                    for q in range(4):
                        c = half * PANEL + q * P
                        mm = pe.transpose(dst[:, q * P:(q + 1) * P], merged[:, tok, c:c + P], ident)
                    mm.then_inc(M.w_ready[b], 1)

            def out_product(i, h, n, chunk):
                par = (M.total + n) % 2
                pe.wait_ge(lo_done, chunk_no(g, chunk) + RING)
                for tok in range(TT):
                    if h == 0:
                        pe.wait_ge(M.m_free[par][tok], l * M.m_uses[par] + M.m_uses[par])
                    mm = pe_part(pe, chunk, m_banks(par)[tok], tok, 4 * h, 4, h == 0, h == 1, xT_hi, xT_lo)
                    if i == 3 and tok == 0:
                        mm.then_inc(acc_ready, 1)
                mm.then_inc(chunk_used, 1)

            return take, freed, panel, values, o_transposes, branch, merged_transposes, out_product

        def pe_mix1(pe, g, ph, l):
            M = M1
            take, freed, panel, values, o_transposes, branch, merged_transposes, out_product = pe_common(pe, M, g, l, l)

            def rope_transposes(r):
                for tok in range(TT):
                    b, dst = take(("rope", r, tok))
                    pe.wait_ge(rope_done, l * (ROPES * TT) + (r * TT + tok + 1))
                    for q in range(4):
                        mm = pe.transpose(dst[:, q * P:(q + 1) * P], rope_out[:, tok, q * P:(q + 1) * P], ident)
                    mm.then_inc(M.w_ready[b], 1)

            def scores(kind, n):
                for u, (tile, heads) in enumerate(UNITS):
                    b, dst = take((kind, u) if n is None else (kind, n, u))
                    keys = P * (tile + 1)
                    for at, h in enumerate(heads):
                        half = slice(64 * (h % 2), 64 * (h % 2) + 64)
                        q = qi_T if n is None else Q_OF[n]
                        k = {None: kx_T[half, 3, 0:keys], "C": kx_T[half, 2, 0:keys],
                             "B": kx_T[half, h // 4, 0:keys], "A": ka_T[half, h // 2, 0:keys]}[n]
                        mm = pe.matmul(dst[:, at * keys:(at + 1) * keys],
                                       q[half, h // 2, tile * P:(tile + 1) * P], k, start=True, stop=True)
                    mm.then_inc(M.w_ready[b], 1)

            pe_first_panel(pe, g, ph, A, M.panel_ready, (x, x_ready, ph * 2), MISC_W)
            panel(1)
            rope_transposes(0)
            panel(2)
            rope_transposes(1)
            freed(("rope", 1, 1))
            scores("index", None)
            panel(3)
            rope_transposes(2)
            panel(4)
            rope_transposes(3)
            panel(5)
            rope_transposes(4)
            freed(("rope", 3, 1))
            scores("score", "B")
            panel(6)
            rope_transposes(5)
            values("B")
            panel(7)
            o_transposes("B")
            scores("score", "C")
            panel(8)
            values("C")
            panel(9)
            o_transposes("C")
            freed(("rope", 5, 1))
            scores("score", "A")
            panel(10)
            for tok in range(TT):
                pe.wait_ge(M.m_free[0][tok], l * M.m_uses[0] + 4)
            values("A")
            panel(11)
            o_transposes("A")
            panel(12)
            for i, n, half in BRANCH_PANELS:
                branch(i, n, half)
                if i == 16:
                    merged_transposes(0, 2)
            for i in range(4):
                h, n = divmod(i, 2)
                if i == 2:
                    merged_transposes(1, 6)
                if n == 0:
                    freed(("mT", h, 1))
                out_product(i, h, n, 32 + i)

        def act_misc_split(act, g, l, h):
            act.wait_ge(misc_loaded[h], l * 64 + 64)
            act_split(act, g, h, MISC_W)

        def act_common(act, M, g, l):
            def ready(job):
                b, src, k = M.small(job)
                act.wait_ge(M.w_ready[b], l * M.uses[b] + (k + 1))
                return b, src

            def panel_wait(i, tok):
                if (i, tok) in M.ready_no:
                    act.wait_ge(M.panel_ready, l * M.panels + M.ready_no[i, tok])
                else:
                    act.wait_ge(chunk_used, chunk_no(g, M.last_chunk(i)) + RING)

            def splits(i):
                for h in range(2):
                    if i < M.first_branch:
                        act_split(act, g, 2 * i + h)

            def exps(n):
                for u, (tile, heads) in enumerate(UNITS):
                    i = M.order.index(n)
                    act.wait_ge(M.smax, l * M.attn + (i * 6 + u + 1))
                    keys = P * (tile + 1)
                    for at, h in enumerate(heads):
                        s = S_sb[:, u, at * keys:(at + 1) * keys]
                        e = act.activation(s, s, ACT.Exp, bias=nmax[:, tile, i, h:h + 1],
                                           accum_out=rsum[:, tile, i, h:h + 1])
                    e.then_inc(M.exp_done, 1)
                if n == "B":
                    for tile in range(TT):
                        act.wait_ge(smax_step, l * 8 + (3 if tile == 0 else 8))
                        act.activation(sinkm[:, tile, :], sinkm[:, tile, :], ACT.Exp).then_inc(sink_exp, 1)

            def p_transposed(n):
                for u, (tile, heads) in enumerate(UNITS):
                    b, src = ready(("pT", n, u))
                    c = (u % 2 if tile == 0 else u - 2) * PANEL
                    act.activation(pT[:, c:c + PANEL], src[:, :], ACT.Copy).then_inc(M.w_free[b], 1)

            def o_split(n):
                for tok in range(TT):
                    b, src = ready(("oT", n, tok))
                    act.activation(oT_hi[n][:, :, tok * P:(tok + 1) * P], src.rearrange("p (k c) -> p k c", k=4),
                                   ACT.Copy).then_inc(M.split_hi, 1)

            def gate(i):
                for tok in range(TT):
                    panel_wait(i, tok)
                    c = (i - M.first_gate) * PANEL
                    act.activation(gates[:, tok, c:c + PANEL], m_banks(i)[tok][:, :], ACT.Tanh,
                                   scale=0.5).then_inc(M.m_free[i % 2][tok], 1)

            def merged_hi(half):
                for tok in range(TT):
                    b, src = ready(("mT", half, tok))
                    act.activation(xT_hi[:, 4 * half:4 * half + 4, tok * P:(tok + 1) * P],
                                   src.rearrange("p (k c) -> p k c", k=4), ACT.Copy, scale=0.5).then_inc(M.split_hi, 1)

            return ready, panel_wait, splits, exps, p_transposed, o_split, gate, merged_hi

        def act_mix1(act, g, ph, l, prefetch):
            M = M1
            ready, panel_wait, splits, exps, p_transposed, o_split, gate, merged_hi = act_common(act, M, g, l)

            def to_q_raw(r):
                for tok in range(TT):
                    panel_wait(r, tok)
                    if r >= 2:
                        act.wait_ge(rope_done, l * (ROPES * TT) + ((r - 1) * TT + tok + 1))
                    act.activation(q_raw[:, tok, :], m_banks(r)[tok][:, :], ACT.Copy).then_inc(M.m_free[r % 2][tok], 1)

            act_xT(act, ph)
            splits(1)
            for tok in range(TT):
                panel_wait(0, tok)
                act.activation(misc[:, tok, :], A[tok][:, 0:MISC_W], ACT.Copy).then_inc(M.m_free[0][tok], 1)
            splits(2)
            to_q_raw(1)
            splits(3)
            for u in range(6):
                b, src = ready(("index", u))
                if u >= 2:
                    act.wait_ge(acc_step, l * ACC_STEPS + ACC_UNIT[u - 2])
                act.activation(relu[:, u % 2, :], src[:, :], ACT.Relu).then_inc(M.w_free[b], 1)
            to_q_raw(2)
            splits(4)
            to_q_raw(3)
            splits(5)
            to_q_raw(4)
            splits(6)
            to_q_raw(5)
            exps("B")
            splits(7)
            for tok in range(TT):
                panel_wait(6, tok)
                act.activation(va[:, tok, :], A[tok][:, :], ACT.Copy).then_inc(M.m_free[0][tok], 1)
            p_transposed("B")
            splits(8)
            gate(7)
            o_split("B")
            exps("C")
            splits(9)
            gate(8)
            p_transposed("C")
            splits(10)
            gate(9)
            o_split("C")
            exps("A")
            splits(11)
            gate(10)
            p_transposed("A")
            splits(12)
            gate(11)
            o_split("A")
            act_split(act, g, 26)
            act_split(act, g, 27)
            gate(12)
            for i in range(28, 32):
                act_split(act, g, i)
            for half in range(2):
                merged_hi(half)
                for i in ((32, 33, 34), (35,))[half]:
                    act_split(act, g, i)
            if prefetch:
                act_split(act, g, 36)
                act_split(act, g, 37)

        def pool_mix1(pool, l):
            M = M1
            n = 0
            for r in range(ROPES):
                for tok in range(TT):
                    par, k = r % 2, r // 2 + 1
                    pool.wait_ge(M.m_free[par][tok], l * M.m_uses[par] + k)
                    if r:
                        b, _, kk = M.small(("rope", r - 1, tok))
                        pool.wait_ge(M.w_ready[b], l * M.uses[b] + (kk + 1))
                    nh = HEADS if r else 4
                    src = (q_raw[:, tok, :] if r else misc[:, tok, 0:256]).rearrange("p (h e) -> p h e", e=HD)
                    t = rope_tmp[:, 0:nh * HD].rearrange("p (h e) -> p h e", e=HD)
                    c = cos[:, tok, :].unsqueeze(1).broadcast_to([P, nh, HD])
                    s0 = sin[:, tok, 0:32].unsqueeze(1).broadcast_to([P, nh, 32])
                    s1 = sin[:, tok, 32:64].unsqueeze(1).broadcast_to([P, nh, 32])
                    if r:
                        outs = [rope_out[:, tok, :].rearrange("p (h e) -> p h e", e=HD)]
                    else:
                        dup = rope_out[:, tok, :].rearrange("p (h u e) -> p h u e", u=2, e=HD)
                        outs = [dup[:, :, 1, :], dup[:, :, 0, :]]
                    pool.tensor_tensor(outs[-1], src, c, ALU.mult).then_inc(rope_step, 1)
                    if r or tok:
                        pool.wait_ge(rope_done, l * (ROPES * TT) + (r * TT + tok))
                    pool.tensor_tensor(t[:, :, 0:32], src[:, :, 32:64], s0, ALU.mult).then_inc(rope_step, 1)
                    pool.tensor_tensor(t[:, :, 32:64], src[:, :, 0:32], s1, ALU.mult).then_inc(rope_step, 1)
                    n += 3
                    pool.wait_ge(rope_step, l * ROPE_STEPS + n)
                    for o in outs[:-1]:
                        pool.tensor_tensor(o, outs[-1], t, ALU.add).then_inc(rope_step, 1)
                        n += 1
                    if len(outs) > 1:
                        pool.wait_ge(rope_step, l * ROPE_STEPS + n)
                    pool.tensor_tensor(outs[-1], outs[-1], t, ALU.add).then_inc(rope_done, 1)
            assert n == ROPE_STEPS, n

        ROPE_STEPS = ROPES * TT * 3 + TT

        ACC_UNIT = [4, 8, 10, 12, 14, 16]
        ACC_STEPS = 16 + 2 * (2 * 8) + 2 * 2

        def dve_common(dve, M, g, l, ml):
            def ready(job):
                b, src, k = M.small(job)
                dve.wait_ge(M.w_ready[b], l * M.uses[b] + (k + 1))
                return b, src

            def splits(i):
                for h in range(2):
                    dve_split(dve, g, 2 * i + h, MISC_W if i == 0 and M is M1 else CH)

            def panel_wait(i, tok):
                if (i, tok) in M.ready_no:
                    dve.wait_ge(M.panel_ready, l * M.panels + M.ready_no[i, tok])
                else:
                    dve.wait_ge(chunk_used, chunk_no(g, M.last_chunk(i)) + RING)

            def normalise(n):
                i = M.order.index(n)
                for tile in range(TT):
                    dve.wait_ge(M.exp_done, l * M.attn + (i * 6 + (2 if tile == 0 else 6)))
                    r = rsum[:, tile, i, :]
                    if n == "B":
                        dve.wait_ge(sink_exp, l * 2 + (tile + 1))
                        dve.tensor_tensor(r, r, sinkm[:, tile, :], ALU.add).then_inc(M.rinv_step, 1)
                        dve.wait_ge(M.rinv_step, l * M.recips + (2 * tile + 1))
                    dve.reciprocal(rinv[:, tile, :], r).then_inc(M.rinv_step, 1)
                    k = 2 * tile + 2 if n == "B" else 2 * ("B" in M.order) + 2 * i + tile + 1
                    dve.wait_ge(M.rinv_step, l * M.recips + k)
                    b, src = ready(("pv", n, tile))
                    dve.tensor_tensor(o_tile[tile].rearrange("p (h e) -> p h e", e=HD),
                                      src.rearrange("p (h e) -> p h e", e=HD),
                                      rinv[:, tile, :].unsqueeze(2).broadcast_to([P, HEADS, HD]),
                                      ALU.mult).then_inc(M.w_free[b], 1)

            def o_split(n):
                for tok in range(TT):
                    b, src, _ = M.small(("oT", n, tok))
                    dve.wait_ge(M.split_hi, l * M.splits + (M.order.index(n) * 2 + tok + 1))
                    o = (slice(None), slice(None), slice(tok * P, (tok + 1) * P))
                    dve.tensor_tensor(oT_lo[n][o], src.rearrange("p (k c) -> p k c", k=4),
                                      oT_hi[n][o].bitcast(F32), ALU.subtract).then_inc(M.w_free[b], 1)

            def merge(i, gate, half, sums):
                for tok in range(TT):
                    panel_wait(i, tok)
                    c = gate * DM + half * PANEL
                    m = merged[:, tok, half * PANEL:(half + 1) * PANEL]
                    dst = m if sums is None else tmp[:]
                    if sums is not None and sums + tok:
                        dve.wait_ge(merge_step, ml * 8 + (sums + tok))
                    dve.scalar_tensor_tensor(dst, gates[:, tok, c:c + PANEL], 1.0, m_banks(i)[tok][:, :],
                                             ALU.add, ALU.mult).then_inc(M.m_free[i % 2][tok], 1)
                    if sums is not None:
                        dve.wait_ge(M.m_free[i % 2][tok], l * M.m_uses[i % 2] + (i // 2 + 1))
                        dve.tensor_tensor(m, m, tmp[:], ALU.add).then_inc(merge_step, 1)

            def merged_lo(half):
                for tok in range(TT):
                    b, src, _ = M.small(("mT", half, tok))
                    dve.wait_ge(M.split_hi, l * M.splits + (M.splits - 4 + half * 2 + tok + 1))
                    o = (slice(None), slice(4 * half, 4 * half + 4), slice(tok * P, (tok + 1) * P))
                    dve.scalar_tensor_tensor(xT_lo[o], src.rearrange("p (k c) -> p k c", k=4), 0.5,
                                             xT_hi[o].bitcast(F32), ALU.mult, ALU.subtract).then_inc(M.w_free[b], 1)

            return ready, splits, panel_wait, normalise, o_split, merge, merged_lo

        def dve_mix1(dve, g, ph, l, prefetch):
            M = M1
            ready, splits, panel_wait, normalise, o_split, merge, merged_lo = dve_common(dve, M, g, l, l)

            def rope_copy(r):
                dst = [kx_T, qi_T, qc_T, qb_T, qa_T, ka_T][r]
                for tok in range(TT):
                    b, src = ready(("rope", r, tok))
                    dve.tensor_copy(dst[:, :, tok * P:(tok + 1) * P],
                                    src.rearrange("p (k c) -> p k c", k=4)).then_inc(M.w_free[b], 1)

            step = [0]

            def stepped(ins):
                step[0] += 1
                ins.then_inc(acc_step, 1)

            def stepped_wait():
                dve.wait_ge(acc_step, l * ACC_STEPS + step[0])

            def index_sums():
                for u, (tile, heads) in enumerate(UNITS):
                    b, _, k = M.small(("index", u))
                    dve.wait_ge(M.w_free[b], l * M.uses[b] + (k + 1))
                    keys = P * (tile + 1)
                    acc = bias_c[:, tile, 0:keys]
                    for at, h in enumerate(heads):
                        if h:
                            stepped_wait()
                        base = acc if h else causal[:, SEQ - keys:SEQ]
                        stepped(dve.scalar_tensor_tensor(acc, relu[:, u % 2, at * keys:(at + 1) * keys],
                                                         misc[:, tile, 448 + h:449 + h], base, ALU.mult, ALU.add))

            def top_k():
                for tile in range(TT):
                    keys = P * (tile + 1)
                    s = bias_c[:, tile, 0:keys]
                    for _ in range(TOPK // 8):
                        stepped_wait()
                        steady(dve)
                        stepped(dve.max(max8[:, tile, :], s))
                        stepped_wait()
                        steady(dve)
                        stepped(dve.match_replace(s, max8[:, tile, :], s, TAKEN))
                for tile in range(TT):
                    keys = P * (tile + 1)
                    s = bias_c[:, tile, 0:keys]
                    stepped_wait()
                    stepped(dve.tensor_scalar(s, s, TAKEN / 2, MASKED, ALU.is_gt, ALU.mult))
                    stepped_wait()
                    stepped(dve.tensor_tensor(s, s, causal[:, SEQ - keys:SEQ], ALU.add))

            def logits(n):
                i = M.order.index(n)
                if n == "C":
                    stepped_wait()
                for u, (tile, heads) in enumerate(UNITS):
                    b, src = ready(("score", n, u))
                    keys = P * (tile + 1)
                    m = {"A": mask_a[:, SEQ - keys:SEQ], "B": mask_b[:, SEQ - keys:SEQ],
                         "C": bias_c[:, tile, 0:keys]}[n]
                    s = S_sb[:, u, :].rearrange("p (h k) -> p h k", k=keys)
                    dve.scalar_tensor_tensor(s, src.rearrange("p (h k) -> p h k", k=keys), SCALE,
                                             m.unsqueeze(1).broadcast_to([P, len(heads), keys]),
                                             ALU.mult, ALU.add).then_inc(M.w_free[b], 1)
                    dve.wait_ge(M.w_free[b], l * M.uses[b] + (M.small(("score", n, u))[2] + 1))
                    nm = of_unit(nmax[:, tile, i, :], heads)
                    red = dve.tensor_reduce(nm, s, AX, ALU.max, negate=True)
                    if n == "B":
                        red.then_inc(smax_step, 1)
                        dve.wait_ge(smax_step, l * 8 + (u + 1 + (u > 1)))
                        if u == 0:
                            dve.wait_ge(sink_loaded, l * 16 + 16)
                        dve.scalar_tensor_tensor(nm, of_unit(sink, heads), -1.0, nm, ALU.mult,
                                                 ALU.min).then_inc(M.smax, 1)
                        if u in (1, 5):
                            dve.wait_ge(M.smax, l * M.attn + (u + 1))
                            dve.tensor_tensor(sinkm[:, tile, :], nmax[:, tile, i, :], sink[:],
                                              ALU.add).then_inc(smax_step, 1)
                    else:
                        red.then_inc(M.smax, 1)

            dve_xT(dve, ph)
            splits(1)
            splits(2)
            rope_copy(0)
            splits(3)
            rope_copy(1)
            index_sums()
            splits(4)
            rope_copy(2)
            top_k()
            splits(5)
            rope_copy(3)
            splits(6)
            rope_copy(4)
            logits("B")
            splits(7)
            rope_copy(5)
            normalise("B")
            splits(8)
            o_split("B")
            logits("C")
            splits(9)
            normalise("C")
            splits(10)
            o_split("C")
            logits("A")
            splits(11)
            normalise("A")
            splits(12)
            o_split("A")
            for i in range(2):
                dve_split(dve, g, 26 + i)
            for i, n, half in BRANCH_PANELS:
                dve_split(dve, g, 28 + i - 13)
                merge(i, "ABC".index(n), half, None if n == ORDER[0] else 4 * half + 2 * (ORDER.index(n) - 1))
                if i == 16:
                    merged_lo(0)
            dve_split(dve, g, 34)
            merged_lo(1)
            dve_split(dve, g, 35)
            if prefetch:
                dve_split(dve, g, 36)
                dve_split(dve, g, 37)

        PH2 = 3 * LAYERS

        def act_head(act, ph):
            for tok in range(TT):
                act.wait_ge(x_ready, ph * 2 + (tok + 1))
                act.activation(hn[:, tok, :], x[:, tok, :], ACT.Square,
                               accum_out=sum_sq[:, tok, :]).then_inc(row_sq, 1)

        def dve_head(dve, ph, tok):
            n = (ph - PH2) * 2 + (tok + 1)
            dve.wait_ge(row_sq, n)
            dve.tensor_scalar(var_eps[:, tok, 0:1], sum_sq[:, tok, :], 1.0 / DM, RMS_EPS, ALU.mult,
                              ALU.add).then_inc(var_ready, 1)
            dve.wait_ge(rstd_ready, ph * 2 + (tok + 1))
            if tok == 0:
                dve.wait_ge(gain_loaded, (ph - PH2) * 16 + 16)
            dve.scalar_tensor_tensor(hn[:, tok, :], x[:, tok, :], rstd[:, tok, 0:1], gb[:, 0, :],
                                     ALU.mult, ALU.mult).then_inc(hn_ready, 1)

        def dve_tail(dve, g, ph, last_chunk, banks, tok):
            if tok == 0:
                dve.wait_ge(acc_ready, ph + 1)
            else:
                dve.wait_ge(chunk_used, chunk_no(g, last_chunk) + RING)
            for n in range(2):
                xs = x[:, tok, n * PANEL:(n + 1) * PANEL]
                add = dve.tensor_tensor(xs, xs, banks[tok][n][:, :], ALU.add)
            add.then_inc(x_ready, 1)

        def sp_mix2(sp, g, ph, l):
            w = d["w_in_2"][l].rearrange("(h t p) n -> h p t n", p=P, t=4)

            def panels(first, columns):
                for i, c in enumerate(columns):
                    for h in range(2):
                        j = 2 * (first + i) + h
                        sp_chunk(sp, g, j, halves(j, w[h, :, :, c:c + PANEL]))

            panels(0, (K2, Q2))
            sp.wait_ge(x_ready, ph * 2 + 2)
            steady(sp)
            sp.dma_start(wf_raw[:], d["w_in_2"][l].rearrange("(t p) n -> p t n", p=P)[:, :, F2:F2 + HEADS]).then_inc(small_loaded, 16)
            sp.dma_start(forget[:, 0, 0, :], d["forget_b_2"][l].partition_broadcast(P)).then_inc(small_loaded, 16)
            sp.dma_start(qk_gain[:, 0, :], d["k_norm_g_2"][l].partition_broadcast(P)).then_inc(small_loaded, 16)
            sp.dma_start(qk_gain[:, 1, :], d["q_norm_g_2"][l].partition_broadcast(P)).then_inc(small_loaded, 16)
            with nc.allow_non_contiguous_dma(reason="a channel's taps, one channel per partition"):
                for c in range(2):
                    sp.dma_start(conv_taps[:, c, :], d["conv_w_2"][l].rearrange("j (c p) -> c p j", p=P)[c]).then_inc(small_loaded, 16)
            sp.dma_start(inv_count[:], d["c_pool"]).then_inc(small_loaded, 16)
            panels(2, (V2, CX2, CC2, *(GATES2 + PANEL * q for q in range(6))))
            groups = d["pool_w_2"][l].rearrange("(b h) c n -> (h c) b n", h=2)
            v = w_raw[:, POOL_CHUNK % RING, 0:512].rearrange("p (b n) -> p b n", b=2)
            sp_chunk(sp, g, POOL_CHUNK, [(v[:, b, :], groups[:, b, :]) for b in range(2)])
            v = w_raw[:, CONV_CHUNK % RING, :].rearrange("p (t n) -> p t n", t=2)
            taps_out = d["w_conv_out_2"][l].rearrange("(t p) n -> p t n", p=P)
            sp_chunk(sp, g, CONV_CHUNK, [(v[:, t, :], taps_out[:, t, :]) for t in range(2)])
            b, _, k = M2.small(("qk", 1, 1))
            sp.wait_ge(M2.w_ready[b], l * M2.uses[b] + (k + 1))
            steady(sp)
            sp.dma_start(gb[:, 1, :], d["pool_scale_2"][l].partition_broadcast(P)).then_inc(scale_loaded, 16)
            sp.dma_start(gb[:, 0, :], d["norm_ffn_g_2"][l].partition_broadcast(P)).then_inc(gain_loaded, 16)
            src = d["w_attn_out_2"][l].rearrange("(t p) n -> p t n", p=P)
            for i in range(2):
                sp_chunk(sp, g, ATTN_CHUNK + i, halves(ATTN_CHUNK + i, src[:, :, i * PANEL:(i + 1) * PANEL]))
            wo = d["w_o_2"][l].rearrange("(h t p) n -> h p t n", p=P, t=4)
            for i in range(4):
                h, n = divmod(i, 2)
                sp_chunk(sp, g, WO_CHUNK + i, halves(WO_CHUNK + i, wo[h, :, :, n * PANEL:(n + 1) * PANEL]))

        def pe_mix2(pe, g, ph, l):
            M = M2
            ml = l + LAYERS
            take, freed, panel, values, o_transposes, branch, merged_transposes, out_product = pe_common(pe, M, g, l, ml)

            def qk_transposes(r):
                for tok in range(TT):
                    b, dst = take(("qk", r, tok))
                    pe.wait_ge(qk_done, l * 4 + (2 * r + tok + 1))
                    for q in range(4):
                        mm = pe.transpose(dst[:, q * P:(q + 1) * P], rope_out[:, tok, q * P:(q + 1) * P], ident)
                    mm.then_inc(M.w_ready[b], 1)

            def forget_product():
                b, dst = take(("f",))
                pe.wait_ge(wf_lo_done, l + 1)
                for tok in range(TT):
                    for kt in range(KT):
                        mm = three(pe, dst[:, tok * HEADS:(tok + 1) * HEADS], xT_hi[:, kt, tok * P:(tok + 1) * P],
                                   xT_lo[:, kt, tok * P:(tok + 1) * P], wf_hi[:, kt, :], wf_lo[:, kt, :],
                                   kt == 0, kt == KT - 1)
                mm.then_inc(M.w_ready[b], 1)

            def running_sums():
                b, dst = take(("c",))
                pe.wait_ge(f_step, l * F_STEPS + F_STEPS)
                pe.matmul(dst[:, 0:HEADS], up_to[:, 0:P], logf_wide[:, 0, 0:HEADS], start=True, stop=True)
                pe.matmul(dst[:, HEADS:2 * HEADS], up_to[:, P:SEQ], logf_wide[:, 0, 0:HEADS], start=True, stop=False)
                pe.matmul(dst[:, HEADS:2 * HEADS], up_to[:, 0:P], logf_wide[:, 1, 0:HEADS], start=False,
                          stop=True).then_inc(M.w_ready[b], 1)
                b, dst = take(("cT",))
                pe.matmul(dst[:, 0:SEQ], logf_wide[:, 0, :], up_to[:, 0:SEQ], start=True, stop=False, skip_group_check=True)
                pe.matmul(dst[:, P:SEQ], logf_wide[:, 1, :], up_to[:, 0:P], start=False, stop=True,
                          skip_group_check=True).then_inc(M.w_ready[b], 1)

            def channel_panel(i):
                for h in range(2):
                    pe.wait_ge(lo_done, chunk_no(g, 2 * i + h) + RING)
                    for q in range(4):
                        if h == 0 and q % 2 == 0:
                            pe.wait_ge(M.m_free[i % 2][q // 2], l * M.m_uses[i % 2] + i // 2)
                        dst = m_banks(i)[q // 2][:, (q % 2) * SEQ:(q % 2 + 1) * SEQ]
                        for t in range(4):
                            c = t * PANEL + q * P
                            s = (2 * i + h) % RING
                            mm = three(pe, dst, w_hi[:, s, c:c + P], w_lo[:, s, c:c + P], xT_hi[:, 4 * h + t, :],
                                       xT_lo[:, 4 * h + t, :], h == 0 and q % 2 == 0 and t == 0, h == 1 and t == 3)
                        if h == 1 and q == 1:
                            mm.then_inc(M.panel_ready, 1)
                    mm.then_inc(chunk_used, 1)

            def pool_product():
                pe.wait_ge(lo_done, chunk_no(g, POOL_CHUNK) + RING)
                pe.wait_ge(pool_lo_done, l + 1)
                for i in (11, 12):
                    half = slice(64 * (i - 11), 64 * (i - 11) + 64)
                    for tok in range(TT):
                        pe.wait_ge(M.m_free[i % 2][tok], l * M.m_uses[i % 2] + i // 2)
                        for c in range(2):
                            tokens = slice(tok * P, (tok + 1) * P)
                            s = POOL_CHUNK % RING
                            mm = three(pe, m_banks(i)[tok][:, c * 256:(c + 1) * 256], pool_hi[half, c, tokens],
                                       pool_lo[half, c, tokens], w_hi[half, s, c * 256:(c + 1) * 256],
                                       w_lo[half, s, c * 256:(c + 1) * 256], True, True)
                        mm.then_inc(*((M.panel_ready, 1) if i == 11 or tok == 0 else (chunk_used, 1)))

            def conv_product():
                pe.wait_ge(lo_done, chunk_no(g, CONV_CHUNK) + RING)
                pe.wait_ge(conv_lo_done, l + 1)
                for i in (13, 14):
                    for tok in range(TT):
                        pe.wait_ge(M.m_free[i % 2][tok], l * M.m_uses[i % 2] + i // 2)
                        mm = pe_part(pe, CONV_CHUNK, m_banks(i)[tok], tok, 0, 2, True, True, conv_hi, conv_lo,
                                     col=(i - 13) * PANEL, pitch=DM)
                        mm.then_inc(*((M.panel_ready, 1) if i == 13 or tok == 0 else (chunk_used, 1)))

            def scores():
                for u, (tile, heads) in enumerate(UNITS):
                    b, dst = take(("score", "D", u))
                    keys = P * (tile + 1)
                    for at, h in enumerate(heads):
                        half = slice(64 * (h % 2), 64 * (h % 2) + 64)
                        row = 64 * (h % 2) + h
                        pe.matmul(dst[:, at * keys:(at + 1) * keys], q2_T[half, h // 2, tile * P:(tile + 1) * P],
                                  k2_T[half, h // 2, 0:keys], start=True, stop=False)
                        mm = pe.matmul(dst[:, at * keys:(at + 1) * keys],
                                       ident[half, row:row + 1].broadcast_to([64, P]), neg_cT[half, 0:keys],
                                       start=False, stop=True)
                    mm.then_inc(M.w_ready[b], 1)

            pe_first_panel(pe, g, ph, A, M.panel_ready, (hn, hn_ready, (ph - PH2) * 2))
            panel(1)
            qk_transposes(0)
            forget_product()
            panel(2)
            qk_transposes(1)
            running_sums()
            channel_panel(3)
            freed(("cT",))
            scores()
            channel_panel(4)
            panel(5)
            for tok in range(TT):
                pe.wait_ge(M.m_free[0][tok], l * M.m_uses[0] + 2)
            values("D")
            panel(6)
            o_transposes("D")
            for i in range(7, 11):
                panel(i)
            pool_product()
            conv_product()
            branch(15, "D", 0)
            branch(16, "D", 1)
            merged_transposes(0, 4)
            freed(("mT", 0, 1))
            out_product(0, 0, 0, WO_CHUNK)
            merged_transposes(1, 6)
            out_product(1, 0, 1, WO_CHUNK + 1)
            freed(("mT", 1, 1))
            out_product(2, 1, 0, WO_CHUNK + 2)
            out_product(3, 1, 1, WO_CHUNK + 3)

        def act_mix2(act, g, ph, l):
            M = M2
            ready, panel_wait, splits, exps, p_transposed, o_split, gate, merged_hi = act_common(act, M, g, l)

            def staged(r):
                for tok in range(TT):
                    panel_wait(r, tok)
                    if r:
                        act.wait_ge(qk_done, l * 4 + (tok + 1))
                    act.activation(q_raw[:, tok, :], m_banks(r)[tok][:, :], ACT.Copy)
                    act.activation(S_sb[:, 2 * r + tok, :], m_banks(r)[tok][:, :], ACT.Square).then_inc(M.m_free[r % 2][tok], 1)

            act_head(act, ph)
            act_xT(act, ph)
            act.wait_ge(small_loaded, l * (16 * (SMALL_LOADS)) + 16 * (SMALL_LOADS))
            act.activation(wf_hi[:], wf_raw[:], ACT.Copy).then_inc(wf_hi_done, 1)
            splits(1)
            staged(0)
            splits(2)
            staged(1)
            act.wait_ge(f_step, l * F_STEPS + 2)
            act.activation(forget[:, 2, :, :], forget[:, 2, :, :], ACT.Exp).then_inc(f_exp, 1)
            act.wait_ge(f_step, l * F_STEPS + 3)
            act.activation(forget[:, 2, :, :], forget[:, 2, :, :], ACT.Ln).then_inc(f_exp, 1)
            splits(3)
            for tok in range(TT):
                panel_wait(2, tok)
                act.activation(va[:, tok, :], A[tok][:, :], ACT.Copy).then_inc(M.m_free[0][tok], 1)
            splits(4)
            for bank_no, dst in enumerate((cx_sb, cb_sb)):
                panel_wait(3, bank_no)
                act.activation(dst, m_banks(3)[bank_no].rearrange("p (c s) -> p c s", c=2), ACT.Copy).then_inc(M.m_free[1][bank_no], 1)
            splits(5)
            exps("D")
            panel_wait(4, 1)
            act.wait_ge(pads_set, l * PADS + PADS)
            act.activation(u_pad[:, :, LAG:], A[1].rearrange("p (c s) -> p c s", c=2), ACT.Copy).then_inc(M.m_free[0][1], 1)
            splits(6)
            act.wait_ge(conv_step, l * CONV_STEPS + CONV_STEPS)
            act.activation(conv_hi[:], tmp[:].rearrange("p (c s) -> p c s", c=2), ACT.Copy).then_inc(conv_hi_done, 1)
            gate(5)
            act.wait_ge(pool_made, l + 1)
            act.activation(pool_hi[:], window_d[:], ACT.Copy).then_inc(pool_hi_done, 1)
            p_transposed("D")
            splits(7)
            gate(6)
            o_split("D")
            splits(8)
            gate(7)
            splits(9)
            gate(8)
            splits(10)
            gate(9)
            act_split(act, g, POOL_CHUNK, 512)
            act_split(act, g, CONV_CHUNK)
            gate(10)
            for i in range(ATTN_CHUNK, WO_CHUNK + 2):
                act_split(act, g, i)
            merged_hi(0)
            act_split(act, g, WO_CHUNK + 2)
            merged_hi(1)
            act_split(act, g, WO_CHUNK + 3)

        PADS = 3
        POOL_STEPS = 7

        def pool_mix2(pool, ph, l):
            M = M2
            pool.wait_ge(xT_lo_done, ph * 4 + 4)
            steady(pool)
            pool.memset(u_pad[:, :, 0:LAG], 0.0).then_inc(pads_set, 1)
            pool.memset(z_pad[:, :, 0:2], 0.0).then_inc(pads_set, 1)
            pool.memset(logf_wide[:], 0.0).then_inc(pads_set, 1)
            for r in range(2):
                for tok in range(TT):
                    n = l * 4 + 2 * r + (tok + 1)
                    pool.wait_ge(qk_var_ready, n)
                    pool.tensor_tensor(qk_rstd[:, r, tok, :], qk_var[:, r, tok, :], minus_half[:, 0:HEADS],
                                       ALU.pow).then_inc(qk_rstd_ready, 1)
                    pool.wait_ge(qk_rstd_ready, n)
                    if r:
                        b, _, k = M.small(("qk", 0, tok))
                        pool.wait_ge(M.w_ready[b], l * M.uses[b] + (k + 1))
                    o = rope_out[:, tok, :].rearrange("p (h e) -> p h e", e=HD)
                    pool.tensor_tensor(o, q_raw[:, tok, :].rearrange("p (h e) -> p h e", e=HD),
                                       qk_rstd[:, r, tok, :].unsqueeze(2).broadcast_to([P, HEADS, HD]),
                                       ALU.mult).then_inc(qk_half, 1)
                    pool.wait_ge(qk_half, n)
                    if not r and not tok:
                        pool.wait_ge(small_loaded, l * (16 * (SMALL_LOADS)) + 16 * (SMALL_LOADS))
                    pool.tensor_tensor(o, o, qk_gain[:, r, :].unsqueeze(1).broadcast_to([P, HEADS, HD]),
                                       ALU.mult).then_inc(qk_done, 1)
            steps = [0]

            def stepped(ins):
                steps[0] += 1
                ins.then_inc(pool_step, 1)
                pool.wait_ge(pool_step, l * POOL_STEPS + steps[0])

            pool.wait_ge(M.m_free[0][1], l * M.m_uses[0] + 3)
            end = LAG + SEQ
            stepped(pool.tensor_tensor(run_a[:, :, 1:], u_pad[:, :, 1:], u_pad[:, :, 0:end - 1], ALU.add))
            stepped(pool.tensor_tensor(run_b[:, :, 3:], run_a[:, :, 3:], run_a[:, :, 1:end - 2], ALU.add))
            low, high = slice(0, 64), slice(64, 128)
            stepped(pool.tensor_tensor(window_d[low, 0, :], run_a[low, 0, LAG:], inv_count[low, 0, :], ALU.mult))
            stepped(pool.tensor_tensor(window_d[high, 0, :], run_b[high, 0, LAG:], inv_count[high, 0, :], ALU.mult))
            stepped(pool.tensor_tensor(run_a[:, 1, 7:], run_b[:, 1, 7:], run_b[:, 1, 3:end - 4], ALU.add))
            stepped(pool.tensor_tensor(window_d[low, 1, :], run_a[low, 1, LAG:], inv_count[low, 1, :], ALU.mult))
            stepped(pool.tensor_tensor(run_b[high, 1, 15:], run_a[high, 1, 15:], run_a[high, 1, 7:end - 8], ALU.add))
            pool.tensor_tensor(window_d[high, 1, :], run_b[high, 1, LAG:], inv_count[high, 1, :], ALU.mult).then_inc(pool_half, 1)
            pool.wait_ge(pool_half, l + 1)
            pool.tensor_tensor(window_d[:], window_d[:], u_pad[:, :, LAG:], ALU.subtract).then_inc(pool_made, 1)
            assert steps[0] == POOL_STEPS, steps
            pool.wait_ge(scale_loaded, l * 16 + 16)
            for tok in range(TT):
                for i in (11, 12):
                    pool.wait_ge(M.m_free[i % 2][tok], l * M.m_uses[i % 2] + (i // 2 + 1))
                pool.tensor_tensor(merged[:, tok, :], merged[:, tok, :], gb[:, 1, :], ALU.mult).then_inc(scaled, 1)

        F_STEPS = 5
        CONV_STEPS = 8

        def dve_mix2(dve, g, ph, l):
            M = M2
            ml = l + LAYERS
            ready, splits, panel_wait, normalise, o_split, merge, merged_lo = dve_common(dve, M, g, l, ml)

            def mean_squares(r):
                for tok in range(TT):
                    dve.wait_ge(M.m_free[r % 2][tok], l * M.m_uses[r % 2] + 1)
                    v = qk_var[:, r, tok, :]
                    dve.tensor_reduce(v, S_sb[:, 2 * r + tok, :].rearrange("p (h e) -> p h e", e=HD), AX,
                                      ALU.add).then_inc(qk_step, 1)
                    dve.wait_ge(qk_step, l * 4 + (2 * r + tok + 1))
                    dve.tensor_scalar(v, v, 1.0 / HD, RMS_EPS, ALU.mult, ALU.add).then_inc(qk_var_ready, 1)

            def transposed(r):
                for tok in range(TT):
                    b, src = ready(("qk", r, tok))
                    dst = (k2_T, q2_T)[r][:, :, tok * P:(tok + 1) * P]
                    src = src.rearrange("p (k c) -> p k c", k=4)
                    if r:
                        dve.tensor_scalar(dst, src, SCALE, None, ALU.mult).then_inc(M.w_free[b], 1)
                    else:
                        dve.tensor_copy(dst, src).then_inc(M.w_free[b], 1)

            def log_forget():
                bias, z, e = forget[:, 0, 0, :], forget[:, 1, :, :], forget[:, 2, :, :]
                b, src = ready(("f",))
                dve.tensor_tensor(z, src[:, 0:2 * HEADS].rearrange("p (t h) -> p t h", t=TT),
                                  bias.unsqueeze(1).broadcast_to([P, TT, HEADS]), ALU.add).then_inc(M.w_free[b], 1)
                dve.wait_ge(M.w_free[b], l * M.uses[b] + (M.small(("f",))[2] + 1))
                dve.tensor_scalar(e, z, -1.0, None, ALU.mult).then_inc(f_step, 1)
                dve.wait_ge(f_step, l * F_STEPS + 1)
                dve.tensor_tensor(e, e, z, ALU.min).then_inc(f_step, 1)
                dve.wait_ge(f_exp, l * 2 + 1)
                dve.tensor_scalar(e, e, 1.0, None, ALU.add).then_inc(f_step, 1)
                dve.wait_ge(f_exp, l * 2 + 2)
                dve.wait_ge(pads_set, l * PADS + PADS)
                for c in (0, 64):
                    dve.scalar_tensor_tensor(logf_wide[:, :, c:c + HEADS], z, 0.0, e, ALU.min,
                                             ALU.subtract).then_inc(f_step, 1)

            def sums_read():
                b, src = ready(("c",))
                dve.tensor_copy(forget[:, 3, :, :], src[:, 0:2 * HEADS].rearrange("p (t h) -> p t h", t=TT)).then_inc(M.w_free[b], 1)
                b, src = ready(("cT",))
                dve.tensor_scalar(neg_cT, src[:, 0:SEQ], -1.0, None, ALU.mult).then_inc(M.w_free[b], 1)

            def logits():
                for u, (tile, heads) in enumerate(UNITS):
                    b, src = ready(("score", "D", u))
                    keys = P * (tile + 1)
                    for at, h in enumerate(heads):
                        ins = dve.scalar_tensor_tensor(S_sb[:, u, at * keys:(at + 1) * keys], src[:, at * keys:(at + 1) * keys],
                                                       forget[:, 3, tile, h:h + 1], causal[:, SEQ - keys:SEQ],
                                                       ALU.add, ALU.add)
                    ins.then_inc(M.w_free[b], 1)
                    dve.wait_ge(M.w_free[b], l * M.uses[b] + (M.small(("score", "D", u))[2] + 1))
                    dve.tensor_reduce(of_unit(nmax[:, tile, 0, :], heads), S_sb[:, u, :].rearrange("p (h k) -> p h k", k=keys),
                                      AX, ALU.max, negate=True).then_inc(M.smax, 1)

            def convolve():
                for bank_no in range(2):
                    dve.wait_ge(M.m_free[1][bank_no], l * M.m_uses[1] + 2)
                dve.wait_ge(pads_set, l * PADS + PADS)
                panel_wait(4, 0)
                dve.tensor_tensor(z_pad[:, :, 2:], A[0].rearrange("p (c s) -> p c s", c=2), cx_sb,
                                  ALU.mult).then_inc(M.m_free[0][0], 1)
                dve.wait_ge(M.m_free[0][0], l * M.m_uses[0] + 3)
                y = [tmp[:, c * SEQ:(c + 1) * SEQ] for c in range(2)]
                n = 0
                for j in range(4):
                    for c in range(2):
                        if n >= 2:
                            dve.wait_ge(conv_step, l * CONV_STEPS + (n - 1))
                        if j == 0:
                            ins = dve.tensor_scalar(y[c], z_pad[:, c, 0:SEQ], conv_taps[:, c, 0:1], None, ALU.mult)
                        elif j < 3:
                            ins = dve.scalar_tensor_tensor(y[c], z_pad[:, c, j:j + SEQ], conv_taps[:, c, j:j + 1], y[c],
                                                           ALU.mult, ALU.add)
                        else:
                            ins = dve.tensor_tensor(y[c], y[c], cb_sb[:, c, :], ALU.mult)
                        ins.then_inc(conv_step, 1)
                        n += 1

            def pool_merge(i):
                def groups(ap):
                    return ap.rearrange("p (a b c) -> p a b c", a=2, b=2)[:, :, i - 11, :]

                for tok in range(TT):
                    panel_wait(i, tok)
                    dve.scalar_tensor_tensor(groups(merged[:, tok, :]), groups(gates[:, tok, 2 * DM:3 * DM]), 1.0,
                                             m_banks(i)[tok].rearrange("p (a c) -> p a c", a=2),
                                             ALU.add, ALU.mult).then_inc(M.m_free[i % 2][tok], 1)

            dve_xT(dve, ph)
            dve.wait_ge(wf_hi_done, l + 1)
            dve.tensor_tensor(wf_lo[:], wf_raw[:], wf_hi[:].bitcast(F32), ALU.subtract).then_inc(wf_lo_done, 1)
            splits(1)
            mean_squares(0)
            splits(2)
            transposed(0)
            mean_squares(1)
            log_forget()
            splits(3)
            transposed(1)
            sums_read()
            splits(4)
            logits()
            splits(5)
            convolve()
            splits(6)
            dve.wait_ge(conv_hi_done, l + 1)
            dve.tensor_tensor(conv_lo[:], tmp[:].rearrange("p (c s) -> p c s", c=2), conv_hi[:].bitcast(F32),
                              ALU.subtract).then_inc(conv_lo_done, 1)
            dve.wait_ge(pool_hi_done, l + 1)
            dve.tensor_tensor(pool_lo[:], window_d[:], pool_hi[:].bitcast(F32), ALU.subtract).then_inc(pool_lo_done, 1)
            normalise("D")
            splits(7)
            o_split("D")
            splits(8)
            splits(9)
            splits(10)
            dve_split(dve, g, POOL_CHUNK, 512)
            dve_split(dve, g, CONV_CHUNK)
            dve_split(dve, g, ATTN_CHUNK)
            pool_merge(11)
            pool_merge(12)
            dve_split(dve, g, ATTN_CHUNK + 1)
            dve.wait_ge(scaled, l * 2 + 2)
            merge(13, 1, 0, 0)
            merge(14, 1, 1, 2)
            dve_split(dve, g, WO_CHUNK)
            merge(15, 0, 0, 4)
            dve_split(dve, g, WO_CHUNK + 1)
            merge(16, 0, 1, 6)
            merged_lo(0)
            dve_split(dve, g, WO_CHUNK + 2)
            merged_lo(1)
            dve_split(dve, g, WO_CHUNK + 3)

        SETUP = {}

        def dve_setup(dve):
            n = [0]

            def link(ins):
                n[0] += 1
                ins.then_inc(setup, 1)
                dve.wait_ge(setup, n[0])

            dve.sem_inc(lo_done, RING)
            dve.wait_ge(pos_loaded, 16)
            dve.wait_ge(consts_loaded, 16)
            link(dve.tensor_copy(pos_f[:], pos_i[:]))
            for tok in range(TT):
                link(dve.tensor_scalar(ang[:, tok, :], inv_freq, pos_f[:, tok:tok + 1], None, ALU.mult))
            for scale in (2.0 ** 14, 1.0):
                link(dve.tensor_scalar(turns[:], ang[:], float(1 / (2 * np.pi * scale)), None, ALU.mult))
                link(dve.tensor_scalar(turns[:], turns[:], MAGIC, None, ALU.add))
                link(dve.tensor_scalar(turns[:], turns[:], -MAGIC, None, ALU.add))
                for part in two_pi_parts():
                    link(dve.scalar_tensor_tensor(ang[:], turns[:], -part * scale, ang[:], ALU.mult, ALU.add))
            link(dve.tensor_scalar(ang[:], ang[:], 3.1415925, -3.1415925, ALU.min, ALU.max))
            SETUP["angle"] = n[0]
            link(dve.tensor_scalar(turns[:], ang[:], -1.0, None, ALU.mult))
            link(dve.tensor_tensor(turns[:], turns[:], ang[:], ALU.min))
            link(dve.tensor_scalar(turns[:], turns[:], float(np.pi / 2), None, ALU.add))
            SETUP["co_angle"] = n[0]
            dve.wait_ge(setup_act, 2)
            dve.tensor_scalar(sin[:, :, 0:32], sin[:, :, 0:32], -1.0, None, ALU.mult).then_inc(setup, 1)
            SETUP["tables"] = n[0] + 1
            dve.wait_ge(x_loaded, 16)
            dve.sem_inc(x_ready, 2)

        ANGLE = 3 + 2 * (3 + 5) + 1
        CO_ANGLE = ANGLE + 3
        TABLES = CO_ANGLE + 1

        block = ctx.enter_context(nc.Block())

        @block.sync
        def _(sp):
            sp.dma_start(x[:], d["x"].rearrange("a (t p) n -> p (a t) n", p=P)).then_inc(x_loaded, 16)
            sp.dma_start(wide[:], d["c_wide"]).then_inc(consts_loaded, 16)
            with nc.allow_non_contiguous_dma(reason="256 positions, one per partition"):
                sp.dma_start(pos_i[:], d["positions"].rearrange("a (t p) -> p (a t)", p=P)).then_inc(pos_loaded, 16)

            def ffn_weights(name_in, name_out, l):
                return (d[name_in][l].rearrange("(h t p) (s f) -> h p t s f", p=P, t=4, s=2), d[name_out][l])

            with sp.Fori(0, LAYERS) as l:
                g = l * G_L1
                sp_ffn(sp, g, *ffn_weights("ffn1_in", "ffn1_out", l))
                sp_gain_bias(sp, l * 3, d["ln_g"][l, 0, :], d["ln_b"][l, 0, :])
                sp_mix1(sp, g + G_FFN, l * 3 + 1, l)
                sp_ffn(sp, g + G_FFN + G_MIX1, *ffn_weights("ffn2_in", "ffn2_out", l))
                sp_gain_bias(sp, l * 3 + 2, d["ln_g"][l, 2, :], d["ln_b"][l, 2, :])
            sp.wait_ge(x_ready, PH2 * 2 + 2)
            steady(sp)
            sp.dma_start(gb[:, 0, :], d["norm_mix_g_2"][0].partition_broadcast(P)).then_inc(gain_loaded, 16)
            with sp.Fori(0, LAYERS) as l:
                g = LAYERS * G_L1 + l * G_L2
                ph = PH2 + l * 2
                sp_mix2(sp, g, ph, l)
                sp_ffn(sp, g + G_MIX2, *ffn_weights("w_ffn_in_2", "w_ffn_out_2", l))
                sp.wait_ge(hn_ready, l * 4 + 4)
                steady(sp)
                sp.dma_start(gb[:, 0, :], d["norm_mix_g_2"][LAYERS - 1].partition_broadcast(P)).then_inc(gain_loaded, 16)
            sp.wait_ge(x_ready, (PH2 + 2 * LAYERS) * 2 + 2)
            sp.dma_start(out.rearrange("a (t p) n -> p (a t) n", p=P), x[:]).then_inc(stored, 16)
            sp.wait_ge(stored, 16)

        @block.tensor
        def _(pe):
            pe.sem_inc(chunk_used, RING)
            pe.wait_ge(consts_loaded, 16)
            with pe.Fori(0, LAYERS) as l:
                g = l * G_L1
                pe_ffn(pe, g, l * 3, l * 2, (x, x_ready, l * 6))
                pe_mix1(pe, g + G_FFN, l * 3 + 1, l)
                pe_ffn(pe, g + G_FFN + G_MIX1, l * 3 + 2, l * 2 + 1, (x, x_ready, l * 6 + 4))
            with pe.Fori(0, LAYERS) as l:
                g = LAYERS * G_L1 + l * G_L2
                ph = PH2 + l * 2
                pe_mix2(pe, g, ph, l)
                pe_ffn(pe, g + G_MIX2, ph + 1, 2 * LAYERS + l, (hn, hn_ready, l * 4 + 2))

        @block.scalar
        def _(act):
            act.wait_ge(setup, ANGLE)
            act.activation(sin[:], ang[:], ACT.Sin).then_inc(setup_act, 1)
            act.wait_ge(setup, CO_ANGLE)
            act.activation(cos[:], turns[:], ACT.Sin).then_inc(setup_act, 1)
            with act.Fori(0, LAYERS) as l:
                g = l * G_L1
                g1, g2 = g + G_FFN, g + G_FFN + G_MIX1
                act_ffn(act, g, l * 3, l * 2, False, lambda h: act_misc_split(act, g1, l, h))
                act_mix1(act, g1, l * 3 + 1, l, True)
                act_ffn(act, g2, l * 3 + 2, l * 2 + 1, True, None)
            with act.Fori(0, LAYERS) as l:
                g = LAYERS * G_L1 + l * G_L2
                ph = PH2 + l * 2
                act_split(act, g, 0)
                act_split(act, g, 1)
                act_mix2(act, g, ph, l)
                act_split(act, g + G_MIX2, 0)
                act_split(act, g + G_MIX2, 1)
                act_head(act, ph + 1)
                act_ffn(act, g + G_MIX2, ph + 1, 2 * LAYERS + l, True, None)

        @block.vector
        def _(dve):
            dve_setup(dve)
            assert SETUP == {"angle": ANGLE, "co_angle": CO_ANGLE, "tables": TABLES}, SETUP
            with dve.Fori(0, LAYERS) as l:
                g = l * G_L1
                g1, g2 = g + G_FFN, g + G_FFN + G_MIX1
                dve_ffn(dve, g, l * 3, l * 2, False, lambda h: dve_split(dve, g1, h, MISC_W), 0.25)
                dve_layer_norm(dve, g, l * 3, 32, [O[0:2], O[2:4]], l * 3)
                dve_mix1(dve, g1, l * 3 + 1, l, True)
                dve_layer_norm(dve, g1, l * 3 + 1, 35, [[O[0], A[0]], [O[1], A[1]]], l * 3 + 1)
                dve_ffn(dve, g2, l * 3 + 2, l * 2 + 1, True, None, 0.25)
                dve_layer_norm(dve, g2, l * 3 + 2, 32, [O[0:2], O[2:4]], l * 3 + 2)
            with dve.Fori(0, LAYERS) as l:
                g = LAYERS * G_L1 + l * G_L2
                ph = PH2 + l * 2
                dve_split(dve, g, 0)
                dve_split(dve, g, 1)
                for tok in range(TT):
                    dve_head(dve, ph, tok)
                dve_mix2(dve, g, ph, l)
                dve_split(dve, g + G_MIX2, 0)
                dve_split(dve, g + G_MIX2, 1)
                for tok in range(TT):
                    dve_tail(dve, g, ph, WO_CHUNK + 3, [[O[0], A[0]], [O[1], A[1]]], tok)
                    dve_head(dve, ph + 1, tok)
                dve_ffn(dve, g + G_MIX2, ph + 1, 2 * LAYERS + l, True, None, 0.5)
                for tok in range(TT):
                    dve_tail(dve, g + G_MIX2, ph + 1, 32, [O[0:2], O[2:4]], tok)

        @block.gpsimd
        def _(pool):
            pool.memset(minus_half[:], -0.5).then_inc(half_set, 1)
            pool.wait_ge(half_set, 1)
            pool.wait_ge(setup, TABLES)
            pool.wait_ge(setup_act, 2)
            with pool.Fori(0, LAYERS) as l:
                pool_rstd(pool, l * 3)
                pool_mix1(pool, l)
                pool_rstd(pool, l * 3 + 1)
                pool_rstd(pool, l * 3 + 2)
            with pool.Fori(0, LAYERS) as l:
                ph = PH2 + l * 2
                pool_rstd(pool, ph)
                pool_mix2(pool, ph, l)
                pool_rstd(pool, ph + 1)


INPUTS = ("x", "positions", "w_in", "sink_b", "w_br_a", "w_br_b", "w_br_c", "w_out", "ffn1_in", "ffn1_out",
          "ffn2_in", "ffn2_out", "ln_g", "ln_b", "norm_mix_g_2", "w_in_2", "forget_b_2", "q_norm_g_2",
          "k_norm_g_2", "w_attn_out_2", "conv_w_2", "w_conv_out_2", "pool_w_2", "pool_scale_2", "w_o_2",
          "norm_ffn_g_2", "w_ffn_in_2", "w_ffn_out_2")


def kernel(**inputs):
    import concourse.bacc as _bacc
    from concourse.bass_utils import run_bass_kernel_spmd as _run

    nc = _bacc.Bacc("TRN2", target_bir_lowering=False, num_devices=1)
    arrays, d = {}, {}
    for name, value in [(name, inputs[name]) for name in INPUTS] + list(shape_constants().items()):
        a = np.ascontiguousarray(value)
        arrays[f"in_{name}_dram"] = a
        d[name] = nc.dram_tensor(f"in_{name}_dram", a.shape, mybir.dt.from_np(a.dtype), kind="ExternalInput").ap()
    out = nc.dram_tensor("out_0_dram", (1, SEQ, DM), F32, kind="ExternalOutput").ap()
    build_program(nc, d, out)
    r = _run(nc, [arrays], core_ids=[0])
    return r.results[0]["out_0_dram"]
```

```python
from contextlib import ExitStack

import numpy as np

import concourse.bass as bass
from concourse import mybir

F32 = mybir.dt.float32
F32R = mybir.dt.float32r
I32 = mybir.dt.int32
ALU = mybir.AluOpType
ACT = mybir.ActivationFunctionType
AX = mybir.AxisListType.X

P = 128
SEQ, DM, LAYERS = 256, 1024, 2
TT = SEQ // P
KT = DM // P
HD = 64
HEADS = 8
DFF = 2816
PANEL = 512
FJ = DFF // 256
RING = 3
CH = 2048
DN_ALPHA = float((2 * LAYERS) ** 0.25)
LN_EPS, RMS_EPS = 1e-5, 1e-6
TOPK = 64
LAG = 16
SCALE = HD ** -0.5
MASKED = -1e30
TAKEN = -3e38
MAGIC = 12582912.0

G_FFN = 3 * FJ // RING
G_MIX1 = 36 // RING
G_MIX2 = 30 // RING
G_L1 = 2 * G_FFN + G_MIX1
G_L2 = G_FFN + G_MIX2

QA, KA, VA, QB, KB, VB, QC, KC, VC, QI, KI, WI, GATES1 = (
    0, 512, 1024, 1536, 2048, 2176, 2304, 2816, 2880, 2944, 3456, 3520, 3528)
MISC_W = 456
Q2, K2, V2, F2, CX2, CC2, GATES2 = 0, 512, 1024, 1536, 1544, 2056, 2568


def two_pi_parts():
    rest, parts = 2 * np.pi, []
    for _ in range(4):
        step = 2.0 ** (np.floor(np.log2(rest)) - 7)
        part = np.floor(rest / step) * step
        parts.append(float(part))
        rest -= part
    return parts + [float(rest)]


def shape_constants():
    t = np.arange(P)[:, None] + P
    s = np.arange(SEQ)[None, :]
    dist = t - s
    count = (dist <= 128) + 0 * dist + (dist % 4 == 0) + (dist % 16 == 0)
    count = np.where(dist >= 0, count, 0)
    mask_a = np.where(count > 0, np.log(np.maximum(count, 1)), MASKED)
    mask_b = np.where((dist >= 0) & (dist <= 127), 0.0, MASKED)
    causal = np.where(dist >= 0, 0.0, MASKED)
    up_to = (np.arange(P)[:, None] <= np.arange(SEQ)[None, :]).astype(np.float32)
    inv = 10000.0 ** (-np.arange(0, HD, 2) / HD)
    wide = np.concatenate(
        [np.eye(P), np.broadcast_to(np.concatenate([inv, inv]), (P, HD)), mask_a, mask_b, causal, up_to], 1)
    pool = np.zeros((P, 2, SEQ))
    for ch in range(2):
        for half in range(2):
            w = (2, 4, 8, 16)[2 * ch + half]
            pool[64 * half:64 * half + 64, ch] = 1.0 / np.minimum(np.arange(SEQ) + 1.0, w)
    return {"c_wide": wide.astype(np.float32), "c_pool": pool.astype(np.float32)}


def build_program(nc, d, out):
    with ExitStack() as ctx:
        def sem(name):
            return ctx.enter_context(nc.semaphore(name))

        def sb(name, shape, dt=F32, scope=ctx):
            return scope.enter_context(nc.sbuf_tensor(name, shape, dt))

        def bank(name):
            return ctx.enter_context(nc.psum_tensor(name, [P, PANEL], F32))

        A = [bank("bankA0"), bank("bankA1")]
        O = [bank(f"bankO{i}") for i in range(4)]
        T = [bank("bankT0"), bank("bankT1")]

        w_raw = sb("w_raw", [P, RING, CH])
        w_hi = sb("w_hi", [P, RING, CH], F32R)
        w_lo = sb("w_lo", [P, RING, CH], F32R)
        x = sb("x", [P, TT, DM])
        xT_hi = sb("xT_hi", [P, KT, SEQ], F32R)
        xT_lo = sb("xT_lo", [P, KT, SEQ], F32R)
        wide = sb("wide", [P, 128 + 4 * SEQ + HD])
        ident = wide[:, 0:P]
        inv_freq = wide[:, P:P + HD]
        mask_a, mask_b, causal, up_to = (wide[:, P + HD + i * SEQ:P + HD + (i + 1) * SEQ] for i in range(4))
        cos = sb("cos", [P, TT, HD])
        sin = sb("sin", [P, TT, HD])
        stats = sb("stats", [P, TT, 2, 6])
        mean_var = sb("mean_var", [P, TT, 2])
        var_eps = sb("var_eps", [P, TT, 16])
        rstd = sb("rstd", [P, TT, 16])
        sum_sq = sb("sum_sq", [P, TT, 1])
        qk_var = sb("qk_var", [P, 2, TT, HEADS])
        qk_rstd = sb("qk_rstd", [P, 2, TT, HEADS])
        minus_half = sb("minus_half", [P, 16])

        with ExitStack() as ff:
            gb = sb("gb", [P, 2, DM], scope=ff)
            h_sb = sb("h_sb", [P, 512], scope=ff)
            th_sb = sb("th_sb", [P, 512], scope=ff)
            hT_hi = sb("hT_hi", [P, 2, SEQ], F32R, scope=ff)
            hT_lo = sb("hT_lo", [P, 2, SEQ], F32R, scope=ff)
            last_hi = sb("last_hi", [P, 2, SEQ], F32R, scope=ff)
            last_lo = sb("last_lo", [P, 2, SEQ], F32R, scope=ff)
            pos_i = sb("pos_i", [P, TT], I32, scope=ff)
            pos_f = sb("pos_f", [P, TT], scope=ff)
            ang = sb("ang", [P, TT, HD], scope=ff)
            turns = sb("turns", [P, TT, HD], scope=ff)
            hn = sb("hn", [P, TT, DM], scope=ff)
            mix_gain = sb("mix_gain", [P, DM], scope=ff)
        with ExitStack() as mx:
            q_raw = sb("q_raw", [P, TT, PANEL], scope=mx)
            rope_out = sb("rope_out", [P, TT, PANEL], scope=mx)
            S_sb = sb("S_sb", [P, 6, PANEL], scope=mx)
            merged = S_sb[:, 0:4, :].rearrange("p (t n) c -> p t (n c)", t=TT)
            misc = sb("misc", [P, TT, MISC_W], scope=mx)
            gates = sb("gates", [P, TT, 3 * DM], scope=mx)
            qi_T = sb("qi_T", [P, 4, SEQ], scope=mx)
            qc_T = sb("qc_T", [P, 4, SEQ], scope=mx)
            kx_T = sb("kx_T", [P, 4, SEQ], scope=mx)
            va = sb("va", [P, TT, 512], scope=mx)
            pT = sb("pT", [P, CH], scope=mx)
            bias_c = sb("bias_c", [P, TT, SEQ], scope=mx)
            max8 = sb("max8", [P, TT, 8], scope=mx)
            nmax = sb("nmax", [P, TT, 3, HEADS], scope=mx)
            rsum = sb("rsum", [P, TT, 3, HEADS], scope=mx)
            rinv = sb("rinv", [P, TT, HEADS], scope=mx)
            sink = sb("sink", [P, HEADS], scope=mx)
            sinkm = sb("sinkm", [P, TT, HEADS], scope=mx)
            tmp = sb("tmp", [P, PANEL], scope=mx)
            qb_T = sb("qb_T", [P, 4, SEQ], scope=mx)
            oT_hi = {"B": sb("oT_hiB", [P, 4, SEQ], F32R, scope=mx)}
            oT_lo = {"B": sb("oT_loB", [P, 4, SEQ], F32R, scope=mx)}
            with ExitStack() as m1:
                oT_hi["C"] = sb("oT_hiC", [P, 4, SEQ], F32R, scope=m1)
                oT_lo["C"] = sb("oT_loC", [P, 4, SEQ], F32R, scope=m1)
                with ExitStack() as early:
                    ka_T = sb("ka_T", [P, 4, SEQ], scope=early)
                    rope_tmp = sb("rope_tmp", [P, PANEL], scope=early)
                oT_hi["A"] = sb("oT_hiA", [P, 4, SEQ], F32R, scope=m1)
                oT_lo["A"] = sb("oT_loA", [P, 4, SEQ], F32R, scope=m1)
            with ExitStack() as m2:
                conv_hi = sb("conv_hi", [P, 2, SEQ], F32R, scope=m2)
                conv_lo = sb("conv_lo", [P, 2, SEQ], F32R, scope=m2)
                pool_hi = sb("pool_hi", [P, 2, SEQ], F32R, scope=m2)
                pool_lo = sb("pool_lo", [P, 2, SEQ], F32R, scope=m2)
                z_pad = sb("z_pad", [P, 2, 2 + SEQ], scope=m2)
                run_b = sb("run_b", [P, 2, LAG + SEQ], scope=m2)
                inv_count = sb("inv_count", [P, 2, SEQ], scope=m2)
                conv_taps = sb("conv_taps", [P, 2, 3], scope=m2)
                wf_raw = sb("wf_raw", [P, KT, HEADS], scope=m2)
                wf = sb("wf", [P, KT, 2 * HEADS], F32R, scope=m2)
                qk_gain = sb("qk_gain", [P, 2, HD], scope=m2)
                forget = sb("forget", [P, 4, TT, HEADS], scope=m2)
        q2_T, k2_T = qi_T, qc_T
        oT_hi["D"], oT_lo["D"] = oT_hi["B"], oT_lo["B"]
        cx_sb, cb_sb = qb_T[:, 0:2, :], qb_T[:, 2:4, :]
        u_pad = misc[:].rearrange("p t c -> p (t c)")[:, 0:2 * (LAG + SEQ)].rearrange("p (c s) -> p c s", c=2)
        kx_flat = kx_T[:].rearrange("p a b -> p (a b)")
        run_a = kx_flat[:, 0:2 * (LAG + SEQ)].rearrange("p (c s) -> p c s", c=2)
        neg_cT = kx_flat[:, 2 * (LAG + SEQ):2 * (LAG + SEQ) + SEQ]
        window_d = bias_c
        logf_wide = pT[:, 0:2 * P].rearrange("p (t c) -> p t c", t=TT)
        relu = pT[:, 0:1024].rearrange("p (b c) -> p b c", b=2)
        qa_T = qi_T
        addend = [tmp[:], pT[:, 0:PANEL]]
        o_tile = [S_sb[:, 0, :], S_sb[:, 1, :]]

        consts_loaded = sem("consts_loaded")
        masks_loaded = sem("masks_loaded")
        waits_met = sem("waits_met")
        x_loaded = sem("x_loaded")
        pos_loaded = sem("pos_loaded")
        setup = sem("setup")
        setup_act = sem("setup_act")
        half_set = sem("half_set")
        raw_loaded = [sem(f"raw_loaded{i}") for i in range(RING)]
        misc_loaded = [sem(f"misc_loaded{i}") for i in range(2)]
        hi_done = sem("hi_done")
        lo_done = sem("lo_done")
        chunk_used = sem("chunk_used")
        x_ready = sem("x_ready")
        xT_psum = sem("xT_psum")
        xT_hi_done = sem("xT_hi_done")
        xT_lo_done = sem("xT_lo_done")
        gu_ready = sem("gu_ready")
        th_ready = sem("th_ready")
        t1_done = sem("t1_done")
        h_ready = sem("h_ready")
        hT_psum = sem("hT_psum")
        hT_hi_done = sem("hT_hi_done")
        hT_lo_done = sem("hT_lo_done")
        acc_ready = sem("acc_ready")
        ln_step = sem("ln_step")
        var_ready = sem("var_ready")
        rstd_ready = sem("rstd_ready")
        gb_loaded = sem("gb_loaded")
        stored = sem("stored")
        sink_loaded = sem("sink_loaded")
        rope_step = sem("rope_step")
        rope_done = sem("rope_done")
        acc_step = sem("acc_step")
        smax_step = sem("smax_step")
        sink_exp = sem("sink_exp")
        merge_step = sem("merge_step")

        hn_ready = sem("hn_ready")
        row_sq = sem("row_sq")
        gain_loaded = sem("gain_loaded")
        small_loaded = sem("small_loaded")
        scale_loaded = sem("scale_loaded")
        qk_step = sem("qk_step")
        qk_var_ready = sem("qk_var_ready")
        qk_rstd_ready = sem("qk_rstd_ready")
        qk_half = sem("qk_half")
        qk_done = sem("qk_done")
        wf_hi_done = sem("wf_hi_done")
        wf_lo_done = sem("wf_lo_done")
        f_step = sem("f_step")
        f_exp = sem("f_exp")
        conv_step = sem("conv_step")
        conv_hi_done = sem("conv_hi_done")
        conv_lo_done = sem("conv_lo_done")
        pool_step = sem("pool_step")
        pool_made = sem("pool_made")
        pool_hi_done = sem("pool_hi_done")
        pool_lo_done = sem("pool_lo_done")
        scaled = sem("scaled")
        pads_set = sem("pads_set")
        pool_half = sem("pool_half")

        class Mixer:

            def __init__(self, tag, jobs, order, total, last_chunk, ready_no, first_gate, first_branch):
                self.ticket = {job: k for k, job in enumerate(jobs)}
                self.uses = [sum(k % 4 == b for k in range(len(jobs))) for b in range(4)]
                self.order, self.total, self.last_chunk, self.ready_no = order, total, last_chunk, ready_no
                self.first_gate, self.first_branch = first_gate, first_branch
                self.panels = len(ready_no)
                self.m_uses = [(total + 1) // 2, total // 2]
                self.splits = 2 * len(order) + 4
                self.recips = 2 * len(order) + 2 * ("B" in order)
                self.attn = 6 * len(order)
                self.panel_ready = sem(tag + "panel_ready")
                self.m_free = [[sem(f"{tag}m_free{p}{t}") for t in range(TT)] for p in range(2)]
                self.w_ready = [sem(f"{tag}w_ready{b}") for b in range(4)]
                self.w_free = [sem(f"{tag}w_free{b}") for b in range(4)]
                self.smax = sem(tag + "smax")
                self.exp_done = sem(tag + "exp_done")
                self.rinv_step = sem(tag + "rinv_step")
                self.split_hi = sem(tag + "split_hi")

            def small(self, job):
                k = self.ticket[job]
                return k % 4, SMALL[k % 4], k // 4

        def loaded(g, i):
            return g * 32 + 32 * (i // RING + 1)

        def steady(eng):
            eng.sem_inc(waits_met, 1)

        def chunk_no(g, i):
            return g * RING + (i + 1)

        def sp_chunk(sp, g, i, pieces):
            sp.wait_ge(lo_done, chunk_no(g, i))
            steady(sp)
            for dst, src in pieces:
                sp.dma_start(dst, src).then_inc(raw_loaded[i % RING], 16)

        def halves(i, src, width=PANEL):
            v = w_raw[:, i % RING, :].rearrange("p (t c) -> p t c", t=4)
            return [(v[:, 0:2, 0:width], src[:, 0:2, :]), (v[:, 2:4, 0:width], src[:, 2:4, :])]

        def act_split(act, g, i, n=CH):
            act.wait_ge(raw_loaded[i % RING], loaded(g, i))
            act.wait_ge(chunk_used, chunk_no(g, i))
            act.activation(cut(w_hi, i, n), cut(w_raw, i, n), ACT.Copy).then_inc(hi_done, 1)

        def cut(ring, i, n):
            v = ring[:, i % RING, :]
            if n == MISC_W:
                return v.rearrange("p (t c) -> p t c", t=4)[:, :, 0:n]
            return v[:, 0:n]

        def dve_split(dve, g, i, n=CH):
            dve.wait_ge(hi_done, chunk_no(g, i))
            dve.tensor_tensor(cut(w_lo, i, n), cut(w_raw, i, n), cut(w_hi, i, n).bitcast(F32),
                              ALU.subtract).then_inc(lo_done, 1)

        def three(pe, dst, hi, lo, whi, wlo, start, stop):
            pe.matmul(dst, hi, whi, start=start, stop=False, skip_group_check=True)
            pe.matmul(dst, hi, wlo, start=False, stop=False, skip_group_check=True)
            return pe.matmul(dst, lo, whi, start=False, stop=stop, skip_group_check=True)

        def pe_part(pe, i, dst, tok, k0, nk, first, last, hiT, loT, n=PANEL, col=0, pitch=PANEL):
            for t in range(nk):
                c = t * pitch + col
                mm = three(pe, dst[:, 0:n], hiT[:, k0 + t, tok * P:(tok + 1) * P],
                           loT[:, k0 + t, tok * P:(tok + 1) * P],
                           w_hi[:, i % RING, c:c + n], w_lo[:, i % RING, c:c + n],
                           first and t == 0, last and t == nk - 1)
            return mm

        def pe_transposes(pe, ph, src, tok):
            buf, ready, base = src
            pe.wait_ge(ready, base + (tok + 1))
            for half in range(2):
                if tok == 1:
                    pe.wait_ge(xT_lo_done, ph * 4 + (half + 1))
                for q in range(4):
                    kt = 4 * half + q
                    mm = pe.transpose(T[half][:, q * P:(q + 1) * P], buf[:, tok, kt * P:(kt + 1) * P], ident)
                mm.then_inc(xT_psum, 1)

        def pe_first_panel(pe, g, ph, banks, ready, src, n=PANEL):
            for tok in range(TT):
                pe_transposes(pe, ph, src, tok)
                for h in range(2):
                    pe.wait_ge(lo_done, chunk_no(g, h) + RING)
                    pe.wait_ge(xT_lo_done, ph * 4 + (2 * tok + h + 1))
                    mm = pe_part(pe, h, banks[tok], tok, 4 * h, 4, h == 0, h == 1, xT_hi, xT_lo, n)
                    if tok == 1:
                        mm.then_inc(chunk_used, 1)
                    elif h == 1:
                        mm.then_inc(ready, 1)

        def act_xT(act, ph):
            for u in range(4):
                tok, half = divmod(u, 2)
                act.wait_ge(xT_psum, ph * 4 + (u + 1))
                act.activation(xT_hi[:, 4 * half:4 * half + 4, tok * P:(tok + 1) * P],
                               T[half].rearrange("p (k c) -> p k c", k=4), ACT.Copy).then_inc(xT_hi_done, 1)

        def dve_xT(dve, ph, tok):
            for half in range(2):
                dve.wait_ge(xT_hi_done, ph * 4 + (2 * tok + half + 1))
                o = (slice(None), slice(4 * half, 4 * half + 4), slice(tok * P, (tok + 1) * P))
                dve.tensor_tensor(xT_lo[o], T[half].rearrange("p (k c) -> p k c", k=4),
                                  xT_hi[o].bitcast(F32), ALU.subtract).then_inc(xT_lo_done, 1)

        def sp_ffn(sp, g, w_in, w_out):
            def load_in(gg, i, k, h):
                v = w_raw[:, i % RING, :].rearrange("p (t s c) -> p t s c", t=4, s=2)
                sp_chunk(sp, gg, i, [(v[:, :, s, :], w_in[h, :, :, s, bass.ds(k * 256, 256)]) for s in range(2)])

            def load_out(gg, i, k):
                v = w_raw[:, i % RING, :].rearrange("p (t c) -> p t c", t=2)
                sp_chunk(sp, gg, i, [(v[:, t, :], w_out[bass.ds(k * 256 + t * P, P), :]) for t in range(2)])

            load_in(g, 0, 0, 0)
            load_in(g, 1, 0, 1)
            load_in(g, 2, 1, 0)
            load_in(g, 3, 1, 1)
            load_out(g, 4, 0)
            with sp.Fori(1, FJ - 1) as j:
                load_in(g + j, 2, j + 1, 0)
                load_in(g + j, 3, j + 1, 1)
                load_out(g + j, 4, j)
            load_out(g, 32, FJ - 1)

        H_STEPS = FJ + 1

        def pe_ffn(pe, g, ph, f, src):
            def down(i, tok, first, last, hi, lo):
                for n in range(2):
                    mm = pe_part(pe, i, O[2 * tok + n], tok, 0, 2, first, last, hi, lo, col=n * PANEL, pitch=DM)
                return mm

            def gate_up(gg, i, between=None):
                for h in range(2):
                    if h == 1 and between:
                        between()
                    pe.wait_ge(lo_done, chunk_no(gg, i + h) + RING)
                    for s in range(2):
                        for q in range(2):
                            for t in range(4):
                                c = t * PANEL + s * 256 + q * P
                                mm = three(pe, A[s][:, q * SEQ:(q + 1) * SEQ], w_hi[:, (i + h) % RING, c:c + P],
                                           w_lo[:, (i + h) % RING, c:c + P], xT_hi[:, 4 * h + t, :],
                                           xT_lo[:, 4 * h + t, :], h == 0 and q == 0 and t == 0, h == 1 and t == 3)
                        if h == 1 and s == 0:
                            mm.then_inc(gu_ready, 1)
                    mm.then_inc(chunk_used, 1)

            pe_first_panel(pe, g, ph, O[0:2], gu_ready, src)

            def h_transposes():
                for tok in range(TT):
                    pe.wait_ge(h_ready, f * H_STEPS + (tok + 1))
                    for t in range(2):
                        mm = pe.transpose(T[0][:, (2 * t + tok) * P:(2 * t + tok + 1) * P],
                                          h_sb[:, tok * 256 + t * P:tok * 256 + (t + 1) * P], ident)
                mm.then_inc(hT_psum, 1)

            gate_up(g, 2, between=h_transposes)
            pe.wait_ge(hT_lo_done, f * FJ + 1)
            pe.wait_ge(lo_done, chunk_no(g, 4) + RING)
            for tok in range(TT):
                mm = down(4, tok, True, False, hT_hi, hT_lo)
            mm.then_inc(chunk_used, 1)
            with pe.Fori(1, FJ - 2) as j:
                pe.wait_ge(h_ready, f * H_STEPS + (j + 2))
                gate_up(g + j, 2)
                pe.wait_ge(hT_lo_done, f * FJ + (j + 1))
                pe.wait_ge(lo_done, chunk_no(g + j, 4) + RING)
                for tok in range(TT):
                    mm = down(4, tok, False, False, hT_hi, hT_lo)
                mm.then_inc(chunk_used, 1)
            pe.wait_ge(h_ready, f * H_STEPS + FJ)
            gate_up(g, 29)
            pe.wait_ge(hT_lo_done, f * FJ + (FJ - 1))
            pe.wait_ge(lo_done, chunk_no(g, 31) + RING)
            down(31, 0, False, False, hT_hi, hT_lo)
            pe.wait_ge(hT_lo_done, f * FJ + FJ)
            pe.wait_ge(lo_done, chunk_no(g, 32) + RING)
            down(32, 0, False, True, last_hi, last_lo).then_inc(acc_ready, 1)
            down(31, 1, False, False, hT_hi, hT_lo).then_inc(chunk_used, 1)
            down(32, 1, False, True, last_hi, last_lo).then_inc(chunk_used, 1)

        def act_ffn(act, g, ph, f, prefetched, prefetch):
            def first_tanh():
                for tok in range(TT):
                    if tok == 0:
                        act.wait_ge(gu_ready, f * FJ + 1)
                    else:
                        act.wait_ge(chunk_used, chunk_no(g, 1) + RING)
                    act.activation(th_sb[:, tok * 256:(tok + 1) * 256], O[tok][:, 0:256], ACT.Tanh,
                                   scale=0.5).then_inc(th_ready, 1)

            def tanh(k):
                act.wait_ge(h_ready, f * H_STEPS + (k + 1))
                act.wait_ge(gu_ready, f * FJ + (k + 1))
                act.activation(th_sb[:], A[0][:, :], ACT.Tanh, scale=0.5).then_inc(th_ready, 1)

            def hT(k, dst, gg=None):
                act.wait_ge(h_ready, f * H_STEPS + (k + 2))
                if gg is not None:
                    act.wait_ge(chunk_used, chunk_no(gg, 1) + RING)
                act.activation(dst[:], h_sb[:].rearrange("p (t c) -> p t c", t=2), ACT.Copy).then_inc(hT_hi_done, 1)

            if not prefetched:
                act_split(act, g, 0)
                act_split(act, g, 1)
            act_xT(act, ph)
            act_split(act, g, 2)
            act_split(act, g, 3)
            first_tanh()
            act_split(act, g, 4)
            act.wait_ge(hT_psum, f + 1)
            act.activation(hT_hi[:], T[0].rearrange("p (k c) -> p k c", k=2), ACT.Copy).then_inc(hT_hi_done, 1)
            act_split(act, g, 5)
            tanh(1)
            act_split(act, g, 6)
            hT(1, hT_hi, g + 1)
            with act.Fori(1, FJ - 2) as j:
                act_split(act, g + j, 4)
                act_split(act, g + j, 5)
                tanh(j + 1)
                act_split(act, g + j, 6)
                hT(j + 1, hT_hi, g + (j + 1))
            act_split(act, g, 31)
            act_split(act, g, 32)
            tanh(FJ - 1)
            hT(FJ - 1, last_hi)
            if prefetch:
                prefetch(0)
                prefetch(1)

        def dve_ffn(dve, g, ph, f, h_scale):
            def swiglu(n, th, gate, up, h, wait_up=None):
                dve.wait_ge(th_ready, n)
                dve.scalar_tensor_tensor(th, th, 1.0, gate, ALU.add, ALU.mult).then_inc(t1_done, 1)
                dve.wait_ge(t1_done, n)
                if wait_up is not None:
                    dve.wait_ge(chunk_used, wait_up)
                dve.scalar_tensor_tensor(h, th, h_scale, up, ALU.mult, ALU.mult).then_inc(h_ready, 1)

            def step(k, gg, i):
                swiglu(f * H_STEPS + (k + 2), th_sb[:], A[0][:, :], A[1][:, :], h_sb[:], chunk_no(gg, i) + RING)

            def hT(k, hi, lo):
                dve.wait_ge(hT_hi_done, f * FJ + (k + 1))
                dve.tensor_tensor(lo[:], h_sb[:].rearrange("p (t c) -> p t c", t=2), hi[:].bitcast(F32),
                                  ALU.subtract).then_inc(hT_lo_done, 1)

            dve_split(dve, g, 2)
            dve_split(dve, g, 3)
            for tok in range(TT):
                c = slice(tok * 256, (tok + 1) * 256)
                swiglu(f * H_STEPS + (tok + 1), th_sb[:, c], O[tok][:, 0:256], O[tok][:, 256:512], h_sb[:, c])
            dve_split(dve, g, 4)
            dve.wait_ge(hT_hi_done, f * FJ + 1)
            dve.tensor_tensor(hT_lo[:], T[0].rearrange("p (k c) -> p k c", k=2), hT_hi[:].bitcast(F32),
                              ALU.subtract).then_inc(hT_lo_done, 1)
            dve_split(dve, g, 5)
            step(1, g, 3)
            dve_split(dve, g, 6)
            hT(1, hT_hi, hT_lo)
            with dve.Fori(1, FJ - 2) as j:
                dve_split(dve, g + j, 4)
                dve_split(dve, g + j, 5)
                step(j + 1, g + j, 3)
                dve_split(dve, g + j, 6)
                hT(j + 1, hT_hi, hT_lo)
            dve_split(dve, g, 31)
            dve_split(dve, g, 32)
            step(FJ - 1, g, 30)
            hT(FJ - 1, last_hi, last_lo)

        FFN_BANKS, MIX_BANKS = [O[0:2], O[2:4]], [[O[0], A[0]], [O[1], A[1]]]

        LN_STEPS = 6

        def ln_sums(dve, g, ph, last_chunk, banks, tok):
            base = ph * (2 * LN_STEPS) + tok * LN_STEPS
            if tok == 0:
                dve.wait_ge(acc_ready, ph + 1)
            else:
                dve.wait_ge(chunk_used, chunk_no(g, last_chunk) + RING)
            for n in range(2):
                xs = x[:, tok, n * PANEL:(n + 1) * PANEL]
                dve.scalar_tensor_tensor(xs, xs, DN_ALPHA, banks[tok][n][:, :], ALU.mult, ALU.add).then_inc(ln_step, 1)
            for n in range(2):
                dve.wait_ge(ln_step, base + (n + 1))
                dve.bn_stats(stats[:, tok, n, :], x[:, tok, n * PANEL:(n + 1) * PANEL]).then_inc(ln_step, 1)
            dve.wait_ge(ln_step, base + 4)
            steady(dve)
            dve.bn_aggr(mean_var[:, tok, :], stats[:, tok, :, :].rearrange("p a b -> p (a b)")).then_inc(ln_step, 1)
            dve.wait_ge(ln_step, base + 5)
            dve.tensor_scalar(var_eps[:, tok, 0:1], mean_var[:, tok, 1:2], LN_EPS, None, ALU.add).then_inc(var_ready, 1)

        def ln_apply(dve, ph, tok):
            base = ph * (2 * LN_STEPS) + tok * LN_STEPS
            dve.wait_ge(gb_loaded, ph * 32 + 32)
            dve.scalar_tensor_tensor(x[:, tok, :], x[:, tok, :], mean_var[:, tok, 0:1], gb[:, 0, :],
                                     ALU.subtract, ALU.mult).then_inc(ln_step, 1)
            dve.wait_ge(rstd_ready, ph * 2 + (tok + 1))
            steady(dve)
            dve.wait_ge(ln_step, base + 6)
            dve.scalar_tensor_tensor(x[:, tok, :], x[:, tok, :], rstd[:, tok, 0:1], gb[:, 1, :],
                                     ALU.mult, ALU.add).then_inc(x_ready, 1)

        def pool_rstd(pool, ph, n=1):
            for tok in range(TT):
                pool.wait_ge(var_ready, ph * 2 + (tok + 1))
                pool.tensor_tensor(rstd[:, tok, 0:n], var_eps[:, tok, 0:n], minus_half[:, 0:n], ALU.pow).then_inc(rstd_ready, 1)

        def sp_gain_bias(sp, ph, gain, bias):
            sp.wait_ge(x_ready, ph * 2 + 2)
            steady(sp)
            sp.dma_start(gb[:, 0, :], gain.partition_broadcast(P)).then_inc(gb_loaded, 16)
            sp.dma_start(gb[:, 1, :], bias.partition_broadcast(P)).then_inc(gb_loaded, 16)

        SMALL = [O[2], O[3], T[0], T[1]]
        ROPES = 6
        jobs1 = [("rope", 0, t) for t in range(TT)]
        jobs1 += [("rope", 1, t) for t in range(TT)]
        jobs1 += [("index", u) for u in range(6)]
        jobs1 += [("rope", 2, t) for t in range(TT)]
        jobs1 += [("rope", 3, t) for t in range(TT)]
        jobs1 += [("score", "B", u) for u in range(6)]
        jobs1 += [("rope", 4, t) for t in range(TT)]
        jobs1 += [("rope", 5, t) for t in range(TT)]

        def value_jobs(n):
            return [("pT", n, 0), ("pT", n, 1), ("pT", n, 2), ("pT", n, 3), ("pv", n, 0), ("pT", n, 4), ("pT", n, 5),
                    ("pv", n, 1)]

        jobs1 += value_jobs("B")
        jobs1 += [("oT", "B", t) for t in range(TT)]
        jobs1 += [("score", "C", u) for u in range(6)] + value_jobs("C")
        jobs1 += [("oT", "C", t) for t in range(TT)]
        jobs1 += [("score", "A", u) for u in range(6)] + value_jobs("A")
        jobs1 += [("oT", "A", t) for t in range(TT)]
        jobs1 += [("mT", n, t) for n in range(2) for t in range(TT)]
        ORDER = "BCA"
        BRANCH_PANELS = [(13 + i, "BCA"[i % 3], i // 3) for i in range(6)]
        Q_OF = {"A": qa_T, "B": qb_T, "C": qc_T}
        UNITS = [(0, (0, 2, 4, 6)), (0, (1, 3, 5, 7)), (1, (0, 2)), (1, (1, 3)), (1, (4, 6)), (1, (5, 7))]

        def of_unit(ap, heads):
            return ap[:, heads[0]:heads[-1] + 1:2]

        def m_banks(i):
            return A if i % 2 == 0 else O[0:2]

        def panel_chunk(i):
            return 2 * i + 1 if i < 13 else 26 + i - 13

        M1 = Mixer("m1_", jobs1, ORDER, 19, panel_chunk, {(i, 0): i + 1 for i in range(19)}, 7, 13)

        jobs2 = [("qk", 0, t) for t in range(TT)] + [("f",)] + [("qk", 1, t) for t in range(TT)] + [("c",), ("cT",)]
        jobs2 += [("score", "D", u) for u in range(6)] + value_jobs("D") + [("oT", "D", t) for t in range(TT)]
        jobs2 += [("mT", n, t) for n in range(2) for t in range(TT)]
        POOL_CHUNK, CONV_CHUNK, ATTN_CHUNK, WO_CHUNK = 22, 23, 24, 26

        def panel_chunk2(i):
            branches = (POOL_CHUNK, POOL_CHUNK, CONV_CHUNK, CONV_CHUNK, ATTN_CHUNK, ATTN_CHUNK + 1)
            return 2 * i + 1 if i < 11 else branches[i - 11]

        ready2 = {(i, 0): i + 1 for i in range(11)}
        for at in ((11, 0), (11, 1), (12, 0), (13, 0), (13, 1), (14, 0), (15, 0), (16, 0)):
            ready2[at] = len(ready2) + 1
        M2 = Mixer("m2_", jobs2, "D", 17, panel_chunk2, ready2, 5, 11)
        SMALL_LOADS = 7

        def sp_mix1(sp, g, ph, l):
            M = M1
            w = d["w_in"][l].rearrange("(h t p) n -> h p t n", p=P, t=4)
            for h in range(2):
                sp.wait_ge(lo_done, chunk_no(g, h))
                steady(sp)
                v = w_raw[:, h, :].rearrange("p (t c) -> p t c", t=4)
                for c, src, n, s in ((0, KB, 128, raw_loaded[h]), (128, KC, 64, raw_loaded[h]),
                                     (192, KI, 64, misc_loaded[h]), (256, VB, 128, misc_loaded[h]),
                                     (384, VC, 64, misc_loaded[h]), (448, WI, 8, misc_loaded[h])):
                    sp.dma_start(v[:, :, c:c + n], w[h, :, :, src:src + n]).then_inc(s, 16)
            for i, c in enumerate((QI, QC, QB, QA, KA, VA, *(GATES1 + PANEL * q for q in range(6)))):
                for h in range(2):
                    sp_chunk(sp, g, 2 + 2 * i + h, halves(2 + 2 * i + h, w[h, :, :, c:c + PANEL]))
                if i == 1:
                    sp.wait_ge(x_ready, ph * 2 + 2)
                    steady(sp)
                    sp.dma_start(sink[:], d["sink_b"][l].partition_broadcast(P)).then_inc(sink_loaded, 16)
            for i, n, half in BRANCH_PANELS:
                src = d["w_br_" + n.lower()][l].rearrange("(t p) n -> p t n", p=P)
                sp_chunk(sp, g, 26 + i - 13, halves(26 + i - 13, src[:, :, half * PANEL:(half + 1) * PANEL]))
            b, _, k = M.small(("rope", 5, 1))
            sp.wait_ge(M.w_ready[b], l * M.uses[b] + (k + 1))
            steady(sp)
            sp_gain_bias(sp, ph, d["ln_g"][l, 1, :], d["ln_b"][l, 1, :])
            wo = d["w_out"][l].rearrange("(h t p) n -> h p t n", p=P, t=4)
            for i in range(4):
                h, n = divmod(i, 2)
                sp_chunk(sp, g, 32 + i, halves(32 + i, wo[h, :, :, n * PANEL:(n + 1) * PANEL]))

        def pe_common(pe, M, g, l, ml):
            def take(job):
                b, dst, k = M.small(job)
                if k:
                    pe.wait_ge(M.w_free[b], l * M.uses[b] + k)
                return b, dst

            def freed(job):
                b, _, k = M.small(job)
                pe.wait_ge(M.w_free[b], l * M.uses[b] + (k + 1))
                steady(pe)

            def panel(i, n=PANEL):
                for h in range(2):
                    pe.wait_ge(lo_done, chunk_no(g, 2 * i + h) + RING)
                    for tok in range(TT):
                        if h == 0 and i >= 2:
                            pe.wait_ge(M.m_free[i % 2][tok], l * M.m_uses[i % 2] + i // 2)
                        mm = pe_part(pe, 2 * i + h, m_banks(i)[tok], tok, 4 * h, 4, h == 0, h == 1, xT_hi, xT_lo, n)
                        if h == 1 and tok == 0:
                            mm.then_inc(M.panel_ready, 1)
                    mm.then_inc(chunk_used, 1)

            def values(n):
                for u, (tile, heads) in enumerate(UNITS):
                    b, dst = take(("pT", n, u))
                    pe.wait_ge(M.exp_done, l * M.attn + (M.order.index(n) * 6 + u + 1))
                    for q in range(4):
                        mm = pe.transpose(dst[:, q * P:(q + 1) * P], S_sb[:, u, q * P:(q + 1) * P], ident)
                    mm.then_inc(M.w_ready[b], 1)
                    if u in (3, 5):
                        tile = u // 5
                        b, dst = take(("pv", n, tile))
                        for h in range(HEADS):
                            if tile == 0 and h == 0:
                                freed(("pT", n, 1))
                            elif tile == 1 and h in (0, 4):
                                freed(("pT", n, 3 + h // 2))
                            for kk in range(tile + 1):
                                v = {"A": va[:, kk, h * 64:h * 64 + 64], "D": va[:, kk, h * 64:h * 64 + 64],
                                     "B": misc[:, kk, 256 + 64 * (h // 4):320 + 64 * (h // 4)],
                                     "C": misc[:, kk, 384:448]}[n]
                                unit = h % 2 if tile == 0 else 2 + 2 * (h // 4) + h % 2
                                c = (unit % 4 * 4 + (h // 2 if tile == 0 else h % 4 // 2 * 2 + kk)) * P
                                mm = pe.matmul(dst[:, h * 64:h * 64 + 64], pT[:, c:c + P], v,
                                               start=kk == 0, stop=kk == tile)
                        mm.then_inc(M.w_ready[b], 1)

            def o_transposes(n):
                for tok in range(TT):
                    b, dst = take(("oT", n, tok))
                    freed(("pv", n, tok))
                    for q in range(4):
                        mm = pe.transpose(dst[:, q * P:(q + 1) * P], o_tile[tok][:, q * P:(q + 1) * P], ident)
                    mm.then_inc(M.w_ready[b], 1)

            def branch(i, n, half):
                ch = M.last_chunk(i)
                pe.wait_ge(lo_done, chunk_no(g, ch) + RING)
                if half == 0:
                    freed(("oT", n, 1))
                for tok in range(TT):
                    pe.wait_ge(M.m_free[i % 2][tok], l * M.m_uses[i % 2] + i // 2)
                    mm = pe_part(pe, ch, m_banks(i)[tok], tok, 0, 4, True, True, oT_hi[n], oT_lo[n])
                    if tok == 0:
                        mm.then_inc(M.panel_ready, 1)
                mm.then_inc(chunk_used, 1)

            def merged_transposes(half, sums):
                for tok in range(TT):
                    b, dst = take(("mT", half, tok))
                    pe.wait_ge(merge_step, ml * 8 + (sums + tok + 1))
                    for q in range(4):
                        c = half * PANEL + q * P
                        mm = pe.transpose(dst[:, q * P:(q + 1) * P], merged[:, tok, c:c + P], ident)
                    mm.then_inc(M.w_ready[b], 1)

            def out_product(n, chunk):
                par = (M.total + n) % 2
                pe.wait_ge(lo_done, chunk_no(g, chunk) + RING)
                for tok in range(TT):
                    pe.wait_ge(M.m_free[par][tok], l * M.m_uses[par] + M.m_uses[par])
                    mm = pe_part(pe, chunk, m_banks(par)[tok], tok, 0, 4, True, False, xT_hi, xT_lo)
                mm.then_inc(chunk_used, 1)

            def out_product_end(chunk):
                for tok in range(TT):
                    for n in range(2):
                        if tok == 0:
                            pe.wait_ge(lo_done, chunk_no(g, chunk + n) + RING)
                        mm = pe_part(pe, chunk + n, m_banks(M.total + n)[tok], tok, 4, 4, False, True, xT_hi, xT_lo)
                        if tok == 1:
                            mm.then_inc(chunk_used, 1)
                        elif n == 1:
                            mm.then_inc(acc_ready, 1)

            return take, freed, panel, values, o_transposes, branch, merged_transposes, out_product, out_product_end

        def pe_mix1(pe, g, ph, l):
            M = M1
            (take, freed, panel, values, o_transposes, branch, merged_transposes, out_product,
             out_product_end) = pe_common(pe, M, g, l, l)

            def rope_transposes(r):
                for tok in range(TT):
                    b, dst = take(("rope", r, tok))
                    pe.wait_ge(rope_done, l * (ROPES * TT) + (r * TT + tok + 1))
                    for q in range(4):
                        mm = pe.transpose(dst[:, q * P:(q + 1) * P], rope_out[:, tok, q * P:(q + 1) * P], ident)
                    mm.then_inc(M.w_ready[b], 1)

            def scores(kind, n):
                for u, (tile, heads) in enumerate(UNITS):
                    b, dst = take((kind, u) if n is None else (kind, n, u))
                    keys = P * (tile + 1)
                    for at, h in enumerate(heads):
                        half = slice(64 * (h % 2), 64 * (h % 2) + 64)
                        q = qi_T if n is None else Q_OF[n]
                        k = {None: kx_T[half, 3, 0:keys], "C": kx_T[half, 2, 0:keys],
                             "B": kx_T[half, h // 4, 0:keys], "A": ka_T[half, h // 2, 0:keys]}[n]
                        mm = pe.matmul(dst[:, at * keys:(at + 1) * keys],
                                       q[half, h // 2, tile * P:(tile + 1) * P], k, start=True, stop=True)
                    mm.then_inc(M.w_ready[b], 1)

            pe_first_panel(pe, g, ph, A, M.panel_ready, (x, x_ready, ph * 2), MISC_W)
            panel(1)
            rope_transposes(0)
            panel(2)
            rope_transposes(1)
            freed(("rope", 1, 1))
            scores("index", None)
            panel(3)
            rope_transposes(2)
            panel(4)
            rope_transposes(3)
            panel(5)
            freed(("rope", 3, 1))
            scores("score", "B")
            rope_transposes(4)
            panel(6)
            rope_transposes(5)
            values("B")
            panel(7)
            o_transposes("B")
            scores("score", "C")
            panel(8)
            values("C")
            panel(9)
            o_transposes("C")
            freed(("rope", 5, 1))
            scores("score", "A")
            panel(10)
            for tok in range(TT):
                pe.wait_ge(M.m_free[0][tok], l * M.m_uses[0] + 4)
            values("A")
            panel(11)
            o_transposes("A")
            panel(12)
            for i, n, half in BRANCH_PANELS:
                branch(i, n, half)
                if i == 16:
                    merged_transposes(0, 2)
            freed(("mT", 0, 1))
            out_product(0, 32)
            merged_transposes(1, 6)
            out_product(1, 33)
            freed(("mT", 1, 1))
            out_product_end(34)

        def act_misc_split(act, g, l, h):
            act.wait_ge(misc_loaded[h], l * 64 + 64)
            act_split(act, g, h, MISC_W)

        def act_common(act, M, g, l):
            def ready(job):
                b, src, k = M.small(job)
                act.wait_ge(M.w_ready[b], l * M.uses[b] + (k + 1))
                return b, src

            def panel_wait(i, tok):
                if (i, tok) in M.ready_no:
                    act.wait_ge(M.panel_ready, l * M.panels + M.ready_no[i, tok])
                else:
                    act.wait_ge(chunk_used, chunk_no(g, M.last_chunk(i)) + RING)

            def splits(i):
                for h in range(2):
                    if i < M.first_branch:
                        act_split(act, g, 2 * i + h)

            def exps(n):
                for u, (tile, heads) in enumerate(UNITS):
                    i = M.order.index(n)
                    act.wait_ge(M.smax, l * M.attn + (i * 6 + u + 1))
                    keys = P * (tile + 1)
                    for at, h in enumerate(heads):
                        s = S_sb[:, u, at * keys:(at + 1) * keys]
                        e = act.activation(s, s, ACT.Exp, bias=nmax[:, tile, i, h:h + 1],
                                           accum_out=rsum[:, tile, i, h:h + 1])
                    e.then_inc(M.exp_done, 1)
                if n == "B":
                    for tile in range(TT):
                        act.wait_ge(smax_step, l * 8 + (3 if tile == 0 else 8))
                        act.activation(sinkm[:, tile, :], sinkm[:, tile, :], ACT.Exp).then_inc(sink_exp, 1)

            def p_transposed(n):
                for u, (tile, heads) in enumerate(UNITS):
                    b, src = ready(("pT", n, u))
                    c = u % 4 * PANEL
                    act.activation(pT[:, c:c + PANEL], src[:, :], ACT.Copy).then_inc(M.w_free[b], 1)

            def o_split(n):
                for tok in range(TT):
                    b, src = ready(("oT", n, tok))
                    act.activation(oT_hi[n][:, :, tok * P:(tok + 1) * P], src.rearrange("p (k c) -> p k c", k=4),
                                   ACT.Copy).then_inc(M.split_hi, 1)

            def gate(i):
                for tok in range(TT):
                    panel_wait(i, tok)
                    c = (i - M.first_gate) * PANEL
                    act.activation(gates[:, tok, c:c + PANEL], m_banks(i)[tok][:, :], ACT.Tanh,
                                   scale=0.5).then_inc(M.m_free[i % 2][tok], 1)

            def merged_hi(half):
                for tok in range(TT):
                    b, src = ready(("mT", half, tok))
                    act.activation(xT_hi[:, 4 * half:4 * half + 4, tok * P:(tok + 1) * P],
                                   src.rearrange("p (k c) -> p k c", k=4), ACT.Copy, scale=0.5).then_inc(M.split_hi, 1)

            return ready, panel_wait, splits, exps, p_transposed, o_split, gate, merged_hi

        def act_mix1(act, g, ph, l, prefetch):
            M = M1
            ready, panel_wait, splits, exps, p_transposed, o_split, gate, merged_hi = act_common(act, M, g, l)

            def to_q_raw(r):
                for tok in range(TT):
                    panel_wait(r, tok)
                    if r >= 2:
                        act.wait_ge(rope_done, l * (ROPES * TT) + ((r - 1) * TT + tok + 1))
                    act.activation(q_raw[:, tok, :], m_banks(r)[tok][:, :], ACT.Copy).then_inc(M.m_free[r % 2][tok], 1)

            act_xT(act, ph)
            splits(1)
            for tok in range(TT):
                panel_wait(0, tok)
                act.activation(misc[:, tok, :], A[tok][:, 0:MISC_W], ACT.Copy).then_inc(M.m_free[0][tok], 1)
            splits(2)
            to_q_raw(1)
            splits(3)
            for u in range(6):
                b, src = ready(("index", u))
                if u >= 2:
                    act.wait_ge(acc_step, l * ACC_STEPS + ACC_UNIT[u - 2])
                act.activation(relu[:, u % 2, :], src[:, :], ACT.Relu).then_inc(M.w_free[b], 1)
            to_q_raw(2)
            splits(4)
            to_q_raw(3)
            splits(5)
            to_q_raw(4)
            splits(6)
            to_q_raw(5)
            exps("B")
            splits(7)
            for tok in range(TT):
                panel_wait(6, tok)
                act.activation(va[:, tok, :], A[tok][:, :], ACT.Copy).then_inc(M.m_free[0][tok], 1)
            p_transposed("B")
            splits(8)
            gate(7)
            o_split("B")
            exps("C")
            splits(9)
            gate(8)
            p_transposed("C")
            splits(10)
            gate(9)
            o_split("C")
            exps("A")
            splits(11)
            gate(10)
            p_transposed("A")
            splits(12)
            gate(11)
            o_split("A")
            act_split(act, g, 26)
            act_split(act, g, 27)
            gate(12)
            for i in range(28, 34):
                act_split(act, g, i)
            merged_hi(0)
            act_split(act, g, 34)
            merged_hi(1)
            act_split(act, g, 35)
            if prefetch:
                act_split(act, g, 36)
                act_split(act, g, 37)

        def pool_sums(pool, M, l, ml, panels):
            s = 0
            for i, half in panels:
                for tok in range(TT):
                    pool.wait_ge(M.m_free[i % 2][tok], l * M.m_uses[i % 2] + (i // 2 + 1))
                    if s >= 2:
                        pool.wait_ge(merge_step, ml * 8 + (s - 1))
                    m = merged[:, tok, half * PANEL:(half + 1) * PANEL]
                    pool.tensor_tensor(m, m, addend[tok], ALU.add).then_inc(merge_step, 1)
                    s += 1

        def pool_mix1(pool, l):
            M = M1
            n = 0
            for r in range(ROPES):
                for tok in range(TT):
                    par, k = r % 2, r // 2 + 1
                    pool.wait_ge(M.m_free[par][tok], l * M.m_uses[par] + k)
                    if r:
                        b, _, kk = M.small(("rope", r - 1, tok))
                        pool.wait_ge(M.w_ready[b], l * M.uses[b] + (kk + 1))
                    nh = HEADS if r else 4
                    src = (q_raw[:, tok, :] if r else misc[:, tok, 0:256]).rearrange("p (h e) -> p h e", e=HD)
                    t = rope_tmp[:, 0:nh * HD].rearrange("p (h e) -> p h e", e=HD)
                    c = cos[:, tok, :].unsqueeze(1).broadcast_to([P, nh, HD])
                    s0 = sin[:, tok, 0:32].unsqueeze(1).broadcast_to([P, nh, 32])
                    s1 = sin[:, tok, 32:64].unsqueeze(1).broadcast_to([P, nh, 32])
                    if r:
                        outs = [rope_out[:, tok, :].rearrange("p (h e) -> p h e", e=HD)]
                    else:
                        dup = rope_out[:, tok, :].rearrange("p (h u e) -> p h u e", u=2, e=HD)
                        outs = [dup[:, :, 1, :], dup[:, :, 0, :]]
                    pool.tensor_tensor(outs[-1], src, c, ALU.mult).then_inc(rope_step, 1)
                    if r or tok:
                        pool.wait_ge(rope_done, l * (ROPES * TT) + (r * TT + tok))
                    pool.tensor_tensor(t[:, :, 0:32], src[:, :, 32:64], s0, ALU.mult).then_inc(rope_step, 1)
                    pool.tensor_tensor(t[:, :, 32:64], src[:, :, 0:32], s1, ALU.mult).then_inc(rope_step, 1)
                    n += 3
                    pool.wait_ge(rope_step, l * ROPE_STEPS + n)
                    for o in outs[:-1]:
                        pool.tensor_tensor(o, outs[-1], t, ALU.add).then_inc(rope_step, 1)
                        n += 1
                    if len(outs) > 1:
                        pool.wait_ge(rope_step, l * ROPE_STEPS + n)
                    pool.tensor_tensor(outs[-1], outs[-1], t, ALU.add).then_inc(rope_done, 1)
            assert n == ROPE_STEPS, n
            pool_sums(pool, M, l, l, [(i, half) for i, name, half in BRANCH_PANELS if name != ORDER[0]])

        ROPE_STEPS = ROPES * TT * 3 + TT

        ACC_UNIT = [4, 8, 10, 12, 14, 16]
        ACC_STEPS = 16 + 2 * (2 * 8) + 2 * 2

        def dve_common(dve, M, g, l, ml):
            def ready(job):
                b, src, k = M.small(job)
                dve.wait_ge(M.w_ready[b], l * M.uses[b] + (k + 1))
                return b, src

            def splits(i):
                for h in range(2):
                    dve_split(dve, g, 2 * i + h, MISC_W if i == 0 and M is M1 else CH)

            def panel_wait(i, tok):
                if (i, tok) in M.ready_no:
                    dve.wait_ge(M.panel_ready, l * M.panels + M.ready_no[i, tok])
                else:
                    dve.wait_ge(chunk_used, chunk_no(g, M.last_chunk(i)) + RING)

            def normalise(n):
                i = M.order.index(n)
                for tile in range(TT):
                    dve.wait_ge(M.exp_done, l * M.attn + (i * 6 + (2 if tile == 0 else 6)))
                    r = rsum[:, tile, i, :]
                    if n == "B":
                        dve.wait_ge(sink_exp, l * 2 + (tile + 1))
                        dve.tensor_tensor(r, r, sinkm[:, tile, :], ALU.add).then_inc(M.rinv_step, 1)
                        dve.wait_ge(M.rinv_step, l * M.recips + (2 * tile + 1))
                    dve.reciprocal(rinv[:, tile, :], r).then_inc(M.rinv_step, 1)
                    k = 2 * tile + 2 if n == "B" else 2 * ("B" in M.order) + 2 * i + tile + 1
                    dve.wait_ge(M.rinv_step, l * M.recips + k)
                    b, src = ready(("pv", n, tile))
                    dve.tensor_tensor(o_tile[tile].rearrange("p (h e) -> p h e", e=HD),
                                      src.rearrange("p (h e) -> p h e", e=HD),
                                      rinv[:, tile, :].unsqueeze(2).broadcast_to([P, HEADS, HD]),
                                      ALU.mult).then_inc(M.w_free[b], 1)

            def o_split(n):
                for tok in range(TT):
                    b, src, _ = M.small(("oT", n, tok))
                    dve.wait_ge(M.split_hi, l * M.splits + (M.order.index(n) * 2 + tok + 1))
                    o = (slice(None), slice(None), slice(tok * P, (tok + 1) * P))
                    dve.tensor_tensor(oT_lo[n][o], src.rearrange("p (k c) -> p k c", k=4),
                                      oT_hi[n][o].bitcast(F32), ALU.subtract).then_inc(M.w_free[b], 1)

            def merge(i, gate, half, sums):
                for tok in range(TT):
                    panel_wait(i, tok)
                    c = gate * DM + half * PANEL
                    m = merged[:, tok, half * PANEL:(half + 1) * PANEL]
                    if sums is not None and sums + tok >= 2:
                        dve.wait_ge(merge_step, ml * 8 + (sums + tok - 1))
                    dve.scalar_tensor_tensor(m if sums is None else addend[tok], gates[:, tok, c:c + PANEL], 1.0,
                                             m_banks(i)[tok][:, :], ALU.add, ALU.mult).then_inc(M.m_free[i % 2][tok], 1)

            def merged_lo(half):
                for tok in range(TT):
                    b, src, _ = M.small(("mT", half, tok))
                    dve.wait_ge(M.split_hi, l * M.splits + (M.splits - 4 + half * 2 + tok + 1))
                    o = (slice(None), slice(4 * half, 4 * half + 4), slice(tok * P, (tok + 1) * P))
                    dve.scalar_tensor_tensor(xT_lo[o], src.rearrange("p (k c) -> p k c", k=4), 0.5,
                                             xT_hi[o].bitcast(F32), ALU.mult, ALU.subtract).then_inc(M.w_free[b], 1)

            return ready, splits, panel_wait, normalise, o_split, merge, merged_lo

        def dve_mix1(dve, g, ph, l):
            M = M1
            ready, splits, panel_wait, normalise, o_split, merge, merged_lo = dve_common(dve, M, g, l, l)

            def rope_copy(r):
                dst = [kx_T, qi_T, qc_T, qb_T, qa_T, ka_T][r]
                for tok in range(TT):
                    b, src = ready(("rope", r, tok))
                    dve.tensor_copy(dst[:, :, tok * P:(tok + 1) * P],
                                    src.rearrange("p (k c) -> p k c", k=4)).then_inc(M.w_free[b], 1)

            step = [0]

            def stepped(ins):
                step[0] += 1
                ins.then_inc(acc_step, 1)

            def stepped_wait():
                dve.wait_ge(acc_step, l * ACC_STEPS + step[0])

            def index_sums():
                for u, (tile, heads) in enumerate(UNITS):
                    b, _, k = M.small(("index", u))
                    dve.wait_ge(M.w_free[b], l * M.uses[b] + (k + 1))
                    keys = P * (tile + 1)
                    acc = bias_c[:, tile, 0:keys]
                    for at, h in enumerate(heads):
                        if h:
                            stepped_wait()
                        base = acc if h else causal[:, SEQ - keys:SEQ]
                        stepped(dve.scalar_tensor_tensor(acc, relu[:, u % 2, at * keys:(at + 1) * keys],
                                                         misc[:, tile, 448 + h:449 + h], base, ALU.mult, ALU.add))

            def top_k(between):
                for tile in range(TT):
                    keys = P * (tile + 1)
                    s = bias_c[:, tile, 0:keys]
                    for rnd in range(TOPK // 8):
                        if (tile, rnd) in between:
                            dve_split(dve, g, between[tile, rnd])
                        stepped_wait()
                        steady(dve)
                        stepped(dve.max(max8[:, tile, :], s))
                        stepped_wait()
                        steady(dve)
                        stepped(dve.match_replace(s, max8[:, tile, :], s, TAKEN))
                for tile in range(TT):
                    keys = P * (tile + 1)
                    s = bias_c[:, tile, 0:keys]
                    stepped_wait()
                    stepped(dve.tensor_scalar(s, s, TAKEN / 2, MASKED, ALU.is_gt, ALU.mult))
                    stepped_wait()
                    stepped(dve.tensor_tensor(s, s, causal[:, SEQ - keys:SEQ], ALU.add))

            def logits(n):
                i = M.order.index(n)
                if n == "C":
                    stepped_wait()
                for u, (tile, heads) in enumerate(UNITS):
                    b, src = ready(("score", n, u))
                    keys = P * (tile + 1)
                    m = {"A": mask_a[:, SEQ - keys:SEQ], "B": mask_b[:, SEQ - keys:SEQ],
                         "C": bias_c[:, tile, 0:keys]}[n]
                    s = S_sb[:, u, :].rearrange("p (h k) -> p h k", k=keys)
                    dve.scalar_tensor_tensor(s, src.rearrange("p (h k) -> p h k", k=keys), SCALE,
                                             m.unsqueeze(1).broadcast_to([P, len(heads), keys]),
                                             ALU.mult, ALU.add).then_inc(M.w_free[b], 1)
                    dve.wait_ge(M.w_free[b], l * M.uses[b] + (M.small(("score", n, u))[2] + 1))
                    nm = of_unit(nmax[:, tile, i, :], heads)
                    red = dve.tensor_reduce(nm, s, AX, ALU.max, negate=True)
                    if n == "B":
                        red.then_inc(smax_step, 1)
                        dve.wait_ge(smax_step, l * 8 + (u + 1 + (u > 1)))
                        if u == 0:
                            dve.wait_ge(sink_loaded, l * 16 + 16)
                        dve.scalar_tensor_tensor(nm, of_unit(sink, heads), -1.0, nm, ALU.mult,
                                                 ALU.min).then_inc(M.smax, 1)
                        if u in (1, 5):
                            dve.wait_ge(M.smax, l * M.attn + (u + 1))
                            dve.tensor_tensor(sinkm[:, tile, :], nmax[:, tile, i, :], sink[:],
                                              ALU.add).then_inc(smax_step, 1)
                    else:
                        red.then_inc(M.smax, 1)

            splits(1)
            splits(2)
            rope_copy(0)
            splits(3)
            rope_copy(1)
            index_sums()
            splits(4)
            rope_copy(2)
            top_k({(1, 0): 10, (1, 4): 11})
            rope_copy(3)
            splits(6)
            logits("B")
            rope_copy(4)
            splits(7)
            rope_copy(5)
            normalise("B")
            splits(8)
            o_split("B")
            logits("C")
            splits(9)
            normalise("C")
            splits(10)
            o_split("C")
            logits("A")
            splits(11)
            normalise("A")
            splits(12)
            o_split("A")
            for i in range(2):
                dve_split(dve, g, 26 + i)
            for i, n, half in BRANCH_PANELS:
                dve_split(dve, g, 28 + i - 13)
                merge(i, "ABC".index(n), half, None if n == ORDER[0] else 4 * half + 2 * (ORDER.index(n) - 1))
                if i == 16:
                    merged_lo(0)
            dve_split(dve, g, 34)
            merged_lo(1)
            dve_split(dve, g, 35)

        PH2 = 3 * LAYERS

        def act_head(act, ph, tok):
            act.wait_ge(x_ready, ph * 2 + (tok + 1))
            act.activation(hn[:, tok, :], x[:, tok, :], ACT.Square, accum_out=sum_sq[:, tok, :]).then_inc(row_sq, 1)

        def dve_head(dve, ph, tok, gain):
            n = (ph - PH2) * 2 + (tok + 1)
            dve.wait_ge(row_sq, n)
            dve.tensor_scalar(var_eps[:, tok, 0:1], sum_sq[:, tok, :], 1.0 / DM, RMS_EPS, ALU.mult,
                              ALU.add).then_inc(var_ready, 1)
            dve.wait_ge(rstd_ready, ph * 2 + (tok + 1))
            if tok == 0:
                dve.wait_ge(gain_loaded, (ph - PH2) * 16 + 16)
            dve.scalar_tensor_tensor(hn[:, tok, :], x[:, tok, :], rstd[:, tok, 0:1], gain,
                                     ALU.mult, ALU.mult).then_inc(hn_ready, 1)

        def dve_tail(dve, g, ph, last_chunk, banks, tok):
            if tok == 0:
                dve.wait_ge(acc_ready, ph + 1)
            else:
                dve.wait_ge(chunk_used, chunk_no(g, last_chunk) + RING)
            for n in range(2):
                xs = x[:, tok, n * PANEL:(n + 1) * PANEL]
                add = dve.tensor_tensor(xs, xs, banks[tok][n][:, :], ALU.add)
            add.then_inc(x_ready, 1)

        def sp_mix2(sp, g, ph, l):
            w = d["w_in_2"][l].rearrange("(h t p) n -> h p t n", p=P, t=4)

            def panels(first, columns):
                for i, c in enumerate(columns):
                    for h in range(2):
                        j = 2 * (first + i) + h
                        sp_chunk(sp, g, j, halves(j, w[h, :, :, c:c + PANEL]))

            panels(0, (K2, Q2))
            sp.wait_ge(x_ready, ph * 2 + 2)
            steady(sp)
            forget_columns = d["w_in_2"][l].rearrange("(t p) n -> p t n", p=P)[:, :, F2:F2 + HEADS]
            sp.dma_start(wf_raw[:], forget_columns).then_inc(small_loaded, 16)
            sp.dma_start(forget[:, 0, 0, :], d["forget_b_2"][l].partition_broadcast(P)).then_inc(small_loaded, 16)
            sp.dma_start(qk_gain[:, 0, :], d["k_norm_g_2"][l].partition_broadcast(P)).then_inc(small_loaded, 16)
            sp.dma_start(qk_gain[:, 1, :], d["q_norm_g_2"][l].partition_broadcast(P)).then_inc(small_loaded, 16)
            with nc.allow_non_contiguous_dma(reason="a channel's taps, one channel per partition"):
                for c in range(2):
                    taps = d["conv_w_2"][l].rearrange("j (c p) -> c p j", p=P)[c]
                    sp.dma_start(conv_taps[:, c, :], taps).then_inc(small_loaded, 16)
            sp.dma_start(inv_count[:], d["c_pool"]).then_inc(small_loaded, 16)
            panels(2, (V2, CX2, CC2, *(GATES2 + PANEL * q for q in range(6))))
            groups = d["pool_w_2"][l].rearrange("(b h) c n -> (h c) b n", h=2)
            v = w_raw[:, POOL_CHUNK % RING, 0:512].rearrange("p (b n) -> p b n", b=2)
            sp_chunk(sp, g, POOL_CHUNK, [(v[:, b, :], groups[:, b, :]) for b in range(2)])
            v = w_raw[:, CONV_CHUNK % RING, :].rearrange("p (t n) -> p t n", t=2)
            taps_out = d["w_conv_out_2"][l].rearrange("(t p) n -> p t n", p=P)
            sp_chunk(sp, g, CONV_CHUNK, [(v[:, t, :], taps_out[:, t, :]) for t in range(2)])
            b, _, k = M2.small(("qk", 1, 1))
            sp.wait_ge(M2.w_ready[b], l * M2.uses[b] + (k + 1))
            steady(sp)
            sp.dma_start(gb[:, 1, :], d["pool_scale_2"][l].partition_broadcast(P)).then_inc(scale_loaded, 16)
            sp.dma_start(gb[:, 0, :], d["norm_ffn_g_2"][l].partition_broadcast(P)).then_inc(gain_loaded, 16)
            src = d["w_attn_out_2"][l].rearrange("(t p) n -> p t n", p=P)
            for i in range(2):
                sp_chunk(sp, g, ATTN_CHUNK + i, halves(ATTN_CHUNK + i, src[:, :, i * PANEL:(i + 1) * PANEL]))
            wo = d["w_o_2"][l].rearrange("(h t p) n -> h p t n", p=P, t=4)
            for i in range(4):
                h, n = divmod(i, 2)
                sp_chunk(sp, g, WO_CHUNK + i, halves(WO_CHUNK + i, wo[h, :, :, n * PANEL:(n + 1) * PANEL]))

        def pe_mix2(pe, g, ph, l):
            M = M2
            ml = l + LAYERS
            (take, freed, panel, values, o_transposes, branch, merged_transposes, out_product,
             out_product_end) = pe_common(pe, M, g, l, ml)

            def qk_transposes(r):
                for tok in range(TT):
                    b, dst = take(("qk", r, tok))
                    pe.wait_ge(qk_done, l * 4 + (2 * r + tok + 1))
                    for q in range(4):
                        mm = pe.transpose(dst[:, q * P:(q + 1) * P], rope_out[:, tok, q * P:(q + 1) * P], ident)
                    mm.then_inc(M.w_ready[b], 1)

            def forget_product():
                b, dst = take(("f",))
                pe.wait_ge(wf_lo_done, l + 1)
                for tok in range(TT):
                    for kt in range(KT):
                        c, tokens = 2 * tok * HEADS, slice(tok * P, (tok + 1) * P)
                        pe.matmul(dst[:, c:c + 2 * HEADS], xT_hi[:, kt, tokens], wf[:, kt, :], start=kt == 0,
                                  stop=False, skip_group_check=True)
                        mm = pe.matmul(dst[:, c:c + HEADS], xT_lo[:, kt, tokens], wf[:, kt, 0:HEADS], start=False,
                                       stop=kt == KT - 1, skip_group_check=True)
                mm.then_inc(M.w_ready[b], 1)

            def running_sums():
                b, dst = take(("c",))
                pe.wait_ge(f_step, l * F_STEPS + F_STEPS)
                pe.matmul(dst[:, 0:HEADS], up_to[:, 0:P], logf_wide[:, 0, 0:HEADS], start=True, stop=True)
                pe.matmul(dst[:, HEADS:2 * HEADS], up_to[:, P:SEQ], logf_wide[:, 0, 0:HEADS], start=True, stop=False)
                pe.matmul(dst[:, HEADS:2 * HEADS], up_to[:, 0:P], logf_wide[:, 1, 0:HEADS], start=False,
                          stop=True).then_inc(M.w_ready[b], 1)
                b, dst = take(("cT",))
                pe.matmul(dst[:, 0:SEQ], logf_wide[:, 0, :], up_to[:, 0:SEQ], start=True, stop=False, skip_group_check=True)
                pe.matmul(dst[:, P:SEQ], logf_wide[:, 1, :], up_to[:, 0:P], start=False, stop=True,
                          skip_group_check=True).then_inc(M.w_ready[b], 1)

            def channel_panel(i):
                for h in range(2):
                    pe.wait_ge(lo_done, chunk_no(g, 2 * i + h) + RING)
                    for q in range(4):
                        if h == 0 and q % 2 == 0:
                            pe.wait_ge(M.m_free[i % 2][q // 2], l * M.m_uses[i % 2] + i // 2)
                        dst = m_banks(i)[q // 2][:, (q % 2) * SEQ:(q % 2 + 1) * SEQ]
                        for t in range(4):
                            c = t * PANEL + q * P
                            s = (2 * i + h) % RING
                            mm = three(pe, dst, w_hi[:, s, c:c + P], w_lo[:, s, c:c + P], xT_hi[:, 4 * h + t, :],
                                       xT_lo[:, 4 * h + t, :], h == 0 and q % 2 == 0 and t == 0, h == 1 and t == 3)
                        if h == 1 and q == 1:
                            mm.then_inc(M.panel_ready, 1)
                    mm.then_inc(chunk_used, 1)

            def pool_product():
                pe.wait_ge(lo_done, chunk_no(g, POOL_CHUNK) + RING)
                pe.wait_ge(pool_lo_done, l + 1)
                for i in (11, 12):
                    half = slice(64 * (i - 11), 64 * (i - 11) + 64)
                    for tok in range(TT):
                        pe.wait_ge(M.m_free[i % 2][tok], l * M.m_uses[i % 2] + i // 2)
                        for c in range(2):
                            tokens = slice(tok * P, (tok + 1) * P)
                            s = POOL_CHUNK % RING
                            mm = three(pe, m_banks(i)[tok][:, c * 256:(c + 1) * 256], pool_hi[half, c, tokens],
                                       pool_lo[half, c, tokens], w_hi[half, s, c * 256:(c + 1) * 256],
                                       w_lo[half, s, c * 256:(c + 1) * 256], True, True)
                        mm.then_inc(*((M.panel_ready, 1) if i == 11 or tok == 0 else (chunk_used, 1)))

            def conv_product():
                pe.wait_ge(lo_done, chunk_no(g, CONV_CHUNK) + RING)
                pe.wait_ge(conv_lo_done, l + 1)
                for i in (13, 14):
                    for tok in range(TT):
                        pe.wait_ge(M.m_free[i % 2][tok], l * M.m_uses[i % 2] + i // 2)
                        mm = pe_part(pe, CONV_CHUNK, m_banks(i)[tok], tok, 0, 2, True, True, conv_hi, conv_lo,
                                     col=(i - 13) * PANEL, pitch=DM)
                        mm.then_inc(*((M.panel_ready, 1) if i == 13 or tok == 0 else (chunk_used, 1)))

            def scores():
                for u, (tile, heads) in enumerate(UNITS):
                    b, dst = take(("score", "D", u))
                    keys = P * (tile + 1)
                    for at, h in enumerate(heads):
                        half = slice(64 * (h % 2), 64 * (h % 2) + 64)
                        row = 64 * (h % 2) + h
                        pe.matmul(dst[:, at * keys:(at + 1) * keys], q2_T[half, h // 2, tile * P:(tile + 1) * P],
                                  k2_T[half, h // 2, 0:keys], start=True, stop=False)
                        mm = pe.matmul(dst[:, at * keys:(at + 1) * keys],
                                       ident[half, row:row + 1].broadcast_to([64, P]), neg_cT[half, 0:keys],
                                       start=False, stop=True)
                    mm.then_inc(M.w_ready[b], 1)

            pe_first_panel(pe, g, ph, A, M.panel_ready, (hn, hn_ready, (ph - PH2) * 2))
            panel(1)
            qk_transposes(0)
            forget_product()
            panel(2)
            qk_transposes(1)
            running_sums()
            channel_panel(3)
            freed(("cT",))
            scores()
            channel_panel(4)
            panel(5)
            for tok in range(TT):
                pe.wait_ge(M.m_free[0][tok], l * M.m_uses[0] + 2)
            values("D")
            panel(6)
            o_transposes("D")
            for i in range(7, 11):
                panel(i)
            pool_product()
            conv_product()
            branch(15, "D", 0)
            branch(16, "D", 1)
            merged_transposes(0, 4)
            freed(("mT", 0, 1))
            out_product(0, WO_CHUNK)
            merged_transposes(1, 6)
            out_product(1, WO_CHUNK + 1)
            freed(("mT", 1, 1))
            out_product_end(WO_CHUNK + 2)

        def act_mix2(act, g, ph, l):
            M = M2
            ready, panel_wait, splits, exps, p_transposed, o_split, gate, merged_hi = act_common(act, M, g, l)

            def staged(r):
                for tok in range(TT):
                    panel_wait(r, tok)
                    if r:
                        act.wait_ge(qk_done, l * 4 + (tok + 1))
                    act.activation(q_raw[:, tok, :], m_banks(r)[tok][:, :], ACT.Copy)
                    act.activation(S_sb[:, 2 * r + tok, :], m_banks(r)[tok][:, :], ACT.Square).then_inc(M.m_free[r % 2][tok], 1)

            act_head(act, ph, 0)
            act_head(act, ph, 1)
            act_xT(act, ph)
            act.wait_ge(small_loaded, l * (16 * (SMALL_LOADS)) + 16 * (SMALL_LOADS))
            act.activation(wf[:, :, 0:HEADS], wf_raw[:], ACT.Copy).then_inc(wf_hi_done, 1)
            splits(1)
            staged(0)
            splits(2)
            staged(1)
            act.wait_ge(f_step, l * F_STEPS + 3)
            act.activation(forget[:, 2, :, :], forget[:, 2, :, :], ACT.Exp).then_inc(f_exp, 1)
            act.wait_ge(f_step, l * F_STEPS + 4)
            act.activation(forget[:, 2, :, :], forget[:, 2, :, :], ACT.Ln).then_inc(f_exp, 1)
            splits(3)
            for tok in range(TT):
                panel_wait(2, tok)
                act.activation(va[:, tok, :], A[tok][:, :], ACT.Copy).then_inc(M.m_free[0][tok], 1)
            splits(4)
            for bank_no, dst in enumerate((cx_sb, cb_sb)):
                panel_wait(3, bank_no)
                act.activation(dst, m_banks(3)[bank_no].rearrange("p (c s) -> p c s", c=2), ACT.Copy).then_inc(M.m_free[1][bank_no], 1)
            splits(5)
            exps("D")
            panel_wait(4, 1)
            act.wait_ge(pads_set, l * PADS + PADS)
            act.activation(u_pad[:, :, LAG:], A[1].rearrange("p (c s) -> p c s", c=2), ACT.Copy).then_inc(M.m_free[0][1], 1)
            splits(6)
            act.wait_ge(conv_step, l * CONV_STEPS + CONV_STEPS)
            act.activation(conv_hi[:], tmp[:].rearrange("p (c s) -> p c s", c=2), ACT.Copy).then_inc(conv_hi_done, 1)
            gate(5)
            p_transposed("D")
            splits(7)
            gate(6)
            o_split("D")
            act.wait_ge(pool_made, l + 1)
            act.activation(pool_hi[:], window_d[:], ACT.Copy).then_inc(pool_hi_done, 1)
            splits(8)
            gate(7)
            splits(9)
            gate(8)
            splits(10)
            gate(9)
            act_split(act, g, POOL_CHUNK, 512)
            act_split(act, g, CONV_CHUNK)
            gate(10)
            for i in range(ATTN_CHUNK, WO_CHUNK + 2):
                act_split(act, g, i)
            merged_hi(0)
            act_split(act, g, WO_CHUNK + 2)
            merged_hi(1)
            act_split(act, g, WO_CHUNK + 3)

        PADS = 3
        POOL_STEPS = 7

        def pool_mix2(pool, ph, l):
            M = M2
            pool.wait_ge(xT_lo_done, ph * 4 + 4)
            steady(pool)
            pool.memset(u_pad[:, :, 0:LAG], 0.0).then_inc(pads_set, 1)
            pool.memset(z_pad[:, :, 0:2], 0.0).then_inc(pads_set, 1)
            pool.memset(logf_wide[:], 0.0).then_inc(pads_set, 1)
            for r in range(2):
                for tok in range(TT):
                    n = l * 4 + 2 * r + (tok + 1)
                    pool.wait_ge(qk_var_ready, n)
                    pool.tensor_tensor(qk_rstd[:, r, tok, :], qk_var[:, r, tok, :], minus_half[:, 0:HEADS],
                                       ALU.pow).then_inc(qk_rstd_ready, 1)
                    pool.wait_ge(qk_rstd_ready, n)
                    if r:
                        b, _, k = M.small(("qk", 0, tok))
                        pool.wait_ge(M.w_ready[b], l * M.uses[b] + (k + 1))
                    o = rope_out[:, tok, :].rearrange("p (h e) -> p h e", e=HD)
                    pool.tensor_tensor(o, q_raw[:, tok, :].rearrange("p (h e) -> p h e", e=HD),
                                       qk_rstd[:, r, tok, :].unsqueeze(2).broadcast_to([P, HEADS, HD]),
                                       ALU.mult).then_inc(qk_half, 1)
                    pool.wait_ge(qk_half, n)
                    if not r and not tok:
                        pool.wait_ge(small_loaded, l * (16 * (SMALL_LOADS)) + 16 * (SMALL_LOADS))
                    pool.tensor_tensor(o, o, qk_gain[:, r, :].unsqueeze(1).broadcast_to([P, HEADS, HD]),
                                       ALU.mult).then_inc(qk_done, 1)
            steps = [0]

            def stepped(ins):
                steps[0] += 1
                ins.then_inc(pool_step, 1)
                pool.wait_ge(pool_step, l * POOL_STEPS + steps[0])

            pool.wait_ge(M.m_free[0][1], l * M.m_uses[0] + 3)
            end = LAG + SEQ
            stepped(pool.tensor_tensor(run_a[:, :, 1:], u_pad[:, :, 1:], u_pad[:, :, 0:end - 1], ALU.add))
            stepped(pool.tensor_tensor(run_b[:, :, 3:], run_a[:, :, 3:], run_a[:, :, 1:end - 2], ALU.add))
            low, high = slice(0, 64), slice(64, 128)
            stepped(pool.tensor_tensor(window_d[low, 0, :], run_a[low, 0, LAG:], inv_count[low, 0, :], ALU.mult))
            stepped(pool.tensor_tensor(window_d[high, 0, :], run_b[high, 0, LAG:], inv_count[high, 0, :], ALU.mult))
            stepped(pool.tensor_tensor(run_a[:, 1, 7:], run_b[:, 1, 7:], run_b[:, 1, 3:end - 4], ALU.add))
            stepped(pool.tensor_tensor(window_d[low, 1, :], run_a[low, 1, LAG:], inv_count[low, 1, :], ALU.mult))
            stepped(pool.tensor_tensor(run_b[high, 1, 15:], run_a[high, 1, 15:], run_a[high, 1, 7:end - 8], ALU.add))
            pool.tensor_tensor(window_d[high, 1, :], run_b[high, 1, LAG:], inv_count[high, 1, :], ALU.mult).then_inc(pool_half, 1)
            pool.wait_ge(pool_half, l + 1)
            pool.tensor_tensor(window_d[:], window_d[:], u_pad[:, :, LAG:], ALU.subtract).then_inc(pool_made, 1)
            assert steps[0] == POOL_STEPS, steps
            pool.wait_ge(scale_loaded, l * 16 + 16)
            for tok in range(TT):
                for i in (11, 12):
                    pool.wait_ge(M.m_free[i % 2][tok], l * M.m_uses[i % 2] + (i // 2 + 1))
                pool.tensor_tensor(merged[:, tok, :], merged[:, tok, :], gb[:, 1, :], ALU.mult).then_inc(scaled, 1)
            pool.wait_ge(scaled, l * 2 + 2)
            steady(pool)
            pool_sums(pool, M, l, l + LAYERS, [(13, 0), (14, 1), (15, 0), (16, 1)])

        F_STEPS = 6
        CONV_STEPS = 8

        def dve_mix2(dve, g, ph, l):
            M = M2
            ml = l + LAYERS
            ready, splits, panel_wait, normalise, o_split, merge, merged_lo = dve_common(dve, M, g, l, ml)

            def mean_squares(r):
                for tok in range(TT):
                    dve.wait_ge(M.m_free[r % 2][tok], l * M.m_uses[r % 2] + 1)
                    v = qk_var[:, r, tok, :]
                    dve.tensor_reduce(v, S_sb[:, 2 * r + tok, :].rearrange("p (h e) -> p h e", e=HD), AX,
                                      ALU.add).then_inc(qk_step, 1)
                    dve.wait_ge(qk_step, l * 4 + (2 * r + tok + 1))
                    dve.tensor_scalar(v, v, 1.0 / HD, RMS_EPS, ALU.mult, ALU.add).then_inc(qk_var_ready, 1)

            def transposed(r):
                for tok in range(TT):
                    b, src = ready(("qk", r, tok))
                    dst = (k2_T, q2_T)[r][:, :, tok * P:(tok + 1) * P]
                    src = src.rearrange("p (k c) -> p k c", k=4)
                    if r:
                        dve.tensor_scalar(dst, src, SCALE, None, ALU.mult).then_inc(M.w_free[b], 1)
                    else:
                        dve.tensor_copy(dst, src).then_inc(M.w_free[b], 1)

            def log_forget():
                bias, z, e = forget[:, 0, 0, :], forget[:, 1, :, :], forget[:, 2, :, :]
                b, src = ready(("f",))
                parts = src[:, 0:4 * HEADS].rearrange("p (t u h) -> p t u h", t=TT, u=2)
                dve.tensor_tensor(z, parts[:, :, 0, :], bias.unsqueeze(1).broadcast_to([P, TT, HEADS]),
                                  ALU.add).then_inc(f_step, 1)
                dve.wait_ge(f_step, l * F_STEPS + 1)
                dve.tensor_tensor(z, z, parts[:, :, 1, :], ALU.add).then_inc(M.w_free[b], 1)
                dve.wait_ge(M.w_free[b], l * M.uses[b] + (M.small(("f",))[2] + 1))
                dve.tensor_scalar(e, z, -1.0, None, ALU.mult).then_inc(f_step, 1)
                dve.wait_ge(f_step, l * F_STEPS + 2)
                dve.tensor_tensor(e, e, z, ALU.min).then_inc(f_step, 1)
                dve.wait_ge(f_exp, l * 2 + 1)
                dve.tensor_scalar(e, e, 1.0, None, ALU.add).then_inc(f_step, 1)
                dve.wait_ge(f_exp, l * 2 + 2)
                dve.wait_ge(pads_set, l * PADS + PADS)
                for c in (0, 64):
                    dve.scalar_tensor_tensor(logf_wide[:, :, c:c + HEADS], z, 0.0, e, ALU.min,
                                             ALU.subtract).then_inc(f_step, 1)

            def sums_read():
                b, src = ready(("c",))
                dve.tensor_copy(forget[:, 3, :, :], src[:, 0:2 * HEADS].rearrange("p (t h) -> p t h", t=TT)).then_inc(M.w_free[b], 1)
                b, src = ready(("cT",))
                dve.tensor_scalar(neg_cT, src[:, 0:SEQ], -1.0, None, ALU.mult).then_inc(M.w_free[b], 1)

            def logits():
                for u, (tile, heads) in enumerate(UNITS):
                    b, src = ready(("score", "D", u))
                    keys = P * (tile + 1)
                    for at, h in enumerate(heads):
                        ins = dve.scalar_tensor_tensor(S_sb[:, u, at * keys:(at + 1) * keys], src[:, at * keys:(at + 1) * keys],
                                                       forget[:, 3, tile, h:h + 1], causal[:, SEQ - keys:SEQ],
                                                       ALU.add, ALU.add)
                    ins.then_inc(M.w_free[b], 1)
                    dve.wait_ge(M.w_free[b], l * M.uses[b] + (M.small(("score", "D", u))[2] + 1))
                    dve.tensor_reduce(of_unit(nmax[:, tile, 0, :], heads), S_sb[:, u, :].rearrange("p (h k) -> p h k", k=keys),
                                      AX, ALU.max, negate=True).then_inc(M.smax, 1)

            def convolve():
                for bank_no in range(2):
                    dve.wait_ge(M.m_free[1][bank_no], l * M.m_uses[1] + 2)
                dve.wait_ge(pads_set, l * PADS + PADS)
                panel_wait(4, 0)
                dve.tensor_tensor(z_pad[:, :, 2:], A[0].rearrange("p (c s) -> p c s", c=2), cx_sb,
                                  ALU.mult).then_inc(M.m_free[0][0], 1)
                dve.wait_ge(M.m_free[0][0], l * M.m_uses[0] + 3)
                y = [tmp[:, c * SEQ:(c + 1) * SEQ] for c in range(2)]
                n = 0
                for j in range(4):
                    for c in range(2):
                        if n >= 2:
                            dve.wait_ge(conv_step, l * CONV_STEPS + (n - 1))
                        if j == 0:
                            ins = dve.tensor_scalar(y[c], z_pad[:, c, 0:SEQ], conv_taps[:, c, 0:1], None, ALU.mult)
                        elif j < 3:
                            ins = dve.scalar_tensor_tensor(y[c], z_pad[:, c, j:j + SEQ], conv_taps[:, c, j:j + 1], y[c],
                                                           ALU.mult, ALU.add)
                        else:
                            ins = dve.tensor_tensor(y[c], y[c], cb_sb[:, c, :], ALU.mult)
                        ins.then_inc(conv_step, 1)
                        n += 1

            def pool_merge(i):
                def groups(ap):
                    return ap.rearrange("p (a b c) -> p a b c", a=2, b=2)[:, :, i - 11, :]

                for tok in range(TT):
                    panel_wait(i, tok)
                    dve.wait_ge(M.m_free[0][tok], l * M.m_uses[0] + 6)
                    dve.scalar_tensor_tensor(groups(merged[:, tok, :]), groups(gates[:, tok, 2 * DM:3 * DM]), 1.0,
                                             m_banks(i)[tok].rearrange("p (a c) -> p a c", a=2),
                                             ALU.add, ALU.mult).then_inc(M.m_free[i % 2][tok], 1)

            dve.wait_ge(wf_hi_done, l + 1)
            dve.tensor_tensor(wf[:, :, HEADS:], wf_raw[:], wf[:, :, 0:HEADS].bitcast(F32), ALU.subtract).then_inc(wf_lo_done, 1)
            splits(1)
            mean_squares(0)
            splits(2)
            transposed(0)
            mean_squares(1)
            log_forget()
            splits(3)
            transposed(1)
            sums_read()
            splits(4)
            logits()
            splits(5)
            convolve()
            splits(6)
            dve.wait_ge(conv_hi_done, l + 1)
            dve.tensor_tensor(conv_lo[:], tmp[:].rearrange("p (c s) -> p c s", c=2), conv_hi[:].bitcast(F32),
                              ALU.subtract).then_inc(conv_lo_done, 1)
            normalise("D")
            splits(7)
            o_split("D")
            dve.wait_ge(pool_hi_done, l + 1)
            dve.tensor_tensor(pool_lo[:], window_d[:], pool_hi[:].bitcast(F32), ALU.subtract).then_inc(pool_lo_done, 1)
            splits(8)
            splits(9)
            splits(10)
            dve_split(dve, g, POOL_CHUNK, 512)
            dve_split(dve, g, CONV_CHUNK)
            pool_merge(11)
            pool_merge(12)
            dve_split(dve, g, ATTN_CHUNK)
            merge(13, 1, 0, 0)
            dve_split(dve, g, ATTN_CHUNK + 1)
            merge(14, 1, 1, 2)
            dve_split(dve, g, WO_CHUNK)
            merge(15, 0, 0, 4)
            merge(16, 0, 1, 6)
            merged_lo(0)
            dve_split(dve, g, WO_CHUNK + 1)
            dve_split(dve, g, WO_CHUNK + 2)
            merged_lo(1)
            dve_split(dve, g, WO_CHUNK + 3)

        SETUP = {}

        def dve_setup(dve):
            n = [0]

            def link(ins):
                n[0] += 1
                ins.then_inc(setup, 1)
                dve.wait_ge(setup, n[0])

            dve.sem_inc(lo_done, RING)
            dve.wait_ge(pos_loaded, 16)
            dve.wait_ge(consts_loaded, 16)
            link(dve.tensor_copy(pos_f[:], pos_i[:]))
            for tok in range(TT):
                link(dve.tensor_scalar(ang[:, tok, :], inv_freq, pos_f[:, tok:tok + 1], None, ALU.mult))
            for scale in (2.0 ** 14, 1.0):
                link(dve.tensor_scalar(turns[:], ang[:], float(1 / (2 * np.pi * scale)), None, ALU.mult))
                link(dve.tensor_scalar(turns[:], turns[:], MAGIC, None, ALU.add))
                link(dve.tensor_scalar(turns[:], turns[:], -MAGIC, None, ALU.add))
                for part in two_pi_parts():
                    link(dve.scalar_tensor_tensor(ang[:], turns[:], -part * scale, ang[:], ALU.mult, ALU.add))
            link(dve.tensor_scalar(ang[:], ang[:], 3.1415925, -3.1415925, ALU.min, ALU.max))
            SETUP["angle"] = n[0]
            link(dve.tensor_scalar(turns[:], ang[:], -1.0, None, ALU.mult))
            link(dve.tensor_tensor(turns[:], turns[:], ang[:], ALU.min))
            link(dve.tensor_scalar(turns[:], turns[:], float(np.pi / 2), None, ALU.add))
            SETUP["co_angle"] = n[0]
            dve.wait_ge(setup_act, 2)
            dve.tensor_scalar(sin[:, :, 0:32], sin[:, :, 0:32], -1.0, None, ALU.mult).then_inc(setup, 1)
            SETUP["tables"] = n[0] + 1
            dve.wait_ge(masks_loaded, 16)

        ANGLE = 3 + 2 * (3 + 5) + 1
        CO_ANGLE = ANGLE + 3
        TABLES = CO_ANGLE + 1

        block = ctx.enter_context(nc.Block())

        @block.sync
        def _(sp):
            with nc.allow_non_contiguous_dma(reason="256 positions, one per partition"):
                sp.dma_start(pos_i[:], d["positions"].rearrange("a (t p) -> p (a t)", p=P)).then_inc(pos_loaded, 16)
            sp.dma_start(wide[:, 0:P + HD], d["c_wide"][:, 0:P + HD]).then_inc(consts_loaded, 16)
            sp.dma_start(x[:], d["x"].rearrange("a (t p) n -> p (a t) n", p=P)).then_inc(x_loaded, 16)
            sp.dma_start(wide[:, P + HD:], d["c_wide"][:, P + HD:]).then_inc(masks_loaded, 16)

            def ffn_weights(name_in, name_out, l):
                return (d[name_in][l].rearrange("(h t p) (s f) -> h p t s f", p=P, t=4, s=2), d[name_out][l])

            with sp.Fori(0, LAYERS) as l:
                g = l * G_L1
                sp_ffn(sp, g, *ffn_weights("ffn1_in", "ffn1_out", l))
                sp_gain_bias(sp, l * 3, d["ln_g"][l, 0, :], d["ln_b"][l, 0, :])
                sp_mix1(sp, g + G_FFN, l * 3 + 1, l)
                sp_ffn(sp, g + G_FFN + G_MIX1, *ffn_weights("ffn2_in", "ffn2_out", l))
                sp_gain_bias(sp, l * 3 + 2, d["ln_g"][l, 2, :], d["ln_b"][l, 2, :])
            sp.wait_ge(x_ready, PH2 * 2)
            steady(sp)
            sp.dma_start(mix_gain[:], d["norm_mix_g_2"][0].partition_broadcast(P)).then_inc(gain_loaded, 16)
            with sp.Fori(0, LAYERS) as l:
                g = LAYERS * G_L1 + l * G_L2
                ph = PH2 + l * 2
                sp_mix2(sp, g, ph, l)
                sp_ffn(sp, g + G_MIX2, *ffn_weights("w_ffn_in_2", "w_ffn_out_2", l))
                sp.wait_ge(x_ready, ph * 2 + 4)
                steady(sp)
                sp.dma_start(mix_gain[:], d["norm_mix_g_2"][LAYERS - 1].partition_broadcast(P)).then_inc(gain_loaded, 16)
            for tok in range(TT):
                sp.wait_ge(x_ready, (PH2 + 2 * LAYERS) * 2 + (tok + 1))
                sp.dma_start(out[0, tok * P:(tok + 1) * P, :], x[:, tok, :]).then_inc(stored, 16)
            sp.wait_ge(stored, 16 * TT)

        @block.tensor
        def _(pe):
            pe.sem_inc(chunk_used, RING)
            pe.wait_ge(consts_loaded, 16)
            with pe.Fori(0, LAYERS) as l:
                g = l * G_L1
                pe_ffn(pe, g, l * 3, l * 2, (x, x_ready, l * 6))
                pe_mix1(pe, g + G_FFN, l * 3 + 1, l)
                pe_ffn(pe, g + G_FFN + G_MIX1, l * 3 + 2, l * 2 + 1, (x, x_ready, l * 6 + 4))
            with pe.Fori(0, LAYERS) as l:
                g = LAYERS * G_L1 + l * G_L2
                ph = PH2 + l * 2
                pe_mix2(pe, g, ph, l)
                pe_ffn(pe, g + G_MIX2, ph + 1, 2 * LAYERS + l, (hn, hn_ready, l * 4 + 2))

        @block.scalar
        def _(act):
            act.wait_ge(setup, ANGLE)
            act.activation(sin[:], ang[:], ACT.Sin).then_inc(setup_act, 1)
            act.wait_ge(setup, CO_ANGLE)
            act.activation(cos[:], turns[:], ACT.Sin).then_inc(setup_act, 1)
            with act.Fori(0, LAYERS) as l:
                g = l * G_L1
                g1, g2 = g + G_FFN, g + G_FFN + G_MIX1
                act_ffn(act, g, l * 3, l * 2, False, lambda h: act_misc_split(act, g1, l, h))
                act_mix1(act, g1, l * 3 + 1, l, True)
                act_ffn(act, g2, l * 3 + 2, l * 2 + 1, True, None)
            with act.Fori(0, LAYERS) as l:
                g = LAYERS * G_L1 + l * G_L2
                ph = PH2 + l * 2
                act_split(act, g, 0)
                act_split(act, g, 1)
                act_mix2(act, g, ph, l)
                act_split(act, g + G_MIX2, 0)
                act_head(act, ph + 1, 0)
                act_split(act, g + G_MIX2, 1)
                act_head(act, ph + 1, 1)
                act_ffn(act, g + G_MIX2, ph + 1, 2 * LAYERS + l, True, None)

        @block.vector
        def _(dve):
            dve_setup(dve)
            assert SETUP == {"angle": ANGLE, "co_angle": CO_ANGLE, "tables": TABLES}, SETUP
            with dve.Fori(0, LAYERS) as l:
                g = l * G_L1
                g1, g2 = g + G_FFN, g + G_FFN + G_MIX1
                ph = l * 3
                dve_split(dve, g, 0)
                dve_xT(dve, ph, 0)
                dve_split(dve, g, 1)
                dve_xT(dve, ph, 1)
                dve_ffn(dve, g, ph, l * 2, 0.25)

                def handover(g, ph, last_chunk, banks, split):
                    split(0)
                    ln_sums(dve, g, ph, last_chunk, banks, 0)
                    ln_apply(dve, ph, 0)
                    ln_sums(dve, g, ph, last_chunk, banks, 1)
                    dve_xT(dve, ph + 1, 0)
                    split(1)
                    ln_apply(dve, ph, 1)
                    dve_xT(dve, ph + 1, 1)

                handover(g, ph, 32, FFN_BANKS, lambda h: dve_split(dve, g1, h, MISC_W))
                dve_mix1(dve, g1, ph + 1, l)
                handover(g1, ph + 1, 35, MIX_BANKS, lambda h: dve_split(dve, g2, h))
                dve_ffn(dve, g2, ph + 2, l * 2 + 1, 0.25)
                for tok in range(TT):
                    ln_sums(dve, g2, ph + 2, 32, FFN_BANKS, tok)
                    ln_apply(dve, ph + 2, tok)
            with dve.Fori(0, LAYERS) as l:
                g = LAYERS * G_L1 + l * G_L2
                ph = PH2 + l * 2
                dve_head(dve, ph, 0, mix_gain[:])
                dve_split(dve, g, 0)
                dve_xT(dve, ph, 0)
                dve_split(dve, g, 1)
                dve_head(dve, ph, 1, mix_gain[:])
                dve_xT(dve, ph, 1)
                dve_mix2(dve, g, ph, l)
                gf = g + G_MIX2
                dve_split(dve, gf, 0)
                dve_tail(dve, g, ph, WO_CHUNK + 3, MIX_BANKS, 0)
                dve_head(dve, ph + 1, 0, gb[:, 0, :])
                dve_tail(dve, g, ph, WO_CHUNK + 3, MIX_BANKS, 1)
                dve_xT(dve, ph + 1, 0)
                dve_split(dve, gf, 1)
                dve_head(dve, ph + 1, 1, gb[:, 0, :])
                dve_xT(dve, ph + 1, 1)
                dve_ffn(dve, gf, ph + 1, 2 * LAYERS + l, 0.5)
                for tok in range(TT):
                    dve_tail(dve, gf, ph + 1, 32, FFN_BANKS, tok)

        @block.gpsimd
        def _(pool):
            pool.wait_ge(x_loaded, 16)
            pool.sem_inc(x_ready, 2)
            pool.memset(minus_half[:], -0.5).then_inc(half_set, 1)
            pool.wait_ge(half_set, 1)
            pool.wait_ge(setup, TABLES)
            pool.wait_ge(setup_act, 2)
            with pool.Fori(0, LAYERS) as l:
                pool_rstd(pool, l * 3)
                pool_mix1(pool, l)
                pool_rstd(pool, l * 3 + 1)
                pool_rstd(pool, l * 3 + 2)
            with pool.Fori(0, LAYERS) as l:
                ph = PH2 + l * 2
                pool_rstd(pool, ph)
                pool_mix2(pool, ph, l)
                pool_rstd(pool, ph + 1)


INPUTS = ("x", "positions", "w_in", "sink_b", "w_br_a", "w_br_b", "w_br_c", "w_out", "ffn1_in", "ffn1_out",
          "ffn2_in", "ffn2_out", "ln_g", "ln_b", "norm_mix_g_2", "w_in_2", "forget_b_2", "q_norm_g_2",
          "k_norm_g_2", "w_attn_out_2", "conv_w_2", "w_conv_out_2", "pool_w_2", "pool_scale_2", "w_o_2",
          "norm_ffn_g_2", "w_ffn_in_2", "w_ffn_out_2")


def kernel(**inputs):
    import concourse.bacc as _bacc
    from concourse.bass_utils import run_bass_kernel_spmd as _run

    nc = _bacc.Bacc("TRN2", target_bir_lowering=False, num_devices=1)
    arrays, d = {}, {}
    for name, value in [(name, inputs[name]) for name in INPUTS] + list(shape_constants().items()):
        a = np.ascontiguousarray(value)
        arrays[f"in_{name}_dram"] = a
        d[name] = nc.dram_tensor(f"in_{name}_dram", a.shape, mybir.dt.from_np(a.dtype), kind="ExternalInput").ap()
    out = nc.dram_tensor("out_0_dram", (1, SEQ, DM), F32, kind="ExternalOutput").ap()
    build_program(nc, d, out)
    r = _run(nc, [arrays], core_ids=[0])
    return r.results[0]["out_0_dram"]
```
